# Optimizing a Trainium2 kernel written in Bass

```python
import math
import jax, jax.numpy as jnp
from jax import lax
import numpy as np

D_MODEL = 1024
BATCH = 1
SEQ = 512
DEPTH = 2
DEC_BATCH = 1
DEC_SEQ = 64
PAST_LEN = 1024

CHUNK = 64
N_AB = (DEPTH + 1) // 2
N_S5 = DEPTH // 2
LRU_WIDTH = D_MODEL // 2
LRU_HEADS = 8
LRU_HEAD_DIM = LRU_WIDTH // LRU_HEADS
CONV_WIDTH = 4
RG_C = 8.0
HG_WIDTH = D_MODEL // 2
HG_HEADS = 4
HG_DK = HG_WIDTH // HG_HEADS
HG_DV = HG_WIDTH // HG_HEADS
HG_BLOCK = 16
RMS_EPS = 1e-6
S5_WIDTH = D_MODEL
S5_GROUP = 16
S5_GROUPS = S5_WIDTH // S5_GROUP
S5_STATE = 64
N_EXPERTS = 16
N_EXPERT_GROUPS = 4
EXPERTS_PER_GROUP = N_EXPERTS // N_EXPERT_GROUPS
TOP_K = 2
D_EXPERT = 512
ALPHA = (2.0 * DEPTH) ** 0.25
BETA = (8.0 * DEPTH) ** -0.25
LN_EPS = 1e-5
D_IN_AB = 2 * LRU_WIDTH + 4 * HG_WIDTH
AB_SPLITS = [LRU_WIDTH, 2 * LRU_WIDTH, 2 * LRU_WIDTH + HG_WIDTH,
             2 * LRU_WIDTH + 2 * HG_WIDTH, 2 * LRU_WIDTH + 3 * HG_WIDTH]

kernel_name = 'hybrid_rglru_hgrn2_s5_moe_stream_step'

F32 = jnp.float32

def _post_norm(x, f, g, b):
    s = ALPHA * x.astype(F32) + f.astype(F32)
    mu = jnp.mean(s, -1, keepdims=True)
    var = jnp.mean(jnp.square(s - mu), -1, keepdims=True)
    return ((s - mu) * lax.rsqrt(var + LN_EPS) * g.astype(F32) + b.astype(F32)).astype(x.dtype)

def _linear_scan(a, b, h0):
    b = b.at[:, 0].add(a[:, 0] * h0)
    def combine(l, r):
        a_l, b_l = l
        a_r, b_r = r
        return a_l * a_r, a_r * b_l + b_r
    _, h = lax.associative_scan(combine, (a, b), axis=1)
    return h

def _causal_dwconv(u, buf, w, bias):
    T = u.shape[1]
    up = jnp.concatenate([buf.astype(F32), u.astype(F32)], axis=1)
    y = bias.astype(F32) + sum(w[k].astype(F32) * up[:, k:k + T] for k in range(CONV_WIDTH))
    return y, up[:, T:]

def _rg_lru(u, h0, w_r, b_r, w_i, b_i, lam):
    Bn, T, _ = u.shape
    uh = u.reshape(Bn, T, LRU_HEADS, LRU_HEAD_DIM)
    r = jax.nn.sigmoid(jnp.einsum('bthi,hij->bthj', uh, w_r.astype(F32)).reshape(Bn, T, LRU_WIDTH) + b_r.astype(F32))
    i = jax.nn.sigmoid(jnp.einsum('bthi,hij->bthj', uh, w_i.astype(F32)).reshape(Bn, T, LRU_WIDTH) + b_i.astype(F32))
    log_a = -RG_C * r * jax.nn.softplus(-lam.astype(F32))
    a = jnp.exp(log_a)
    mult = jnp.sqrt(-jnp.expm1(2.0 * log_a))
    h = _linear_scan(a, mult * i * u, h0.astype(F32))
    return h, h[:, -1]

def _hgrn2(q, log_f, v, s0):
    Bn, T, H, _ = q.shape
    L = math.gcd(T, HG_BLOCK)
    n = T // L
    k = -jnp.expm1(log_f)
    blk = lambda t: t.reshape(Bn, n, L, H, t.shape[-1])
    q, log_f, k, v = blk(q), blk(log_f), blk(k), blk(v)
    G = jnp.cumsum(log_f, axis=2)
    q_dec = q * jnp.exp(G)
    k_inc = k * jnp.exp(-G)
    causal = jnp.tril(jnp.ones((L, L), bool))
    scores = jnp.where(causal, jnp.einsum('bnthk,bnshk->bnhts', q_dec, k_inc), 0.0)
    o_intra = jnp.einsum('bnhts,bnshv->bnthv', scores, v)
    G_last = G[:, :, -1]
    k_tail = k * jnp.exp(G_last[:, :, None] - G)
    def step(S, inp):
        qd, kt, vb, decay = inp
        o = jnp.einsum('bthk,bhkv->bthv', qd, S)
        S = decay[..., None] * S + jnp.einsum('bshk,bshv->bhkv', kt, vb)
        return S, o
    mv = lambda t: jnp.moveaxis(t, 1, 0)
    s_final, o_inter = lax.scan(step, s0.astype(F32), (mv(q_dec), mv(k_tail), mv(v), mv(jnp.exp(G_last))))
    o = o_intra + jnp.moveaxis(o_inter, 0, 1)
    return o.reshape(Bn, T, H, -1), s_final

def _ab_mixer(x, h0, conv0, s0, w_in, w_out, conv_w, conv_b, w_r, b_r, w_i, b_i, lam, lb, norm_g):
    Bn, T, _ = x.shape
    z = x @ w_in
    z_gate, z_x, z_q, z_f, z_i, z_g = jnp.split(z, AB_SPLITS, axis=-1)
    u, conv_new = _causal_dwconv(z_x, conv0, conv_w, conv_b)
    h, h_last = _rg_lru(u, h0, w_r, b_r, w_i, b_i, lam)
    out_a = h * jax.nn.gelu(z_gate.astype(F32))
    f = lb + (1.0 - lb) * jax.nn.sigmoid(z_f.astype(F32))
    q = z_q.astype(F32).reshape(Bn, T, HG_HEADS, HG_DK)
    log_f = jnp.log(f).reshape(Bn, T, HG_HEADS, HG_DK)
    v = z_i.astype(F32).reshape(Bn, T, HG_HEADS, HG_DV)
    o, s_new = _hgrn2(q, log_f, v, s0)
    o = o * lax.rsqrt(jnp.mean(jnp.square(o), -1, keepdims=True) + RMS_EPS) * norm_g.astype(F32).reshape(HG_HEADS, HG_DV)
    out_b = o.reshape(Bn, T, HG_WIDTH) * jax.nn.silu(z_g.astype(F32))
    y = jnp.concatenate([out_a, out_b], axis=-1).astype(x.dtype) @ w_out
    return y, h_last, conv_new, s_new

def _s5_scan(u, s0_re, s0_im, a_re, a_im, b_re, b_im, c_re, c_im, d, log_dt):
    Bn, T, _ = u.shape
    uf = u.astype(F32)
    A = a_re.astype(F32) + 1j * a_im.astype(F32)
    dt = jnp.exp(log_dt.astype(F32))[:, None]
    A_bar = jnp.exp(dt * A)
    B_bar = ((A_bar - 1.0) / A)[..., None] * (b_re.astype(F32) + 1j * b_im.astype(F32))
    Cm = c_re.astype(F32) + 1j * c_im.astype(F32)
    L = math.gcd(T, CHUNK)
    n = T // L
    u_blk = jnp.moveaxis(uf.reshape(Bn, n, L, S5_GROUPS, S5_GROUP), 1, 0)
    def step(s, ub):
        bu = jnp.einsum('gpc,blgc->blgp', B_bar, ub.astype(jnp.complex64))
        states = _linear_scan(jnp.broadcast_to(A_bar, bu.shape), bu, s)
        y = jnp.einsum('gcp,blgp->blgc', Cm, states).real
        return states[:, -1], y
    s0 = s0_re.astype(F32) + 1j * s0_im.astype(F32)
    s_last, y = lax.scan(step, s0, u_blk)
    y = jnp.moveaxis(y, 0, 1).reshape(Bn, T, S5_WIDTH) + d.astype(F32) * uf
    return y, s_last.real, s_last.imag

def _s5_mixer(x, s0_re, s0_im, w_in, w_out, a_re, a_im, b_re, b_im, c_re, c_im, d, log_dt):
    u = x @ w_in
    y, s_re, s_im = _s5_scan(u, s0_re, s0_im, a_re, a_im, b_re, b_im, c_re, c_im, d, log_dt)
    z = jax.nn.gelu(y).astype(x.dtype) @ w_out
    val, gate = jnp.split(z, 2, axis=-1)
    return val * jax.nn.sigmoid(gate), s_re, s_im

def _moe(x, router_w, router_b, w_gate, w_up, w_down):
    Bn, T, D = x.shape
    xt = x.reshape(-1, D)
    logits = xt.astype(F32) @ router_w.astype(F32) + router_b.astype(F32)
    probs = jax.nn.softmax(logits, axis=-1)
    pg = probs.reshape(-1, N_EXPERT_GROUPS, EXPERTS_PER_GROUP)
    group_score = lax.top_k(pg, TOP_K)[0].sum(-1)
    g_sel = jnp.argmax(group_score, axis=-1)
    p_in = jnp.take_along_axis(pg, g_sel[:, None, None], axis=1)[:, 0]
    top_p, top_i = lax.top_k(p_in, TOP_K)
    gates = top_p / jnp.sum(top_p, -1, keepdims=True)
    expert_ids = g_sel[:, None] * EXPERTS_PER_GROUP + top_i
    combine = jnp.einsum('nk,nke->ne', gates, jax.nn.one_hot(expert_ids, N_EXPERTS, dtype=F32))
    y = jnp.zeros(xt.shape, F32)
    for e in range(N_EXPERTS):
        h = jax.nn.silu(xt @ w_gate[e]) * (xt @ w_up[e])
        y = y + combine[:, e:e + 1] * (h @ w_down[e]).astype(F32)
    return y.reshape(Bn, T, D).astype(x.dtype)

def setup_inputs(seed: int = 0) -> dict:
    key = jax.random.key(seed)
    ks = iter(jax.random.split(key, 48))
    nrm = lambda shape, scale: scale * jax.random.normal(next(ks), shape, F32)
    u_lam = jax.random.uniform(next(ks), (N_AB, LRU_WIDTH), F32, minval=0.9, maxval=0.999)
    p_lam = u_lam ** (1.0 / RG_C)
    log_dt = jax.random.uniform(next(ks), (N_S5, S5_GROUPS), F32, minval=math.log(0.001), maxval=math.log(0.1))
    a_im = jnp.pi * jnp.broadcast_to(jnp.arange(S5_STATE, dtype=F32), (N_S5, S5_GROUPS, S5_STATE)) + nrm((N_S5, S5_GROUPS, S5_STATE), 0.01)
    return {
        'x_prompt': nrm((BATCH, SEQ, D_MODEL), 1.0),
        'x_sample': nrm((DEC_BATCH, DEC_SEQ, D_MODEL), 1.0),
        'state_lru_h': nrm((N_AB, DEC_BATCH, LRU_WIDTH), 0.5),
        'state_lru_conv': nrm((N_AB, DEC_BATCH, CONV_WIDTH - 1, LRU_WIDTH), 1.0),
        'state_hgrn2': nrm((N_AB, DEC_BATCH, HG_HEADS, HG_DK, HG_DV), 0.3),
        'state_s5_re': nrm((N_S5, DEC_BATCH, S5_GROUPS, S5_STATE), 0.3),
        'state_s5_im': nrm((N_S5, DEC_BATCH, S5_GROUPS, S5_STATE), 0.3),
        'ln_mix_g': 1.0 + nrm((DEPTH, D_MODEL), 0.02),
        'ln_mix_b': nrm((DEPTH, D_MODEL), 0.02),
        'ln_ffn_g': 1.0 + nrm((DEPTH, D_MODEL), 0.02),
        'ln_ffn_b': nrm((DEPTH, D_MODEL), 0.02),
        'w_in_ab': nrm((N_AB, D_MODEL, D_IN_AB), D_MODEL ** -0.5),
        'w_out_ab': nrm((N_AB, LRU_WIDTH + HG_WIDTH, D_MODEL), BETA * (LRU_WIDTH + HG_WIDTH) ** -0.5),
        'lru_conv_w': nrm((N_AB, CONV_WIDTH, LRU_WIDTH), CONV_WIDTH ** -0.5),
        'lru_conv_b': nrm((N_AB, LRU_WIDTH), 0.02),
        'lru_w_r': nrm((N_AB, LRU_HEADS, LRU_HEAD_DIM, LRU_HEAD_DIM), LRU_HEAD_DIM ** -0.5),
        'lru_b_r': nrm((N_AB, LRU_WIDTH), 0.02),
        'lru_w_i': nrm((N_AB, LRU_HEADS, LRU_HEAD_DIM, LRU_HEAD_DIM), LRU_HEAD_DIM ** -0.5),
        'lru_b_i': nrm((N_AB, LRU_WIDTH), 0.02),
        'lru_lam': jnp.log(p_lam) - jnp.log1p(-p_lam),
        'hgrn_lb_logits': nrm((N_AB + 1, HG_WIDTH), 0.5),
        'hgrn_norm_g': 1.0 + nrm((N_AB, HG_WIDTH), 0.02),
        'w_in_s5': nrm((N_S5, D_MODEL, S5_WIDTH), D_MODEL ** -0.5),
        'w_out_s5': nrm((N_S5, S5_WIDTH, 2 * D_MODEL), BETA * S5_WIDTH ** -0.5),
        's5_a_re': -0.5 + nrm((N_S5, S5_GROUPS, S5_STATE), 0.01),
        's5_a_im': a_im,
        's5_b_re': nrm((N_S5, S5_GROUPS, S5_STATE, S5_GROUP), (2 * S5_GROUP) ** -0.5),
        's5_b_im': nrm((N_S5, S5_GROUPS, S5_STATE, S5_GROUP), (2 * S5_GROUP) ** -0.5),
        's5_c_re': nrm((N_S5, S5_GROUPS, S5_GROUP, S5_STATE), S5_STATE ** -0.5),
        's5_c_im': nrm((N_S5, S5_GROUPS, S5_GROUP, S5_STATE), S5_STATE ** -0.5),
        's5_d': nrm((N_S5, S5_WIDTH), 0.5),
        's5_log_dt': log_dt,
        'router_w': nrm((D_MODEL, N_EXPERTS), D_MODEL ** -0.5),
        'router_b': nrm((N_EXPERTS,), 0.01),
        'moe_w_gate': nrm((DEPTH, N_EXPERTS, D_MODEL, D_EXPERT), D_MODEL ** -0.5),
        'moe_w_up': nrm((DEPTH, N_EXPERTS, D_MODEL, D_EXPERT), D_MODEL ** -0.5),
        'moe_w_down': nrm((DEPTH, N_EXPERTS, D_EXPERT, D_MODEL), BETA * D_EXPERT ** -0.5),
    }

def reference(x_prompt, x_sample, state_lru_h, state_lru_conv, state_hgrn2, state_s5_re, state_s5_im,
              ln_mix_g, ln_mix_b, ln_ffn_g, ln_ffn_b, w_in_ab, w_out_ab, lru_conv_w, lru_conv_b,
              lru_w_r, lru_b_r, lru_w_i, lru_b_i, lru_lam, hgrn_lb_logits, hgrn_norm_g,
              w_in_s5, w_out_s5, s5_a_re, s5_a_im, s5_b_re, s5_b_im, s5_c_re, s5_c_im, s5_d, s5_log_dt,
              router_w, router_b, moe_w_gate, moe_w_up, moe_w_down):
    bp = x_prompt.shape[0]
    lb_all = jnp.cumsum(jax.nn.softmax(hgrn_lb_logits.astype(F32), axis=0), axis=0)
    yp, ys = x_prompt, x_sample
    p_h, p_conv, p_hg, p_re, p_im = [], [], [], [], []
    s_h, s_conv, s_hg, s_re, s_im = [], [], [], [], []
    for l in range(DEPTH):
        j = l // 2
        if l % 2 == 0:
            w = (w_in_ab[j], w_out_ab[j], lru_conv_w[j], lru_conv_b[j], lru_w_r[j], lru_b_r[j],
                 lru_w_i[j], lru_b_i[j], lru_lam[j], lb_all[j], hgrn_norm_g[j])
            mp, h1, c1, g1 = _ab_mixer(yp, jnp.zeros((bp, LRU_WIDTH), F32),
                                       jnp.zeros((bp, CONV_WIDTH - 1, LRU_WIDTH), F32),
                                       jnp.zeros((bp, HG_HEADS, HG_DK, HG_DV), F32), *w)
            ms, h2, c2, g2 = _ab_mixer(ys, state_lru_h[j], state_lru_conv[j], state_hgrn2[j], *w)
            p_h.append(h1); p_conv.append(c1); p_hg.append(g1)
            s_h.append(h2); s_conv.append(c2); s_hg.append(g2)
        else:
            w = (w_in_s5[j], w_out_s5[j], s5_a_re[j], s5_a_im[j], s5_b_re[j], s5_b_im[j],
                 s5_c_re[j], s5_c_im[j], s5_d[j], s5_log_dt[j])
            zp = jnp.zeros((bp, S5_GROUPS, S5_STATE), F32)
            mp, r1, i1 = _s5_mixer(yp, zp, zp, *w)
            ms, r2, i2 = _s5_mixer(ys, state_s5_re[j], state_s5_im[j], *w)
            p_re.append(r1); p_im.append(i1)
            s_re.append(r2); s_im.append(i2)
        yp = _post_norm(yp, mp, ln_mix_g[l], ln_mix_b[l])
        ys = _post_norm(ys, ms, ln_mix_g[l], ln_mix_b[l])
        yp = _post_norm(yp, _moe(yp, router_w, router_b, moe_w_gate[l], moe_w_up[l], moe_w_down[l]), ln_ffn_g[l], ln_ffn_b[l])
        ys = _post_norm(ys, _moe(ys, router_w, router_b, moe_w_gate[l], moe_w_up[l], moe_w_down[l]), ln_ffn_g[l], ln_ffn_b[l])
    return (yp, ys,
            jnp.stack(p_h).astype(state_lru_h.dtype), jnp.stack(p_conv).astype(state_lru_conv.dtype),
            jnp.stack(p_hg).astype(state_hgrn2.dtype), jnp.stack(p_re).astype(state_s5_re.dtype),
            jnp.stack(p_im).astype(state_s5_im.dtype),
            jnp.stack(s_h).astype(state_lru_h.dtype), jnp.stack(s_conv).astype(state_lru_conv.dtype),
            jnp.stack(s_hg).astype(state_hgrn2.dtype), jnp.stack(s_re).astype(state_s5_re.dtype),
            jnp.stack(s_im).astype(state_s5_im.dtype))


_drawn_inputs = setup_inputs


def setup_inputs(seed=0):
    import zlib

    import numpy as np

    out = dict(_drawn_inputs(seed))
    spreads = {}
    factors = {'lru_b_r': 8.0, 'lru_b_i': 8.0, 'hgrn_norm_g': 3.001, 's5_a_re': 4.52}
    for name, (base, spread) in spreads.items():
        noise = np.random.default_rng([zlib.crc32(name.encode()), seed]).standard_normal(out[name].shape)
        drawn = base * np.exp(spread * noise) if base else spread * noise
        out[name] = __import__('jax').numpy.asarray(drawn.astype(out[name].dtype))
    for name, factor in factors.items():
        out[name] = (out[name] * factor).astype(out[name].dtype)
    return out
```

```python
import concourse.bass as bass
from concourse import mybir
from contextlib import ExitStack

F32 = mybir.dt.float32
F32R = mybir.dt.float32r
I32 = mybir.dt.int32
U32 = mybir.dt.uint32
ALU = mybir.AluOpType
ACT = mybir.ActivationFunctionType
AX_X = mybir.AxisListType.X

P = 128
D = 1024
KT = D // P
T_PROMPT, T_SAMPLE = 512, 64
T = T_PROMPT + T_SAMPLE
TT = 120
TILES = [(t, min(TT, T - t)) for t in range(0, T, TT)]
NT = len(TILES)
HALF = T // 2
LRU = 512
LRU_TILES = LRU // P
CONV = 4
LRU_W = T + 2 * (CONV - 1) + 1
LRU_U = LRU_W - (CONV - 1)
S0_AT = T_PROMPT + CONV - 1
HEADS = 4
BLK = 16
NBLK_P, NBLK_S = T_PROMPT // BLK, T_SAMPLE // BLK
NBLK = NBLK_P + NBLK_S
SRING = 9
HTILES = [(t, min(P, T - t)) for t in range(0, T, P)]
ALPHA = 4.0 ** 0.25
LN_EPS = 1e-5
RMS_EPS = 1e-6
E = 16
GROUPS, PER_GROUP = 4, 4
F_EXP = 512
CAP = 128
ROUNDS_MAX = -(-T // CAP)
SLOTS = E * CAP
DUMP = SLOTS

CHUNK = 4096
SB0 = 16512
RAW_AT = [SB0, SB0 + 16384]
SPL_AT = [SB0 + 32768, SB0 + 65536]
FT_AT = SB0 + 98304
YT_AT = FT_AT + 2 * KT * T * 4
XTOK_AT = YT_AT + 2 * KT * T * 4
TEMP_AT = XTOK_AT + NT * D * 4
SB_END = 229344


def stream_kernel(nc, a, o):
    with ExitStack() as ctx:
        taken = [TEMP_AT]

        def at(name, shape, offset, dt=F32):
            return nc.alloc_sbuf_tensor_at(name, shape, dt, offset=offset)

        def small(name, cols, dt=F32, parts=P):
            t = at(name, [parts] + (cols if isinstance(cols, list) else [cols]), taken[0], dt)
            n = 4
            for c in (cols if isinstance(cols, list) else [cols]):
                n *= c
            taken[0] += -(-n // 32) * 32
            assert taken[0] <= SB_END, name
            return t

        def sem(name):
            return ctx.enter_context(nc.semaphore(name))

        ps = ctx.enter_context(nc.psum_tensor("ps", [P, 8, 512], F32))

        raw = [at(f"raw{i}", [P, CHUNK], RAW_AT[i]) for i in range(2)]
        whi = [at(f"whi{i}", [P, CHUNK], SPL_AT[i], F32R) for i in range(2)]
        wlo = [at(f"wlo{i}", [P, CHUNK], SPL_AT[i] + 4 * CHUNK, F32R) for i in range(2)]
        ft_hi = at("ft_hi", [P, KT, T], FT_AT, F32R)
        ft_lo = at("ft_lo", [P, KT, T], FT_AT + 4 * KT * T, F32R)
        yt_hi = at("yt_hi", [P, KT, T], YT_AT, F32R)
        yt_lo = at("yt_lo", [P, KT, T], YT_AT + 4 * KT * T, F32R)
        xtok = at("xtok", [P, NT, D], XTOK_AT)

        ident = small("ident", P)
        ones = small("ones", P)
        lstrict = small("lstrict", P)
        wt4 = small("wt4", PER_GROUP)
        e128 = small("e128", E)
        eps = small("eps", 2)
        lnst = small("lnst", [2, 2, 6])
        lnmv = small("lnmv", [2, 4])
        gate = small("gate", [2, NT])
        slot = small("slot", [2, NT], U32)
        nstep = small("nstep", 1, I32)
        shared_end = taken[0]
        causal = small("causal", P)
        blkmask = small("blkmask", 8)
        m0 = small("m0", BLK)
        convw = small("convw", [LRU_TILES, CONV])
        convb = small("convb", LRU_TILES)
        b_r = small("b_r", LRU_TILES)
        b_i = small("b_i", LRU_TILES)
        lam = small("lam", LRU_TILES)
        h0 = small("h0", LRU_TILES)
        spl4 = small("spl4", LRU_TILES)
        sp = small("sp", [6, LRU_TILES])
        lbl = small("lbl", [2, HEADS])
        lbs = small("lbs", [4, HEADS])
        lb = small("lb", HEADS)
        omlb = small("omlb", HEADS)
        nomlb = small("nomlb", HEADS)
        hg_g = small("hg_g", HEADS)
        consts_end = taken[0]

        l0_at = [consts_end]
        l0b_at = [XTOK_AT]

        def l0(name, cols, low=False):
            cols = cols if isinstance(cols, list) else [cols]
            n = 4
            for c in cols:
                n *= c
            n = -(-n // 32) * 32
            where = l0b_at if low else l0_at
            t = at(name, [P] + cols, where[0])
            where[0] += n
            assert where[0] <= (TEMP_AT if low else SB_END), name
            return t

        zx = [l0(f"zx{i}", LRU_W, True) for i in range(2)]
        gz = [l0(f"gz{i}", T, True) for i in range(2)]
        lu = l0("lu", LRU_U, True)
        lr = l0("lr", LRU_U, True)
        li = l0("li", LRU_U, True)
        lt = l0("lt", LRU_U, True)
        ld = l0("ld", LRU_U)
        la = l0("la", LRU_U)
        lq = l0("lq", LRU_U)
        wr = l0("wr", P)
        wi = l0("wi", P)
        l0_at_lru_end = l0_at[0]
        xin = [at(f"xin{i}", [P, D], YT_AT + 4 * D * i) for i in range(2)]
        l0_at[0], l0b_at[0] = consts_end, XTOK_AT
        hf = l0("hf", T, True)
        hk = l0("hk", T, True)
        ha = l0("ha", T, True)
        hb = l0("hb", T, True)
        hp = l0("hp", T, True)
        hq = l0("hq", T, True)
        hv = l0("hv", T, True)
        hg = l0("hg", T, True)
        vtok = l0("vtok", [5, P])
        ktok = l0("ktok", [5, P])
        srn = l0("srn", [SRING, P])
        vmask = l0("vmask", [8, P])
        sc = l0("sc", P)
        ho = hk
        hr = hf
        zeros = at("zeros", [P, D], SB_END - 4 * D)
        assert l0_at_lru_end <= SB_END - 4 * D

        taken[0] = shared_end
        lng = small("lng", D)
        lnb = small("lnb", D)
        x1t = small("x1t", [KT, TT])
        rw = small("rw", [KT, E])
        rb = small("rb", E)
        R = {n: small("r_" + n, [NT, E]) for n in ("l", "p", "m1", "m2", "w", "x", "s1")}
        Rg = {n: small("rg_" + n, [NT, GROUPS]) for n in ("a", "b", "c", "d", "e")}
        Rt = {n: small("rt_" + n, NT) for n in ("mx", "z", "p1", "p2")}
        nrow = small("nrow", 4)

        taken[0] = shared_end
        xe = small("xe", D)
        xet_hi = small("xet_hi", [KT, P], F32R)
        xet_lo = small("xet_lo", [KT, P], F32R)
        hx = at("hx", [P, F_EXP], YT_AT + 8 * CHUNK)
        ht_hi = small("ht_hi", [4, P], F32R)
        ht_lo = small("ht_lo", [4, P], F32R)
        raw.append(at("raw2", [P, CHUNK], YT_AT))
        whi.append(at("whi2", [P, CHUNK], FT_AT, F32R))
        wlo.append(at("wlo2", [P, CHUNK], FT_AT + 4 * CHUNK, F32R))
        ysb = at("ysb", [P, D], FT_AT + 8 * CHUNK)
        ygat = [[at(f"ygat{i}{k}", [P, D], YT_AT + 4 * CHUNK + 4 * D * (2 * i + k)) for k in range(2)] for i in range(2)]

        xg = nc.dram_tensor("xg", (ROUNDS_MAX * SLOTS, D), F32, kind="Internal").ap()
        yg = nc.dram_tensor("yg", (ROUNDS_MAX * SLOTS, D), F32, kind="Internal").ap()

        S = {}

        def s(name):
            if name not in S:
                S[name] = sem(name)
            return S[name]

        w_in = a["w_in_ab"][0].rearrange("(k p) n -> p k n", p=P)
        w_out = a["w_out_ab"][0].rearrange("(k p) n -> p k n", p=P)

        chunks0 = []
        for jp in range(LRU_TILES // 2):
            chunks0.append([(w_in[:, :, LRU + 256 * jp:LRU + 256 * jp + 256], 0, 256),
                            (w_in[:, :, 256 * jp:256 * jp + 256], 256, 256)])
        Q_AT, F_AT, V_AT, G_AT = (2 * LRU + 512 * i for i in range(4))
        for h in range(HEADS):
            chunks0.append([(w_in[:, :, b + P * h:b + P * h + P], P * i, P)
                            for i, b in enumerate((F_AT, Q_AT, V_AT, G_AT))])
        for n in range(2):
            chunks0.append([(w_out[:, :, 512 * n:512 * n + 512], 0, 512)])
        n_in = 6
        landed = {}
        count = [0, 0]
        for c, pieces in enumerate(chunks0):
            count[c % 2] += 16 * len(pieces)
            landed[c] = count[c % 2]
        param_dmas = [
            *[(convw[:, :, k], a["lru_conv_w"][0, k].rearrange("(j p) -> p j", p=P)) for k in range(CONV)],
            (convb[:], a["lru_conv_b"][0].rearrange("(j p) -> p j", p=P)),
            (b_r[:], a["lru_b_r"][0].rearrange("(j p) -> p j", p=P)),
            (b_i[:], a["lru_b_i"][0].rearrange("(j p) -> p j", p=P)),
            (lam[:], a["lru_lam"][0].rearrange("(j p) -> p j", p=P)),
            (h0[:], a["state_lru_h"][0, 0].rearrange("(j p) -> p j", p=P)),
            *[(lbl[:, r], a["hgrn_lb_logits"][r].rearrange("(j p) -> p j", p=P)) for r in range(2)],
            (hg_g[:], a["hgrn_norm_g"][0].rearrange("(j p) -> p j", p=P)),
        ]

        def x_rows(t0, n):
            xp, xs = a["x_prompt"][0], a["x_sample"][0]
            if t0 + n <= T_PROMPT:
                return [(0, n, xp[t0:t0 + n])]
            m = T_PROMPT - t0
            return [(0, m, xp[t0:T_PROMPT]), (m, n - m, xs[0:n - m])]


        ln_no = {"mix0": 0, "ffn0": 1, "mix1": 2, "ffn1": 3}

        def ln_gains_pool(pool, tag):
            ln, l = tag[:3], int(tag[3])
            for dst, src in ((lng, a[f"ln_{ln}_g"]), (lnb, a[f"ln_{ln}_b"])):
                pool.dma_start(dst[:], src[l:l + 1, :].to_broadcast([P, D])).then_inc(s("ln_gains"), 16)

        def ln_act(act, tag, tiles=range(NT)):
            for i in tiles:
                n = TILES[i][1]
                act.wait_ge(s("ln_mv"), NT * ln_no[tag] + i + 1)
                nc.scalar.activation(lnmv[0:n, i % 2, 2:3], lnmv[0:n, i % 2, 1:2], ACT.Sqrt,
                                     bias=eps[0:n, 1:2]).then_inc(s("ln_sd"), 1)

        def ln_dve(dve, link, tag, i):
            v, n = nc.vector, TILES[i][1]
            x, st, mv = xtok[0:n, i, :], lnst[0:n, i % 2], lnmv[0:n, i % 2]
            v.bn_stats(st[:, 0, :], x[:, 0:512])
            link(v.bn_stats(st[:, 1, :], x[:, 512:D]))
            v.bn_aggr(mv[:, 0:2], st).then_inc(s("ln_mv"), 1)
            dve.wait_ge(s("ln_sd"), NT * ln_no[tag] + i + 1)
            link(v.reciprocal(mv[:, 3:4], mv[:, 2:3]))
            link(v.tensor_scalar(x, x, mv[:, 0:1], mv[:, 3:4], ALU.subtract, ALU.mult))
            dve.wait_ge(s("ln_gains"), 32 * ln_no[tag] + 32)
            link(v.tensor_tensor(x, x, lng[0:n, :], ALU.mult))
            v.tensor_tensor(x, x, lnb[0:n, :], ALU.add).then_inc(s("ln_x"), 1)

        def route_pool(pool, l):
            L = f"_{l}"
            pool.dma_start(rw[:], a["router_w"].rearrange("(k p) e -> p k e", p=P)).then_inc(s("rw"), 16)
            pool.dma_start(rb[:], a["router_b"].rearrange("(x e) -> x e", x=1).to_broadcast([P, E])
                           ).then_inc(s("rw"), 16)
            pool.wait_ge(s("routed"), 1 * l + 1)
            steps = pool.value_load(nstep[0:1, 0:1], min_val=E, max_val=E * ROUNDS_MAX)
            with pool.If(steps > E):
                nc.gpsimd.memset(ysb[:], 0.0).then_inc(s("rest_zero" + L), 1)
                pool.wait_ge(s("rest_zero" + L), 1)
                with pool.Fori(1, ROUNDS_MAX) as rr:
                    for q in range(E):
                        for buf in (xg, yg):
                            pool.dma_start(buf[bass.ds(rr * SLOTS + CAP * q, CAP)], ysb[:]).then_inc(s("xg_rest" + L), 16)
                pool.wait_ge(s("xg_rest" + L), 32 * E * (ROUNDS_MAX - 1))
            for i, (t0, n) in enumerate(TILES):
                for k in range(2):
                    pool.indirect_dma_start(out=xg, out_offset=bass.IndirectOffsetOnAxis(ap=slot[0:n, k, i:i + 1], axis=0),
                                            in_=xtok[0:n, i, :], in_offset=None).then_inc(s("sent"), 16)
            pool.wait_ge(s("sent"), 32 * NT * l + 32 * NT)

        def route_act(act, l):
            L = f"_{l}"
            for i, (t0, n) in enumerate(TILES):
                act.wait_ge(s("x1T"), NT * l + i + 1)
                if i:
                    act.wait_ge(s("logit"), NT * l + i)
                nc.scalar.activation(x1t[:, :, 0:n].rearrange("p (a k) t -> p a k t", a=2),
                                     ps[:, 4:6, :].rearrange("p a (k t) -> p a k t", t=P)[:, :, :, 0:n],
                                     ACT.Copy).then_inc(s("x1t"), 1)
            act.wait_ge(s("r_shift"), 1 * l + 1)
            nc.scalar.activation(R["p"][0:TT], R["w"][0:TT], ACT.Exp).then_inc(s("r_exp"), 1)

        def route_pe(pe, l):
            L, te = f"_{l}", nc.tensor
            pe.wait_ge(s("rw"), 32 * l + 32)
            for i, (t0, n) in enumerate(TILES):
                pe.wait_ge(s("ln_x"), NT * (2 * l) + i + 1)
                if i:
                    pe.wait_ge(s("x1t"), NT * l + i)
                for k in range(KT):
                    ins = te.transpose(ps[:, 4 + k // 4, P * (k % 4):P * (k % 4) + n], xtok[0:n, i, P * k:P * k + P],
                                       ident[0:n, 0:n])
                ins.then_inc(s("x1T"), 1)
                pe.wait_ge(s("x1t"), NT * l + i + 1)
                for k in range(KT):
                    ins = te.matmul(ps[0:n, 6, E * i:E * i + E], x1t[:, k, 0:n], rw[:, k, :],
                                    start=(k == 0), stop=(k == KT - 1))
                ins.then_inc(s("logit"), 1)
            pe.wait_ge(s("chosen"), 1 * l + 1)
            m = R["x"]
            for i, (t0, n) in enumerate(TILES):
                for q in range(i + 1):
                    nq = TILES[q][1]
                    te.matmul(ps[0:n, 7, E * i:E * i + E], (lstrict if q == i else ones)[0:nq, 0:n], m[0:nq, q, :],
                              start=(q == 0), stop=(q == i))
            for q in range(NT):
                nq = TILES[q][1]
                ins = te.matmul(ps[:, 7, E * NT:E * NT + E], ones[0:nq, :], m[0:nq, q, :],
                                start=(q == 0), stop=(q == NT - 1))
            ins.then_inc(s("ranked"), 1)

        def route_dve(dve, link, l):
            L, v = f"_{l}", nc.vector
            n = TT
            lg, pr, m1, m2, w, x, s1 = (R[q][0:n] for q in ("l", "p", "m1", "m2", "w", "x", "s1"))
            ga, gb, gc, gd, ge = (Rg[q][0:n] for q in ("a", "b", "c", "d", "e"))
            mx, z, p1, p2 = (Rt[q][0:n] for q in ("mx", "z", "p1", "p2"))
            col = lambda q: q.rearrange("p (i x) -> p i x", x=1)
            grp = lambda q: q.rearrange("p i (g j) -> p (i g) j", j=PER_GROUP)
            flat_g = lambda q: q.rearrange("p i g -> p (i g)")
            over16 = lambda q: col(q).to_broadcast([n, NT, E])
            over4 = lambda q: col(q).to_broadcast([n, NT, GROUPS])
            wide = lambda q: flat_g(q).rearrange("p (i x) -> p i x", x=1).to_broadcast([n, NT * GROUPS, PER_GROUP])
            tt, rdc = v.tensor_tensor, v.tensor_reduce
            link(v.memset(R["l"][:], 0.0))
            dve.wait_ge(s("rw"), 32 * l + 32)
            dve.wait_ge(s("logit"), NT * l + NT)
            nl = TILES[-1][1]
            tt(R["l"][0:n, 0:NT - 1, :], ps[0:n, 6, 0:E * (NT - 1)].rearrange("p (i e) -> p i e", e=E),
               rb[0:n, :].rearrange("p (x e) -> p x e", x=1).to_broadcast([n, NT - 1, E]), ALU.add)
            link(tt(R["l"][0:nl, NT - 1, :], ps[0:nl, 6, E * (NT - 1):E * NT], rb[0:nl, :], ALU.add))
            link(rdc(mx, lg, AX_X, ALU.max))
            tt(w, lg, over16(mx), ALU.subtract).then_inc(s("r_shift"), 1)
            dve.wait_ge(s("r_exp"), 1 * l + 1)
            link(rdc(z, pr, AX_X, ALU.add))
            link(v.reciprocal(z, z))
            link(tt(pr, pr, over16(z), ALU.mult))
            g4 = grp(pr)
            c4 = [g4[:, :, q] for q in range(4)]
            f = flat_g
            tt(f(ga), c4[0], c4[1], ALU.max)
            tt(f(gb), c4[0], c4[1], ALU.min)
            tt(f(gc), c4[2], c4[3], ALU.max)
            link(tt(f(gd), c4[2], c4[3], ALU.min))
            tt(f(ge), f(ga), f(gc), ALU.max)
            link(tt(f(gb), f(gb), f(gd), ALU.max))
            link(tt(f(gd), f(ga), f(gc), ALU.min))
            link(tt(f(gb), f(gb), f(gd), ALU.max))
            link(tt(f(ga), f(ge), f(gb), ALU.add))
            wt_g = wt4[0:n, :].rearrange("p (x g) -> p x g", x=1).to_broadcast([n, NT, GROUPS])
            wt_j = wt4[0:n, :].rearrange("p (x g) -> p x g", x=1).to_broadcast([n, NT * GROUPS, PER_GROUP])
            link(rdc(mx, ga, AX_X, ALU.max))
            link(tt(gb, ga, over4(mx), ALU.is_equal))
            link(tt(gb, gb, wt_g, ALU.mult))
            link(rdc(mx, gb, AX_X, ALU.max))
            link(tt(ge, gb, over4(mx), ALU.is_equal))
            cur = lg
            for dst in (m1, m2):
                link(rdc(f(ga), grp(cur), AX_X, ALU.max))
                link(tt(grp(w), grp(cur), wide(ga), ALU.is_equal))
                link(tt(grp(w), grp(w), wt_j, ALU.mult))
                link(rdc(f(gb), grp(w), AX_X, ALU.max))
                link(tt(grp(dst), grp(w), wide(gb), ALU.is_equal))
                if dst is m1:
                    link(v.scalar_tensor_tensor(out=s1, in0=dst, scalar=-3.0e38, in1=lg, op0=ALU.mult, op1=ALU.add))
                    cur = s1
            link(tt(grp(m1), grp(m1), wide(ge), ALU.mult))
            link(tt(grp(m2), grp(m2), wide(ge), ALU.mult))
            tt(x, m1, m2, ALU.add).then_inc(s("chosen"), 1)
            for m, p in ((m1, p1), (m2, p2)):
                link(tt(w, pr, m, ALU.mult))
                link(rdc(p, w, AX_X, ALU.add))
            link(tt(z, p1, p2, ALU.add))
            link(v.reciprocal(z, z))
            tt(gate[0:n, 0, :], p1, z, ALU.mult)
            link(tt(gate[0:n, 1, :], p2, z, ALU.mult))
            dve.wait_ge(s("ranked"), 1 * l + 1)
            nl = TILES[-1][1]
            link(v.memset(R["l"][:], 0.0))
            v.tensor_copy(R["l"][0:n, 0:NT - 1, :], ps[0:n, 7, 0:E * (NT - 1)].rearrange("p (i e) -> p i e", e=E))
            link(v.tensor_copy(R["l"][0:nl, NT - 1, :], ps[0:nl, 7, E * (NT - 1):E * NT]))
            link(v.tensor_scalar(w, lg, float(CAP), None, ALU.is_ge))
            for q in range(2, ROUNDS_MAX):
                link(v.scalar_tensor_tensor(out=w, in0=lg, scalar=float(CAP * q), in1=w, op0=ALU.is_ge, op1=ALU.add))
            link(v.scalar_tensor_tensor(out=w, in0=w, scalar=float(SLOTS - CAP), in1=lg, op0=ALU.mult, op1=ALU.add))
            link(tt(w, w, e128[0:n, :].rearrange("p (x e) -> p x e", x=1).to_broadcast([n, NT, E]), ALU.add))
            for k, (m, p) in enumerate(((m1, p1), (m2, p2))):
                link(tt(m, w, m, ALU.mult))
                link(rdc(p, m, AX_X, ALU.add))
                link(v.tensor_copy(slot[0:n, k, :], p))
            link(rdc(nrow[0:1, 0:1], ps[0:1, 7, E * NT:E * NT + E], AX_X, ALU.max))
            link(v.tensor_scalar(nrow[0:1, 1:2], nrow[0:1, 0:1], float(CAP), 1.0, ALU.is_gt, ALU.add))
            for q in range(2, ROUNDS_MAX):
                link(v.scalar_tensor_tensor(out=nrow[0:1, 1:2], in0=nrow[0:1, 0:1], scalar=float(CAP * q),
                                            in1=nrow[0:1, 1:2], op0=ALU.is_gt, op1=ALU.add))
            v.tensor_scalar(nstep[0:1, 0:1], nrow[0:1, 1:2], float(E), None, ALU.mult).then_inc(s("routed"), 1)

        mixed = ((s("y"), NT), (s("y"), 3 * NT))

        def step_count(eng, l):
            eng.wait_ge(s("routed"), l + 1)
            return eng.value_load(nstep[0:1, 0:1], min_val=E, max_val=E * ROUNDS_MAX)

        def experts_sp(sp_, l):
            L = f"_{l}"
            w3 = [a["moe_w_gate"][l].rearrange("e (k p) n -> p e k n", p=P),
                  a["moe_w_up"][l].rearrange("e (k p) n -> p e k n", p=P),
                  a["moe_w_down"][l].rearrange("e (k p) n -> p e k n", p=P)]

            def load(q, e, it):
                if isinstance(it, int) and it == 0:
                    if q < 2:
                        sp_.wait_ge(s("lo_done"), (7, 13)[l] + q)
                    else:
                        sp_.wait_ge(*mixed[l])
                else:
                    sp_.wait_ge(s(f"lo{q}" + L), it)
                src = w3[q][:, e:e + 1] if isinstance(e, int) else w3[q][:, bass.ds(e, 1)]
                src = src.rearrange("p e k n -> p (e k) n")
                sp_.dma_start(raw[q][:].rearrange("p (k n) -> p k n", k=src.shape[1]), src
                              ).then_inc(s(f"ld{q}" + L), 16)

            for q in range(3):
                load(q, 0, 0)
            load(0, 1, 1)
            load(1, 1, 1)
            with sp_.Fori(1, E - 1) as e:
                load(0, e + 1, e + 1)
                load(1, e + 1, e + 1)
                load(2, e, e)
            load(2, E - 1, E - 1)
            steps = step_count(sp_, l)
            with sp_.If(steps > E):
                with sp_.Fori(E, steps) as it:
                    for q in range(3):
                        load(q, it % E, it)

        def experts_pool(pool, l):
            L = f"_{l}"

            def load_x(it):
                if not (isinstance(it, int) and it == 0):
                    pool.wait_ge(s("p_xt" + L), it)
                rows = xg[bass.ds(it * CAP, CAP)] if not isinstance(it, int) else xg[it * CAP:it * CAP + CAP]
                pool.dma_start(xe[:], rows).then_inc(s("xe" + L), 16)

            def store_y(it):
                pool.wait_ge(s("y_ev" + L), it + 1)
                rows = yg[bass.ds((it + 1) * CAP - CAP, CAP)] if not isinstance(it, int) else yg[it * CAP:it * CAP + CAP]
                pool.dma_start(rows, ysb[:]).then_inc(s("y_st" + L), 16)

            load_x(0)
            load_x(1)
            load_x(2)
            with pool.Fori(2, E - 1) as it:
                load_x(it + 1)
                store_y(it - 2)
            for it in range(E - 3, E):
                store_y(it)
            steps = step_count(pool, l)
            with pool.If(steps > E):
                with pool.Fori(E, steps) as it:
                    load_x(it)
                    store_y(it)
                    pool.wait_ge(s("y_st" + L), it * 16 + 16)

        def experts_act(act, l):
            L, sa = f"_{l}", nc.scalar

            def hi(q, it, done):
                act.wait_ge(s(f"ld{q}" + L), it * 16 + 16)
                if not (isinstance(it, int) and it == 0):
                    act.wait_ge(s(done + L), it)
                sa.activation(whi[q][:], raw[q][:], ACT.Copy).then_inc(s(f"hi{q}" + L), 1)

            def xt_hi(it):
                act.wait_ge(s("p_xt" + L), it + 1)
                if not (isinstance(it, int) and it == 0):
                    act.wait_ge(s("p_u" + L), it)
                sa.activation(xet_hi[:].rearrange("p (a k) t -> p a (k t)", a=2), ps[:, 4:6, :],
                              ACT.Copy).then_inc(s("xth" + L), 1)

            def silu(it):
                act.wait_ge(s("p_g" + L), it + 1)
                if not (isinstance(it, int) and it == 0):
                    act.wait_ge(s("p_ht" + L), it)
                sa.activation(hx[:], ps[:, 0, :], ACT.Silu).then_inc(s("silu" + L), 1)

            def ht_hi_(it):
                act.wait_ge(s("p_ht" + L), it + 1)
                if not (isinstance(it, int) and it == 0):
                    act.wait_ge(s("p_d" + L), it)
                sa.activation(ht_hi[:].rearrange("p k t -> p (k t)"), ps[:, 6, :], ACT.Copy).then_inc(s("hth" + L), 1)

            def y_ev(it):
                act.wait_ge(s("p_d" + L), it + 1)
                if not (isinstance(it, int) and it == 0):
                    act.wait_ge(s("y_st" + L), it * 16)
                sa.activation(ysb[:].rearrange("p (a c) -> p a c", a=2), ps[:, 2:4, :], ACT.Copy).then_inc(s("y_ev" + L), 1)

            def step(it, prev=True, prev2=True, nxt=True):
                if prev:
                    silu(it - 1)
                    hi(2, it - 1, "p_d")
                if prev2:
                    y_ev(it - 2)
                if prev:
                    ht_hi_(it - 1)
                if nxt:
                    hi(0, it + 1, "p_g")
                    xt_hi(it + 1)
                    hi(1, it + 1, "p_u")

            act.wait_ge(*mixed[l])
            hi(0, 0, "")
            hi(1, 0, "")
            xt_hi(0)
            step(0, prev=False, prev2=False)
            step(1, prev2=False)
            with act.Fori(2, E - 1) as it:
                step(it)
            step(E - 1, nxt=False)
            step(E, nxt=False)
            y_ev(E - 1)
            steps = step_count(act, l)
            with act.If(steps > E):
                with act.Fori(E, steps) as it:
                    xt_hi(it)
                    hi(0, it, "p_g")
                    hi(1, it, "p_u")
                    silu(it)
                    ht_hi_(it)
                    hi(2, it, "p_d")
                    y_ev(it)

        def experts_dve(dve, l):
            L, v = f"_{l}", nc.vector

            def lo(q, it):
                dve.wait_ge(s(f"hi{q}" + L), it + 1)
                v.tensor_tensor(wlo[q][:], raw[q][:], whi[q][:].bitcast(F32), ALU.subtract).then_inc(s(f"lo{q}" + L), 1)

            def xt_lo(it):
                dve.wait_ge(s("xth" + L), it + 1)
                v.tensor_tensor(xet_lo[:].rearrange("p (a k) t -> p a (k t)", a=2), ps[:, 4:6, :],
                                xet_hi[:].bitcast(F32).rearrange("p (a k) t -> p a (k t)", a=2),
                                ALU.subtract).then_inc(s("xtl" + L), 1)

            def h(it):
                dve.wait_ge(s("silu" + L), it + 1)
                dve.wait_ge(s("p_u" + L), it + 1)
                v.tensor_tensor(hx[:], hx[:], ps[:, 1, :], ALU.mult).then_inc(s("h" + L), 1)

            def ht_lo_(it):
                dve.wait_ge(s("hth" + L), it + 1)
                v.tensor_tensor(ht_lo[:].rearrange("p k t -> p (k t)"), ps[:, 6, :],
                                ht_hi[:].bitcast(F32).rearrange("p k t -> p (k t)"), ALU.subtract).then_inc(s("htl" + L), 1)

            def step(it, prev=True, nxt=True):
                if prev:
                    h(it - 1)
                    lo(2, it - 1)
                    ht_lo_(it - 1)
                if nxt:
                    lo(0, it + 1)
                    xt_lo(it + 1)
                    lo(1, it + 1)

            lo(0, 0)
            lo(1, 0)
            xt_lo(0)
            step(0, prev=False)
            with dve.Fori(1, E - 1) as it:
                step(it)
            step(E - 1, nxt=False)
            step(E, nxt=False)
            steps = step_count(dve, l)
            with dve.If(steps > E):
                with dve.Fori(E, steps) as it:
                    xt_lo(it)
                    lo(0, it)
                    lo(1, it)
                    h(it)
                    ht_lo_(it)
                    lo(2, it)

        def experts_pe(pe, mm3, l):
            L, te = f"_{l}", nc.tensor
            first = lambda it: isinstance(it, int) and it == 0

            def xt(it):
                pe.wait_ge(s("xe" + L), it * 16 + 16)
                if not first(it):
                    pe.wait_ge(s("xtl" + L), it)
                for k in range(KT):
                    ins = te.transpose(ps[:, 4 + k // 4, P * (k % 4):P * (k % 4) + P], xe[:, P * k:P * k + P], ident[:])
                ins.then_inc(s("p_xt" + L), 1)

            def up(q, it, done):
                pe.wait_ge(s(f"lo{q}" + L), it + 1)
                pe.wait_ge(s("xtl" + L), it + 1)
                if not first(it):
                    pe.wait_ge(s(("silu" if q == 0 else "h") + L), it)
                wh = whi[q][:].rearrange("p (k n) -> p k n", k=KT)
                wl = wlo[q][:].rearrange("p (k n) -> p k n", k=KT)
                for k in range(KT):
                    ins = mm3(ps[:, q, :], xet_hi[:, k, :], xet_lo[:, k, :], wh[:, k, :], wl[:, k, :], k == 0, k == KT - 1)
                ins.then_inc(s(done + L), 1)

            def ht(it):
                pe.wait_ge(s("h" + L), it + 1)
                if not first(it):
                    pe.wait_ge(s("htl" + L), it)
                for k in range(4):
                    ins = te.transpose(ps[:, 6, P * k:P * k + P], hx[:, P * k:P * k + P], ident[:])
                ins.then_inc(s("p_ht" + L), 1)

            def down(it):
                pe.wait_ge(s("lo2" + L), it + 1)
                pe.wait_ge(s("htl" + L), it + 1)
                if not first(it):
                    pe.wait_ge(s("y_ev" + L), it)
                wh = whi[2][:].rearrange("p (k n) -> p k n", k=4)
                wl = wlo[2][:].rearrange("p (k n) -> p k n", k=4)
                for half in range(2):
                    cols = slice(512 * half, 512 * half + 512)
                    for k in range(4):
                        ins = mm3(ps[:, 2 + half, :], ht_hi[:, k, :], ht_lo[:, k, :], wh[:, k, cols], wl[:, k, cols],
                                  k == 0, k == 3)
                ins.then_inc(s("p_d" + L), 1)

            def step(it, prev=True, nxt=True):
                up(0, it, "p_g")
                if prev:
                    ht(it - 1)
                up(1, it, "p_u")
                if nxt:
                    xt(it + 1)
                if prev:
                    down(it - 1)

            xt(0)
            step(0, prev=False)
            with pe.Fori(1, E - 1) as it:
                step(it)
            step(E - 1, nxt=False)
            ht(E - 1)
            down(E - 1)
            steps = step_count(pe, l)
            with pe.If(steps > E):
                with pe.Fori(E, steps) as it:
                    xt(it)
                    up(0, it, "p_g")
                    up(1, it, "p_u")
                    ht(it)
                    down(it)

        def combine_pool(pool, l):
            L = f"_{l}"
            pool.wait_ge(s("y_st" + L), 16 * E)
            ln_gains_pool(pool, f"ffn{l}")

            def gather(rows):
                for i, (t0, n) in enumerate(TILES):
                    if i >= 2:
                        pool.wait_ge(s("comb"), NT * l + i - 1)
                    for k in range(2):
                        pool.indirect_dma_start(out=ygat[i % 2][k][0:n, :], out_offset=None, in_=rows,
                                                in_offset=bass.IndirectOffsetOnAxis(ap=slot[0:n, k, i:i + 1], axis=0)
                                                ).then_inc(s(f"got{i % 2}"), 16)

            steps = step_count(pool, l)
            with pool.If(steps > E):
                gather(yg)
            with pool.Else():
                gather(yg[0:SLOTS])

        def combine_dve(dve, link, l):
            L, v = f"_{l}", nc.vector
            for i, (t0, n) in enumerate(TILES):
                x = xtok[0:n, i, :]
                dve.wait_ge(s("sent"), 32 * NT * l + 32 * NT)
                link(v.tensor_scalar(x, x, ALPHA, None, ALU.mult))
                dve.wait_ge(s(f"got{i % 2}"), 32 * (l * (3 - i % 2) + i // 2 + 1))
                link(v.scalar_tensor_tensor(out=x, in0=ygat[i % 2][0][0:n, :], scalar=gate[0:n, 0, i:i + 1], in1=x,
                                            op0=ALU.mult, op1=ALU.add))
                v.scalar_tensor_tensor(out=x, in0=ygat[i % 2][1][0:n, :], scalar=gate[0:n, 1, i:i + 1], in1=x,
                                       op0=ALU.mult, op1=ALU.add).then_inc(s("comb"), 1)
                dve.wait_ge(s("comb"), NT * l + i + 1)
                ln_dve(dve, link, f"ffn{l}", i)

        def store_tokens(sp_, tag):
            yp, ys = o["y_prompt"][0], o["y_sample"][0]
            for i, (t0, n) in enumerate(TILES):
                sp_.wait_ge(s("ln_x"), NT * ln_no[tag] + i + 1)
                if t0 + n <= T_PROMPT:
                    parts = [(0, n, yp[t0:t0 + n])]
                else:
                    m = T_PROMPT - t0
                    parts = [(0, m, yp[t0:T_PROMPT]), (m, n - m, ys[0:n - m])]
                for r, m, rows in parts:
                    sp_.dma_start(rows, xtok[r:r + m, i, :]).then_inc(s("tokens_out"), 16)
            sp_.wait_ge(s("tokens_out"), 16 * (NT + 1))


        G, SP_, GC, CL = 64, 64, 16, 8
        NC_P, NC_S = T_PROMPT // CL, T_SAMPLE // CL
        NCH = NC_P + NC_S
        PAIRS = G // 2
        ar0 = SB0
        Z_AT, UT_AT = ar0, ar0 + (NCH + 2) * 2 * PAIRS * 4
        SPAD_AT = UT_AT + G * NCH * 4
        QP = 8
        W_AT = SPAD_AT + 2 * 2 * QP * 2 * NCH * 4
        CH_AT = W_AT + PAIRS * 2 * P * 4
        assert CH_AT + 2 * 4 * P * 8 <= FT_AT
        zst = at("s5_z", [P, NCH + 2, 2, PAIRS], Z_AT)
        ut = at("s5_ut", [P, G, NCH], UT_AT)
        spad = [at(f"s5_spad{i}", [P, 2, QP, 2, NCH], SPAD_AT + 4 * 2 * QP * 2 * NCH * i) for i in range(2)]
        wt = at("s5_wt", [P, PAIRS, CL, GC], SPAD_AT)
        assert PAIRS * P * 4 <= W_AT - SPAD_AT
        wl = at("s5_w", [P, 2, PAIRS, P], W_AT)
        u_g = at("s5_ug", [P, G, CL, GC], W_AT)
        mm_ = at("s5_m", [P, G, P], W_AT)
        ych = [at(f"s5_y{i}", [P, CL, P], CH_AT + 4096 * i) for i in range(2)]
        craw = at("s5_craw", [P, 2, 4, P // 2 * 2], CH_AT)
        ct = at("s5_ct", [P, 2, PAIRS, GC], CH_AT + 4096)
        u72 = at("s5_u", [P, CL, D], FT_AT)
        ksb = at("s5_k", [P, PAIRS, P], FT_AT)
        ox = at("s5_o", [P, 2, CL + 1, PAIRS, GC], YT_AT)
        otmp = wt
        q_at = [Z_AT]

        def pre(name):
            x = at("q_" + name, [P, P], q_at[0])
            q_at[0] += 512
            return x[0:PAIRS, :]
        q = {n: pre(n) for n in ("are", "aim", "x", "y", "t", "e", "ex", "r", "k", "sn", "sh", "cm", "co", "nr", "den",
                                 "ar", "ai", "fr", "fi", "w1", "w2", "sre", "sim", "so0", "so1", "so2", "so3")}
        qdt = at("q_dt", [P, 3, 2], q_at[0])[0:PAIRS]
        qd = at("q_d", [P, 2 * GC], q_at[0] + 32)[0:PAIRS]
        qdi = at("q_di", [P, 2], q_at[0] + 32 + 128, I32)[0:PAIRS]
        q_at[0] += 32
        taken[0] = shared_end
        bb0 = small("s5_b", [2, PAIRS, GC])
        bb = small("s5_bb", [2, PAIRS, GC])
        bd = small("s5_bd", [2, PAIRS, 2 * GC])
        t4 = small("s5_t4", [4, PAIRS])
        pw = at("s5_pw", [P, 2, CL + 1, PAIRS], q_at[0] + 160)
        assert q_at[0] + 160 + 8 * (CL + 1) * PAIRS <= Z_AT + (NC_P + 1) * 8 * PAIRS
        dk = at("s5_dk", [P, PAIRS], FT_AT + PAIRS * P * 4)
        eye = at("s5_eye", [P, GC], FT_AT + PAIRS * P * 4 + 128)
        stf = at("s5_stf", [P, 4, P], FT_AT + PAIRS * P * 4 + 256)
        pr_ = at("s5_pr", [P, 2, CL, PAIRS], CH_AT)
        a8 = at("s5_a8", [P, 2, 2, PAIRS], CH_AT + 2048)
        sctmp = at("s5_tmp", [P, 2, 2, PAIRS], CH_AT + 2048 + 512)
        sg = [at(f"sg{i}", [P, 512], YT_AT + 4 * CHUNK + 2048 * i) for i in range(2)]
        ub = [at(f"ub{i}", [P, D], YT_AT + 4096 * i) for i in range(2)]
        u_d = nc.dram_tensor("u_d", (T, D), F32, kind="Internal").ap()
        wis = a["w_in_s5"][0].rearrange("(k p) n -> p k n", p=P)
        wos = a["w_out_s5"][0].rearrange("(k p) n -> p k n", p=P)
        chunks1 = [wis[:, :, 0:512], wis[:, :, 512:D], wos[:, :, 0:512], wos[:, :, D:D + 512],
                   wos[:, :, 512:D], wos[:, :, D + 512:2 * D]]

        def pairs_of(x):
            return x.rearrange("(a b) p -> a (b p)", b=2)

        def s5_sp(sp_):
            def load(c):
                if c >= 2:
                    sp_.wait_ge(s("lo_done"), 8 + c - 1)
                sp_.dma_start(raw[c % 2][:].rearrange("p (k n) -> p k n", n=512), chunks1[c]).then_inc(s(f"w_landed{c % 2}"), 16)
            steps = step_count(sp_, 0)
            sp_.wait_ge(s("comb"), 1)
            load(0)
            load(1)
            for i, (t0, n) in enumerate(TILES):
                sp_.wait_ge(s("ub"), i + 1)
                sp_.dma_start(u_d[t0:t0 + n], ub[i % 2][0:n, :]).then_inc(s(f"u_out{i % 2}"), 16)
            sp_.wait_ge(s("u_out0"), 16 * 3)
            sp_.wait_ge(s("u_out1"), 16 * 2)
            sp_.wait_ge(s("u1"), NT)
            sp_.dma_start(u72[0:NCH].rearrange("n s c -> n (s c)"), u_d.rearrange("(n s) c -> n (s c)", s=CL)
                          ).then_inc(s("u72"), 16)
            sp_.wait_ge(s("lo_done"), 10)
            for dst, src in ((q["are"], pairs_of(a["s5_a_re"][0])), (q["aim"], pairs_of(a["s5_a_im"][0])),
                             (q["sre"], pairs_of(a["state_s5_re"][0, 0])), (q["sim"], pairs_of(a["state_s5_im"][0, 0])),
                             (qdt[:, 0, :], a["s5_log_dt"][0].rearrange("(a b) -> a b", b=2)),
                             (qd, a["s5_d"][0].rearrange("(a b) -> a b", b=2 * GC))):
                sp_.dma_start(dst, src).then_inc(s("s5_par"), 16)
            for ri, nm in enumerate(("re", "im")):
                b_src = a[f"s5_b_{nm}"][0].rearrange("(a b) p c -> (b p) a c", b=2)
                sp_.dma_start(bb0[:, ri], b_src).then_inc(s("s5_bc"), 16)
                c_src = a[f"s5_c_{nm}"][0].rearrange("(q j b) c p -> q b j c p", b=2, j=8)
                for qq in range(4):
                    for b in range(2):
                        sp_.dma_start(craw[:, ri, qq, 64 * b:64 * b + 64], c_src[qq, b]).then_inc(s("s5_bc"), 16)
            sp_.wait_ge(s("kd"), 1)
            sp_.wait_ge(s("m_zero"), 1)
            for st in range(CL):
                for b in range(2):
                    sp_.dma_start(mm_[GC * st:GC * st + GC, b::2, GC * st:P],
                                  ksb[GC * b:GC * b + GC, :, 0:P - GC * st]).then_inc(s("s5_m"), 16)
            sp_.wait_ge(s("stf"), 1)
            for i, nm in enumerate(("p_s5_re", "p_s5_im", "s_s5_re", "s_s5_im")):
                sp_.dma_start(pairs_of(o[nm][0, 0]), stf[0:PAIRS, i, :]).then_inc(s("s5_so"), 16)
            sp_.wait_ge(s("yt_s5"), 8)
            sp_.wait_ge(s("ytl_s5"), 8)
            load(2)
            load(3)
            load(4)
            load(5)
            sp_.wait_ge(s("s5_so"), 64)

        def by_group(i):
            return (u_g[0:NCH, 16 * i:16 * i + 16].rearrange("n g t c -> n t g c"),
                    u72[0:NCH, :, 256 * i:256 * i + 256].rearrange("n t (g c) -> n t g c", c=GC))

        def s5_pool(pool):
            g = nc.gpsimd
            pool.wait_ge(s("u1"), NT)
            pool.wait_ge(s("u72"), 16)
            for i in (1, 3):
                dst, src = by_group(i)
                g.tensor_copy(dst, src).then_inc(s("ug_pool"), 1)
            pool.wait_ge(s("bbar"), 1)
            g.memset(bd[:], 0.0).then_inc(s("bd"), 1)
            pool.wait_ge(s("bd"), 1)
            for b in range(2):
                r_ = slice(64 * b, 64 * b + 64)
                g.tensor_copy(bd[r_, :, :, GC * b:GC * b + GC], bb[r_]).then_inc(s("bd"), 1)
            pool.wait_ge(s("bd"), 3)
            pool.wait_ge(s("x_done"), 16)
            g.memset(mm_[:], 0.0).then_inc(s("m_zero"), 1)
            for i in range(2):
                if i == 0:
                    pool.wait_ge(s("s5_fill"), 16 + 16)
                g.memset(spad[i][:], 0.0).then_inc(s("spad0"), 1)
            ln_gains_after(pool)

        def ln_gains_after(pool):
            pool.wait_ge(s("yt_s5"), 8)
            ln_gains_pool(pool, "mix1")

        def s5_act(act):
            sa = nc.scalar
            def hi(c):
                act.wait_ge(s(f"w_landed{c % 2}"), count[c % 2] + 16 * (c // 2 + 1))
                if c >= 4:
                    act.wait_ge(s("y"), 2 * NT)
                sa.activation(whi[c % 2][:], raw[c % 2][:], ACT.Copy).then_inc(s("hi_done"), 1)
            for i, (t0, n) in enumerate(TILES):
                for hf_ in range(2):
                    b = 2 * (i % 2) + hf_
                    act.wait_ge(s("xt"), 2 * NT + 2 * i + hf_ + 1)
                    sa.activation(ft_hi[:, 4 * hf_:4 * hf_ + 4, t0:t0 + n],
                                  ps[:, b, :].rearrange("p (k t) -> p k t", t=P)[:, :, 0:n],
                                  ACT.Copy).then_inc(s("xt_hi"), 1)
                if i < 2:
                    hi(i)
            for i, (t0, n) in enumerate(TILES):
                act.wait_ge(s("u1"), i + 1)
                if i == 0:
                    act.wait_ge(s("comb"), NT)
                if i >= 2:
                    act.wait_ge(s(f"u_out{i % 2}"), 16 * (i // 2))
                b = 2 * (i % 2)
                sa.activation(ub[i % 2][0:n, :].rearrange("p (a c) -> p a c", a=2), ps[0:n, b:b + 2, :],
                              ACT.Copy).then_inc(s("ub"), 1)
            act.wait_ge(s("s5d"), 1)
            sa.activation(qdt[:, 1, :], qdt[:, 0, :], ACT.Tanh, scale=0.5).then_inc(s("s5a"), 1)
            act.wait_ge(s("s5d"), 2)
            sa.activation(q["t"], q["x"], ACT.Tanh, scale=0.5).then_inc(s("s5a"), 1)
            act.wait_ge(s("s5d"), 3)
            sa.activation(q["sn"], q["r"], ACT.Sin).then_inc(s("s5a"), 1)
            sa.activation(q["sh"], q["r"], ACT.Sin, scale=0.5).then_inc(s("s5a"), 1)
            act.wait_ge(s("s5_pt"), 2)
            sa.activation(t4[:].rearrange("p a b -> p (a b)"), ps[:, 0, 0:4 * PAIRS], ACT.Copy).then_inc(s("t4"), 1)
            sa.activation(zst[:, NC_P + 1].rearrange("p a b -> p (a b)"), ps[:, 0, 4 * PAIRS:6 * PAIRS],
                          ACT.Copy).then_inc(s("t4"), 1)
            sa.activation(ct[:].rearrange("p a b c -> p a (b c)"), ps[:, 1:3, :], ACT.Copy).then_inc(s("t4"), 1)
            act.wait_ge(s("u72"), 16)
            for i in (0, 2):
                dst, src = by_group(i)
                sa.activation(dst, src, ACT.Copy).then_inc(s("ug_act"), 1)
            for i in range(G // 4):
                act.wait_ge(s("s5_fill"), i + 1)
                sa.activation(ut[:, 4 * i:4 * i + 4, :].rearrange("p g n -> p (g n)"), ps[:, 3 + i % 2, 0:4 * NCH],
                              ACT.Copy).then_inc(s("s5_drain"), 1)
            for ri in range(2):
                for i in range(8):
                    act.wait_ge(s("s5_fill"), 16 + 8 * ri + i + 1)
                    sa.activation(wl[:, ri, 4 * i:4 * i + 4, :].rearrange("p a b -> p (a b)"), ps[:, 3 + i % 2, :],
                                  ACT.Copy).then_inc(s("s5_drain"), 1)
            for i in range(16):
                act.wait_ge(s("x_done"), i + 1)
                for ri in range(2):
                    for sl, n0, n1 in ((1, 0, NC_P), (2, NC_P, NCH)):
                        ins = sa.activation(zst[:, n0 + sl:n1 + sl, ri, 2 * i:2 * i + 2],
                                            ps[:, 5 + i % 2, 0:4 * NCH].rearrange("p (r a n) -> p r n a", r=2, a=2)[:, ri, n0:n1],
                                            ACT.Copy)
                ins.then_inc(s("x_in"), 1)
            for i in range(8):
                act.wait_ge(s("s5_fill"), 32 + i + 1)
                sa.activation(ksb[0:2 * GC, 4 * i:4 * i + 4, :].rearrange("p a b -> p (a b)"), ps[0:2 * GC, 3 + i % 2, :],
                              ACT.Copy).then_inc(s("s5_drain"), 1)
            sa.activation(dk[0:2 * GC, :], ps[0:2 * GC, 7, 0:PAIRS], ACT.Copy).then_inc(s("s5_drain"), 1)
            act.wait_ge(s("z_done"), NCH)
            act.wait_ge(s("spad0"), 2)
            act.wait_ge(s("s5_pt"), 3)
            sa.activation(stf[0:PAIRS].rearrange("p a b -> p (a b)"), ps[0:PAIRS, 0, :], ACT.Copy).then_inc(s("stf"), 1)
            for c in range(4):
                if c >= 2:
                    act.wait_ge(s("y_mm"), 2 * (c - 1))
                for b in range(2):
                    r_ = slice(64 * b, 64 * b + 64)
                    for n0, n1, sl in ((0, NC_P, 0), (NC_P, NCH, 1)):
                        ins = sa.activation(spad[c % 2][r_, :, :, b, n0:n1],
                                            zst[r_, n0 + sl:n1 + sl, :, QP * c:QP * c + QP].rearrange("p n r a -> p r a n"),
                                            ACT.Copy)
                ins.then_inc(s("spad"), 1)
                for u in range(2):
                    i = 2 * c + u
                    act.wait_ge(s("y_mm"), i + 1)
                    if i >= 2:
                        act.wait_ge(s("yt_s5"), i - 1)
                    for hb_ in range(2):
                        ins = sa.activation(ych[i % 2][0:NCH, :, 64 * hb_:64 * hb_ + 64].rearrange("n t (g c) -> n g t c", c=GC),
                                            ps[0:NCH, 2 * (i % 2) + hb_, :].rearrange("n (g t c) -> n g t c", g=4, c=GC),
                                            ACT.Gelu_apprx_tanh)
                    ins.then_inc(s("y_gelu"), 1)
                    act.wait_ge(s("yt_s5"), i + 1)
                    for hb_ in range(2):
                        ins = sa.activation(ft_hi[:, i, :].rearrange("p (n t) -> p t n", t=CL)[:, 4 * hb_:4 * hb_ + 4, :],
                                            ps[:, 4 + 2 * (i % 2) + hb_, 0:4 * NCH].rearrange("p (t n) -> p t n", n=NCH), ACT.Copy)
                    ins.then_inc(s("yth_s5"), 1)
            hi(2)
            hi(3)
            for ph in range(2):
                for i, (t0, n) in enumerate(TILES):
                    j = NT * ph + i
                    act.wait_ge(s("y"), NT + j + 1)
                    if j >= 2:
                        act.wait_ge(s("mix1_glu"), 2 * j - 2)
                    sa.activation(sg[j % 2][0:n, :], ps[0:n, 2 * (j % 2) + 1, :], ACT.Sigmoid).then_inc(s("sg"), 1)
                    if ph and i:
                        ln_act(act, "mix1", [i - 1])
                if ph == 0:
                    hi(4)
                    hi(5)
            ln_act(act, "mix1", [NT - 1])

        def s5_dve(dve, link, split_lo):
            v = nc.vector
            tt, ts = v.tensor_tensor, v.tensor_scalar
            def lo(c):
                dve.wait_ge(s("hi_done"), 8 + c + 1)
                tt(wlo[c % 2][:], raw[c % 2][:], whi[c % 2][:].bitcast(F32), ALU.subtract).then_inc(s("lo_done"), 1)
            for i, (t0, n) in enumerate(TILES):
                for hf_ in range(2):
                    b = 2 * (i % 2) + hf_
                    dve.wait_ge(s("xt_hi"), 2 * NT + 2 * i + hf_ + 1)
                    ins = tt(ft_lo[:, 4 * hf_:4 * hf_ + 4, t0:t0 + n],
                             ps[:, b, :].rearrange("p (k t) -> p k t", t=P)[:, :, 0:n],
                             ft_hi[:, 4 * hf_:4 * hf_ + 4, t0:t0 + n].bitcast(F32), ALU.subtract)
                ins.then_inc(s("x_split"), 1)
                if i < 2:
                    lo(i)
            M, A_, S_ = ALU.mult, ALU.add, ALU.subtract
            MAGIC = 12582912.0
            LN2_HI = 0.693145751953125
            LN2_LO = 0.6931471805599453 - LN2_HI
            d0, d1, d2 = (qdt[:, i, :] for i in range(3))
            dve.wait_ge(s("s5_par"), 16 * 6)
            dve.wait_ge(s("u1"), NT)
            link(ts(d2, d0, 1.0 / 0.6931471805599453, MAGIC, M, A_))
            link(ts(d2, d2, MAGIC, None, S_))
            link(v.scalar_tensor_tensor(out=d0, in0=d2, scalar=-LN2_HI, in1=d0, op0=M, op1=A_))
            v.scalar_tensor_tensor(out=d0, in0=d2, scalar=-LN2_LO, in1=d0, op0=M, op1=A_).then_inc(s("s5d"), 1)
            link(ts(d2, d2, 127.0, 8388608.0, A_, M))
            link(v.tensor_copy(qdi, d2))
            dve.wait_ge(s("s5a"), 1)
            link(ts(d2, d1, -1.0, 1.0, M, A_))
            link(v.reciprocal(d2, d2))
            link(ts(d1, d1, 1.0, None, A_))
            link(tt(d0, d1, d2, M))
            link(tt(d0, d0, qdi.bitcast(F32), M))
            two = lambda x: x.rearrange("p (b k) -> p b k", b=2)
            dtb = d0.rearrange("p (b x) -> p b x", x=1).to_broadcast([PAIRS, 2, SP_])
            tt(two(q["y"]), two(q["aim"]), dtb, M)
            tt(two(q["x"]), two(q["are"]), dtb, M).then_inc(s("s5d"), 1)
            dve.wait_ge(s("s5d"), 2)
            C1 = 6.28125
            C2 = 0.0019350051879882812
            C3 = 6.283185307179586 - C1 - C2
            link(ts(q["k"], q["y"], 1.0 / 6.283185307179586, MAGIC, M, A_))
            link(ts(q["k"], q["k"], MAGIC, None, S_))
            link(v.scalar_tensor_tensor(out=q["r"], in0=q["k"], scalar=-C1, in1=q["y"], op0=M, op1=A_))
            link(v.scalar_tensor_tensor(out=q["r"], in0=q["k"], scalar=-C2, in1=q["r"], op0=M, op1=A_))
            link(v.scalar_tensor_tensor(out=q["r"], in0=q["k"], scalar=-C3, in1=q["r"], op0=M, op1=A_))
            ts(q["r"], q["r"], 3.1415925, -3.1415925, ALU.min, ALU.max).then_inc(s("s5d"), 1)
            dve.wait_ge(s("s5a"), 2)
            link(ts(q["w1"], q["t"], -1.0, 1.0, M, A_))
            link(v.reciprocal(q["w1"], q["w1"]))
            link(v.scalar_tensor_tensor(out=q["e"], in0=q["t"], scalar=2.0, in1=q["w1"], op0=M, op1=M))
            link(ts(q["ex"], q["e"], 1.0, None, A_))
            dve.wait_ge(s("s5a"), 4)
            link(tt(q["cm"], q["sh"], q["sh"], M))
            link(ts(q["co"], q["cm"], -2.0, 1.0, M, A_))
            link(tt(q["ar"], q["ex"], q["co"], M))
            link(tt(q["ai"], q["ex"], q["sn"], M))
            link(tt(q["nr"], q["e"], q["co"], M))
            link(v.scalar_tensor_tensor(out=q["nr"], in0=q["cm"], scalar=-2.0, in1=q["nr"], op0=M, op1=A_))
            link(tt(q["w1"], q["are"], q["are"], M))
            link(tt(q["w2"], q["aim"], q["aim"], M))
            link(tt(q["den"], q["w1"], q["w2"], A_))
            link(v.reciprocal(q["den"], q["den"]))
            link(tt(q["w1"], q["nr"], q["are"], M))
            link(tt(q["w2"], q["ai"], q["aim"], M))
            link(tt(q["w1"], q["w1"], q["w2"], A_))
            link(tt(q["fr"], q["w1"], q["den"], M))
            link(tt(q["w1"], q["ai"], q["are"], M))
            link(tt(q["w2"], q["nr"], q["aim"], M))
            link(tt(q["w1"], q["w1"], q["w2"], S_))
            tt(q["fi"], q["w1"], q["den"], M).then_inc(s("s5d"), 1)
            dve.wait_ge(s("t4"), 3)
            link(v.memset(pw[:, 1, 0, :], 0.0))
            link(v.memset(pw[:, 0, 0, :], 1.0))
            link(v.tensor_copy(pw[:, :, 1, :], t4[:, 0:2, :]))
            tm = sctmp[:].rearrange("p a b n -> p (a b) n")

            def cmul(lo_, n, by):
                ar_, ai_ = (pw[:, r_, lo_:lo_ + n, :] for r_ in range(2))
                br_, bi_ = (pw[:, r_, by:by + 1, :].to_broadcast([P, n, PAIRS]) for r_ in range(2))
                out = slice(lo_ + by, lo_ + by + n)
                tr = tm[:, 0:n, :]
                link(tt(pw[:, 0, out, :], ar_, br_, M))
                link(tt(tr, ai_, bi_, M))
                link(tt(pw[:, 0, out, :], pw[:, 0, out, :], tr, S_))
                link(tt(pw[:, 1, out, :], ar_, bi_, M))
                link(tt(tr, ai_, br_, M))
                link(tt(pw[:, 1, out, :], pw[:, 1, out, :], tr, A_))
            cmul(1, 1, 1)
            cmul(1, 2, 2)
            cmul(1, 4, 4)
            dve.wait_ge(s("s5_bc"), 16 * 18)
            over = lambda x: x.rearrange("p (a x) -> p a x", x=1).to_broadcast([P, PAIRS, GC])
            fr, fi = over(t4[:, 2, :]), over(t4[:, 3, :])
            tb = wt[:].rearrange("p a b c -> p (a b c)")[:, 0:PAIRS * GC].rearrange("p (a c) -> p a c", c=GC)
            link(tt(bb[:, 0], bb0[:, 0], fr, M))
            link(tt(tb, bb0[:, 1], fi, M))
            link(tt(bb[:, 0], bb[:, 0], tb, S_))
            link(tt(bb[:, 1], bb0[:, 1], fr, M))
            link(tt(tb, bb0[:, 0], fi, M))
            tt(bb[:, 1], bb[:, 1], tb, A_).then_inc(s("bbar"), 1)
            dve.wait_ge(s("bbar"), 1)
            cr, ci = ct[:, 0], ct[:, 1]
            ot = otmp[:].rearrange("p a b c -> p (a b c)")
            for tau in range(CL + 1):
                pr0, pi0 = over(pw[:, 0, tau, :]), over(pw[:, 1, tau, :])
                ta, tb_ = (ot[:, 512 * (2 * (tau % 2) + x):512 * (2 * (tau % 2) + x) + 512].rearrange("p (a c) -> p a c", c=GC) for x in range(2))
                tt(ta, ci, pi0, M).then_inc(s("o_c"), 1)
                tt(tb_, ci, pr0, M).then_inc(s("o_c"), 1)
                tt(ox[:, 0, tau], cr, pr0, M).then_inc(s("o_c"), 1)
                tt(ox[:, 1, tau], cr, pi0, M).then_inc(s("o_c"), 1)
                dve.wait_ge(s("o_c"), 6 * tau + 3)
                tt(ox[:, 0, tau], ox[:, 0, tau], ta, S_).then_inc(s("o_c"), 1)
                dve.wait_ge(s("o_c"), 6 * tau + 4)
                v.scalar_tensor_tensor(out=ox[:, 1, tau].rearrange("p a c -> p (a c)"),
                                       in0=ox[:, 1, tau].rearrange("p a c -> p (a c)"), scalar=-1.0,
                                       in1=tb_.rearrange("p a c -> p (a c)"), op0=M, op1=S_).then_inc(s("o_c"), 1)
                dve.wait_ge(s("o_c"), 6 * tau + 6)
            for st in range(CL):
                v.tensor_copy(pr_[:, :, st, :], pw[:, :, CL - 1 - st, :])
            for r_ in range(2):
                link(v.tensor_copy(a8[:, 0, r_, :], pw[:, 0, CL, :]))
            link(v.tensor_copy(a8[:, 1, 0, :], pw[:, 1, CL, :]))
            link(ts(a8[:, 1, 1, :], pw[:, 1, CL, :], -1.0, None, M))
            for ri in range(2):
                if ri:
                    dve.wait_ge(s("s5_fill"), 16 + 8)
                for st in range(CL):
                    x0, x1 = over(pr_[:, 0, st, :]), over(pr_[:, 1, st, :])
                    first, second = (x0, x1) if ri == 0 else (x1, x0)
                    dst = wt[:, :, st, :]
                    tmp = bb0[:, st % 2]
                    tt(dst, bb[:, 0], first, M).then_inc(s("w_m"), 1)
                    tt(tmp, bb[:, 1], second, M).then_inc(s("w_m"), 1)
                    dve.wait_ge(s("w_m"), 3 * (8 * ri + st) + 2)
                    tt(dst, dst, tmp, S_ if ri == 0 else A_).then_inc(s("w_m"), 1)
                    dve.wait_ge(s("w_m"), 3 * (8 * ri + st) + 3)
            dve.wait_ge(s("x_in"), 16)
            link(v.memset(zst[:, 0], 0.0))
            nz = 0
            cnt = 0
            for n in range(NCH):
                sl = n + (n >= NC_P)
                z0, z1 = zst[:, sl], zst[:, sl + 1]
                ta, tb_ = sctmp[:, 0], sctmp[:, 1]
                if n:
                    dve.wait_ge(s("z_done"), n)
                tt(ta, z0, a8[:, 0], M).then_inc(s("z_a"), 1)
                for r_ in range(2):
                    ins = tt(tb_[:, 1 - r_, :], z0[:, r_, :], a8[:, 1, r_, :], M)
                ins.then_inc(s("z_a"), 1)
                dve.wait_ge(s("z_a"), 3 * n + 1)
                tt(z1, z1, ta, A_).then_inc(s("z_a"), 1)
                dve.wait_ge(s("z_a"), 3 * n + 3)
                tt(z1, z1, tb_, A_).then_inc(s("z_done"), 1)
            dve.wait_ge(s("z_done"), NCH)
            dve.wait_ge(s("s5_drain"), 32 + 9)
            g2 = 2 * GC
            link(tt(eye[0:g2, :], ident[0:g2, 0:GC], ident[0:g2, GC:g2], A_))
            tmp = bb0[0:g2, 0]
            link(tt(tmp, dk[0:g2, :].rearrange("p (a x) -> p a x", x=1).to_broadcast([g2, PAIRS, GC]),
                    eye[0:g2, :].rearrange("p (x c) -> p x c", x=1).to_broadcast([g2, PAIRS, GC]), M))
            tt(ksb[0:g2, :, 0:GC], ksb[0:g2, :, 0:GC], tmp, A_).then_inc(s("kd"), 1)
            dve.wait_ge(s("s5_so"), 64)
            for i in range(8):
                dve.wait_ge(s("yth_s5"), i + 1)
                for hb_ in range(2):
                    dst = ft_lo[:, i, :].rearrange("p (n t) -> p t n", t=CL)[:, 4 * hb_:4 * hb_ + 4, :]
                    ins = tt(dst, ps[:, 4 + 2 * (i % 2) + hb_, 0:4 * NCH].rearrange("p (t n) -> p t n", n=NCH),
                             ft_hi[:, i, :].bitcast(F32).rearrange("p (n t) -> p t n", t=CL)[:, 4 * hb_:4 * hb_ + 4, :], S_)
                ins.then_inc(s("ytl_s5"), 1)
            lo(2)
            lo(3)
            for ph in range(2):
                if ph:
                    lo(4)
                    lo(5)
                for i, (t0, n) in enumerate(TILES):
                    j = NT * ph + i
                    dve.wait_ge(s("sg"), j + 1)
                    x = xtok[0:n, i, 512 * ph:512 * ph + 512]
                    tt(sg[j % 2][0:n, :], sg[j % 2][0:n, :], ps[0:n, 2 * (j % 2), :], M).then_inc(s("mix1_glu"), 1)
                    dve.wait_ge(s("mix1_glu"), 2 * j + 1)
                    v.scalar_tensor_tensor(out=x, in0=x, scalar=ALPHA, in1=sg[j % 2][0:n, :], op0=M,
                                           op1=A_).then_inc(s("mix1_glu"), 1)
                    if ph:
                        dve.wait_ge(s("mix1_glu"), 2 * j + 2)
                        ln_dve(dve, link, "mix1", i)

        def s5_pe(pe, mm3):
            te = nc.tensor
            for i, (t0, n) in enumerate(TILES):
                pe.wait_ge(s("ln_x"), NT + i + 1)
                if i >= 2:
                    pe.wait_ge(s("x_split"), NT + i - 1)
                for k in range(KT):
                    b = 2 * (i % 2) + k // 4
                    ins = te.transpose(ps[:, b, P * (k % 4):P * (k % 4) + n], xtok[0:n, i, P * k:P * k + P], ident[0:n, 0:n])
                    if k % 4 == 3:
                        ins.then_inc(s("xt"), 1)
            pe.wait_ge(s("x_split"), 2 * NT)
            pe.wait_ge(s("lo_done"), 10)

            def token_major(i, l_hi, l_lo, sem_):
                t0, n = TILES[i]
                for half in range(2):
                    wh = whi[half][:].rearrange("p (k n) -> p k n", n=512)
                    wl_ = wlo[half][:].rearrange("p (k n) -> p k n", n=512)
                    for k in range(KT):
                        ins = mm3(ps[0:n, 2 * (sem_[1] % 2) + half, :], l_hi[:, k, t0:t0 + n], l_lo[:, k, t0:t0 + n],
                                  wh[:, k, :], wl_[:, k, :], k == 0, k == KT - 1)
                ins.then_inc(s(sem_[0]), 1)

            for i in range(NT):
                if i >= 2:
                    pe.wait_ge(s("ub"), i - 1)
                token_major(i, ft_hi, ft_lo, ("u1", i))
            pe.wait_ge(s("s5d"), 4)
            pe.wait_ge(s("s5_bc"), 16 * 18)
            pe.wait_ge(s("ub"), NT)
            for i, nm in enumerate(("ar", "ai", "fr", "fi", "sre", "sim")):
                te.transpose(ps[:, 0, PAIRS * i:PAIRS * i + PAIRS], q[nm], ident[0:PAIRS, 0:PAIRS])
            te.transpose(ps[0:2 * GC, 7, 0:PAIRS], qd, ident[0:PAIRS, 0:PAIRS]).then_inc(s("s5_pt"), 1)
            for ri in range(2):
                for qq in range(4):
                    ins = te.transpose(ps[:, 1 + ri, P * qq:P * qq + P], craw[:, ri, qq, :], ident[:])
            ins.then_inc(s("s5_pt"), 1)
            for i in range(G // 4):
                if i % 4 == 0:
                    pe.wait_ge(s("ug_pool" if i % 8 else "ug_act"), i // 8 + 1)
                if i >= 2:
                    pe.wait_ge(s("s5_drain"), i - 1)
                for j in range(4):
                    g_ = 4 * i + j
                    ins = te.transpose(ps[:, 3 + i % 2, NCH * j:NCH * j + NCH], u_g[0:NCH, g_].rearrange("n t c -> n (t c)"),
                                       ident[0:NCH, 0:NCH])
                ins.then_inc(s("s5_fill"), 1)
            for ri in range(2):
                pe.wait_ge(s("w_m"), 24 * (ri + 1))
                for i in range(8):
                    pe.wait_ge(s("s5_drain"), 16 + 8 * ri + i - 1)
                    for j in range(4):
                        ins = te.transpose(ps[:, 3 + i % 2, P * j:P * j + P], wt[:, 4 * i + j].rearrange("p a b -> p (a b)"),
                                           ident[:])
                    ins.then_inc(s("s5_fill"), 1)
            pe.wait_ge(s("s5_drain"), 32)
            for i in range(16):
                if i >= 2:
                    pe.wait_ge(s("x_in"), i - 1)
                for ri in range(2):
                    for j in range(2):
                        for b in range(2):
                            pair = 2 * i + j
                            c0 = (2 * ri + j) * NCH
                            ins = te.matmul(ps[64 * b:64 * b + 64, 5 + i % 2, c0:c0 + NCH],
                                            wl[:, ri, pair, 64 * b:64 * b + 64], ut[:, 2 * pair + b, :], start=True, stop=True)
                ins.then_inc(s("x_done"), 1)
            pe.wait_ge(s("bd"), 3)
            for i in range(8):
                if i >= 2:
                    pe.wait_ge(s("s5_drain"), 32 + i - 1)
                for j in range(4):
                    pair = 4 * i + j
                    for ri in range(2):
                        ins = te.matmul(ps[0:2 * GC, 3 + i % 2, P * j:P * j + P], bd[:, ri, pair, :],
                                        ox[:, ri, 0:CL, pair, :], start=(ri == 0), stop=(ri == 1))
                ins.then_inc(s("s5_fill"), 1)
            pe.wait_ge(s("z_done"), NCH)
            for i, (sl, ri) in enumerate(((NC_P, 0), (NC_P, 1), (NCH + 1, 0), (NCH + 1, 1))):
                ins = te.transpose(ps[0:PAIRS, 0, P * i:P * i + P], zst[:, sl, ri, :], ident[:])
            ins.then_inc(s("s5_pt"), 1)
            pe.wait_ge(s("s5_m"), 16 * 16)
            pe.wait_ge(s("stf"), 1)
            pe.wait_ge(s("s5_drain"), 32 + 9)
            pe.wait_ge(s("x_in"), 16)
            for i in range(8):
                pe.wait_ge(s("spad"), i // 2 + 1)
                if i >= 2:
                    pe.wait_ge(s("y_gelu"), i - 1)
                for j in range(8):
                    g_ = 8 * i + j
                    pair, b = g_ // 2, g_ % 2
                    out = ps[0:NCH, 2 * (i % 2) + j // 4, P * (j % 4):P * (j % 4) + P]
                    te.matmul(out, ut[:, g_, :], mm_[:, g_, :], start=True, stop=False)
                    for ri in range(2):
                        ins = te.matmul(out, spad[(i // 2) % 2][:, ri, pair % QP, b, :], ox[:, ri, 1:CL + 1, pair, :],
                                        start=False, stop=(ri == 1))
                ins.then_inc(s("y_mm"), 1)
                pe.wait_ge(s("y_gelu"), i + 1)
                if i >= 2:
                    pe.wait_ge(s("ytl_s5"), i - 1)
                for st in range(CL):
                    ins = te.transpose(ps[:, 4 + 2 * (i % 2) + st // 4, NCH * (st % 4):NCH * (st % 4) + NCH],
                                       ych[i % 2][0:NCH, st, :], ident[0:NCH, 0:NCH])
                ins.then_inc(s("yt_s5"), 1)
            pe.wait_ge(s("ytl_s5"), 8)
            for ph in range(2):
                pe.wait_ge(s("lo_done"), 12 + 2 * ph)
                for i in range(NT):
                    j = NT * ph + i
                    if j >= 2:
                        pe.wait_ge(s("mix1_glu"), 2 * j - 2)
                    token_major(i, ft_hi, ft_lo, ("y", j))

        block = ctx.enter_context(nc.Block())

        @block.sync
        def _(sp_):
            def load_chunk(c):
                if c >= 2:
                    sp_.wait_ge(s("lo_done"), c - 1)
                for src, col, n in chunks0[c]:
                    dst = raw[c % 2][:].rearrange("p (k n) -> p k n", n=512)[:, :, col:col + n]
                    sp_.dma_start(dst, src).then_inc(s(f"w_landed{c % 2}"), 16)

            for i, (t0, n) in enumerate(TILES):
                if i >= 2:
                    sp_.wait_ge(s("x_split"), i - 1)
                for r, m, rows in x_rows(t0, n):
                    sp_.dma_start(xin[i % 2][r:r + m, :], rows).then_inc(s(f"x_landed{i % 2}"), 16)
                if i < 2:
                    load_chunk(i)
            for c in range(2, len(chunks0)):
                load_chunk(c)
            for i, (t0, n) in enumerate(TILES):
                sp_.wait_ge(s("ycat_lo"), KT)
                for r, m, rows in x_rows(t0, n):
                    sp_.dma_start(xtok[r:r + m, i, :], rows).then_inc(s("res_landed"), 16)
            sp_.wait_ge(s("res_landed"), 16 * (NT + 1))
            experts_sp(sp_, 0)
            s5_sp(sp_)
            experts_sp(sp_, 1)
            store_tokens(sp_, "ffn1")

        @block.gpsimd
        def _(pool):
            g = nc.gpsimd
            g.memset(ident[:], 0.0).then_inc(s("pc"), 1)
            g.memset(causal[:], 1.0).then_inc(s("pc"), 1)
            g.memset(blkmask[:], 1.0).then_inc(s("pc"), 1)
            g.memset(ones[:], 1.0).then_inc(s("pc"), 1)
            g.memset(m0[:], 1.0).then_inc(s("pc"), 1)
            g.memset(eps[:, 0:1], RMS_EPS).then_inc(s("pc"), 1)
            g.memset(eps[:, 1:2], LN_EPS).then_inc(s("pc"), 1)
            g.memset(lstrict[:], 1.0).then_inc(s("pc"), 1)
            for q in range(PER_GROUP):
                g.memset(wt4[:, q:q + 1], float(PER_GROUP - q)).then_inc(s("pc"), 1)
            for q in range(E):
                g.memset(e128[:, q:q + 1], float(CAP * q)).then_inc(s("pc"), 1)
            g.memset(zeros[:], 0.0).then_inc(s("pc"), 1)
            pool.wait_ge(s("pc"), 29)
            for q in range(E):
                pool.dma_start(xg[CAP * q:CAP * q + CAP], zeros[:]).then_inc(s("xg_zero"), 16)
            g.affine_select(out=lstrict[:], in_=lstrict[:], compare_op=ALU.is_ge, fill=0.0, base=-1,
                            pattern=[[1, P]], channel_multiplier=-1).then_inc(s("pc"), 1)
            g.affine_select(out=ident[:], in_=ident[:], compare_op=ALU.not_equal, fill=1.0, base=0,
                            pattern=[[-1, P]], channel_multiplier=1).then_inc(s("pc"), 1)
            g.affine_select(out=causal[:], in_=causal[:], compare_op=ALU.is_ge, fill=0.0, base=0,
                            pattern=[[1, P]], channel_multiplier=-1).then_inc(s("pc"), 1)
            g.affine_select(out=blkmask[:], in_=blkmask[:], compare_op=ALU.is_ge, fill=0.0, base=0,
                            pattern=[[-BLK, 8]], channel_multiplier=1).then_inc(s("pc"), 1)
            g.memset(m0[:, 0:1], 0.0).then_inc(s("pc"), 1)
            pool.wait_ge(s("pc"), 34)
            g.affine_select(out=blkmask[:], in_=blkmask[:], compare_op=ALU.is_ge, fill=0.0, base=BLK - 1,
                            pattern=[[BLK, 8]], channel_multiplier=-1).then_inc(s("pc"), 1)
            g.affine_select(out=causal[:].rearrange("p (b i) -> p b i", i=BLK),
                            in_=causal[:].rearrange("p (b i) -> p b i", i=BLK),
                            compare_op=ALU.is_ge, fill=0.0, base=0, pattern=[[-BLK, 8], [0, BLK]],
                            channel_multiplier=1).then_inc(s("pc"), 1)
            for k, (dst, src) in enumerate(param_dmas):
                with nc.allow_non_contiguous_dma(reason="per-channel parameters, one word to a partition"):
                    pool.dma_start(dst, src).then_inc(s("params"), 16)
            g.memset(wr[:], 0.0).then_inc(s("wz"), 1)
            g.memset(wi[:], 0.0).then_inc(s("wz"), 1)
            for i in range(2):
                g.memset(zx[i][:, 0:CONV - 1], 0.0).then_inc(s("wz"), 1)
                g.memset(zx[i][:, LRU_W - 1:LRU_W], 0.0).then_inc(s("wz"), 1)
            pool.wait_ge(s("wz"), 6)
            for j in range(LRU_TILES):
                if j:
                    pool.wait_ge(s("ri"), j)
                if j >= 2:
                    pool.wait_ge(s("u_done"), j - 1)
                    pool.wait_ge(s(f"conv_out{j % 2}"), 32 * (j // 2))
                for hh in range(2):
                    r = slice(64 * hh, 64 * hh + 64)
                    pool.dma_start(wr[r, 64 * hh:64 * hh + 64], a["lru_w_r"][0, 2 * j + hh]).then_inc(s("wri"), 16)
                    pool.dma_start(wi[r, 64 * hh:64 * hh + 64], a["lru_w_i"][0, 2 * j + hh]).then_inc(s("wri"), 16)
                with nc.allow_non_contiguous_dma(reason="3 past conv rows to a channel"):
                    pool.dma_start(zx[j % 2][:, S0_AT:S0_AT + CONV - 1],
                                   a["state_lru_conv"][0, 0, :, P * j:P * j + P].rearrange("k p -> p k")
                                   ).then_inc(s("wri"), 16)
                pool.wait_ge(s("z_free"), 4 * (j // 2) + j % 2 + 1)
                with nc.allow_non_contiguous_dma(reason="3 conv rows to a channel"):
                    pool.dma_start(o["p_lru_conv"][0, 0, :, P * j:P * j + P].rearrange("k p -> p k"),
                                   zx[j % 2][:, T_PROMPT:T_PROMPT + 3]).then_inc(s(f"conv_out{j % 2}"), 16)
                    pool.dma_start(o["s_lru_conv"][0, 0, :, P * j:P * j + P].rearrange("k p -> p k"),
                                   zx[j % 2][:, S0_AT + T_SAMPLE:S0_AT + T_SAMPLE + 3]).then_inc(s(f"conv_out{j % 2}"), 16)
                pool.wait_ge(s("scan"), 2 * (j + 1))
                with nc.allow_non_contiguous_dma(reason="one state word to a channel"):
                    pool.dma_start(o["p_lru_h"][0, 0, P * j:P * j + P].rearrange("(p x) -> p x", x=1),
                                   lr[:, T_PROMPT - 1:T_PROMPT]).then_inc(s("h_out"), 16)
                    pool.dma_start(o["s_lru_h"][0, 0, P * j:P * j + P].rearrange("(p x) -> p x", x=1),
                                   lr[:, S0_AT + T_SAMPLE - 1:S0_AT + T_SAMPLE]).then_inc(s("h_out"), 16)
            pool.wait_ge(s("ycat_lo"), LRU_TILES)
            pool.wait_ge(s("h_out"), 32 * LRU_TILES)
            for i in range(2):
                pool.wait_ge(s(f"conv_out{i}"), 16 * LRU_TILES)
            for h in range(HEADS):
                for tt, (t0, n) in enumerate(HTILES):
                    i = 5 * h + tt
                    nb = n // BLK
                    pool.wait_ge(s("hg_tok"), 4 * h + 2)
                    if i:
                        pool.wait_ge(s("uinc"), i)
                    g.tensor_tensor(vmask[0:n, 0:nb, :],
                                    vtok[0:n, tt:tt + 1, :].to_broadcast([n, nb, P]),
                                    blkmask[0:n, 0:nb].rearrange("p (b x) -> p b x", x=1).to_broadcast([n, nb, P]),
                                    ALU.mult).then_inc(s("vmask"), 1)
                    if tt == 4:
                        pool.wait_ge(s("state"), NBLK * h + NBLK_P)
                        pool.dma_start(o["p_hgrn2"][0, 0, h], srn[:, NBLK_P % SRING, :]).then_inc(s("st_out"), 16)
                        pool.wait_ge(s("o_done"), 5 * h + 4)
                        pool.dma_start(srn[:, (NBLK_P + 1) % SRING, :], a["state_hgrn2"][0, 0, h]).then_inc(s("st_in"), 16)
                        pool.wait_ge(s("state"), NBLK * (h + 1))
                        pool.dma_start(o["s_hgrn2"][0, 0, h], srn[:, (NBLK + 1) % SRING, :]).then_inc(s("st_out"), 16)
            pool.wait_ge(s("st_out"), 32 * HEADS)
            pool.wait_ge(s("xg_zero"), 16 * E)
            pool.wait_ge(s("ycat_lo"), KT)
            ln_gains_pool(pool, "mix0")
            route_pool(pool, 0)
            experts_pool(pool, 0)
            combine_pool(pool, 0)
            s5_pool(pool)
            route_pool(pool, 1)
            experts_pool(pool, 1)
            combine_pool(pool, 1)

        @block.scalar
        def _(act):
            sc_ = nc.scalar
            n_link = [0]

            def link(ins):
                n_link[0] += 1
                ins.then_inc(s("act_chain"), 1)
                act.wait_ge(s("act_chain"), n_link[0])

            def split_hi(c):
                act.wait_ge(s(f"w_landed{c % 2}"), landed[c])
                if c >= 2:
                    act.wait_ge(s("z"), 4 * (c - 1))
                sc_.activation(whi[c % 2][:], raw[c % 2][:], ACT.Copy).then_inc(s("hi_done"), 1)

            act.wait_ge(s("prep"), 1)
            sc_.activation(sp[:, 1, :], sp[:, 0, :], ACT.Exp, scale=-1.0).then_inc(s("prep_a"), 1)
            sc_.activation(lbs[:, 0:2, :], lbs[:, 2:4, :], ACT.Exp).then_inc(s("prep_a"), 1)
            for i, (t0, n) in enumerate(TILES):
                for hf_ in range(2):
                    b = 2 * (i % 2) + hf_
                    act.wait_ge(s("xt"), 2 * i + hf_ + 1)
                    sc_.activation(ft_hi[:, 4 * hf_:4 * hf_ + 4, t0:t0 + n],
                                   ps[:, b, :].rearrange("p (k t) -> p k t", t=P)[:, :, 0:n],
                                   ACT.Copy).then_inc(s("xt_hi"), 1)
                if i < 2:
                    split_hi(i)

            def z_done(ins):
                ins.then_inc(s("z_free"), 1)

            zi = 0
            for jp in range(LRU_TILES // 2):
                c = jp
                for jj in range(2):
                    j = 2 * jp + jj
                    act.wait_ge(s("z"), zi + 1)
                    b = 2 * (zi % 2)
                    if jp:
                        act.wait_ge(s("u_done"), j - 1)
                        act.wait_ge(s(f"conv_out{j % 2}"), 32 * (j // 2))
                    else:
                        act.wait_ge(s("wz"), 6)
                    sc_.activation(zx[jj][:, 3:3 + HALF], ps[:, b, 0:HALF], ACT.Copy)
                    sc_.activation(zx[jj][:, 3 + HALF:3 + T_PROMPT], ps[:, b + 1, 0:T_PROMPT - HALF], ACT.Copy)
                    z_done(sc_.activation(zx[jj][:, S0_AT + 3:S0_AT + 3 + T_SAMPLE],
                                          ps[:, b + 1, T_PROMPT - HALF:HALF], ACT.Copy))
                    zi += 1
                for jj in range(2):
                    j = 2 * jp + jj
                    act.wait_ge(s("z"), zi + 1)
                    b = 2 * (zi % 2)
                    if jp:
                        act.wait_ge(s("lru_y"), j - 1)
                    z_done(sc_.activation(gz[jj][:].rearrange("p (a t) -> p a t", a=2), ps[:, b:b + 2, 0:HALF],
                                          ACT.Gelu_apprx_tanh))
                    zi += 1
                for jj in range(2):
                    j = 2 * jp + jj
                    h2 = LRU_U // 2
                    act.wait_ge(s("params"), 16 * len(param_dmas))
                    act.wait_ge(s("ri"), j + 1)
                    if j:
                        act.wait_ge(s("lru_y"), j)
                        act.wait_ge(s("h_out"), 32 * j)
                    sc_.activation(lr[:].rearrange("p (a t) -> p a t", a=2), ps[:, 4:6, 0:h2], ACT.Sigmoid,
                                   bias=b_r[:, j:j + 1]).then_inc(s("lru_act"), 1)
                    sc_.activation(li[:].rearrange("p (a t) -> p a t", a=2), ps[:, 6:8, 0:h2], ACT.Sigmoid,
                                   bias=b_i[:, j:j + 1]).then_inc(s("lru_act"), 1)
                    act.wait_ge(s("lru_act"), 4 * j + 1)
                    act.wait_ge(s("spl"), 1)
                    sc_.activation(lt[:], lr[:], ACT.Tanh, scale=spl4[:, j:j + 1]).then_inc(s("lru_act"), 1)
                    act.wait_ge(s("lru_act"), 4 * j + 3)
                    sc_.activation(lq[:], lt[:], ACT.Sqrt).then_inc(s("lru_act"), 1)
                    act.wait_ge(s("lru_y"), j + 1)
                    sc_.activation(yt_hi[:, j, :], ld[:, 0:T], ACT.Copy).then_inc(s("ycat_hi"), 1)
                split_hi(c + 2)
            for h in range(HEADS):
                c = 2 + h
                act.wait_ge(s("ycat_lo"), LRU_TILES + h)
                for m, (dst, fn) in enumerate(((hf, ACT.Sigmoid), (hq, ACT.Copy), (hv, ACT.Copy), (hg, ACT.Silu))):
                    act.wait_ge(s("z"), zi + 1)
                    if m == 0 and h == 0:
                        act.wait_ge(s("h_out"), 32 * LRU_TILES)
                        for i in range(2):
                            act.wait_ge(s(f"conv_out{i}"), 16 * LRU_TILES)
                    b = 2 * (zi % 2)
                    sc_.activation(dst[:].rearrange("p (a t) -> p a t", a=2), ps[:, b:b + 2, 0:HALF],
                                   fn).then_inc(s("z_free"), 1)
                    zi += 1
                if h:
                    act.wait_ge(s("vmask"), 5 * h)
                    act.wait_ge(s("o_done"), 5 * h)
                for k, dst in enumerate((vtok, ktok)):
                    act.wait_ge(s("hg_T"), 2 * h + 1 + k)
                    sc_.activation(dst[:, 0:4, :], ps[:, 4, :].rearrange("p (a t) -> p a t", a=4),
                                   ACT.Copy).then_inc(s("hg_tok"), 1)
                    sc_.activation(dst[0:64, 4, :], ps[0:64, 5, 0:P], ACT.Copy).then_inc(s("hg_tok"), 1)
                for tt, (t0, n) in enumerate(HTILES):
                    act.wait_ge(s("o_done"), 5 * h + tt + 1)
                    sc_.activation(ho[:, t0:t0 + n], ps[:, 4, 0:n], ACT.Copy).then_inc(s("ho"), 1)
                act.wait_ge(s("ho"), 5 * (h + 1))
                sc_.activation(hv[:], ho[:], ACT.Square).then_inc(s("hsq"), 1)
                act.wait_ge(s("rms"), h + 1)
                sc_.activation(hr[:].rearrange("p (a t) -> p a t", a=2), ps[:, 6:8, 0:HALF], ACT.Sqrt,
                               bias=eps[:, 0:1], scale=1.0 / P).then_inc(s("hrs"), 1)
                act.wait_ge(s("head_y"), h + 1)
                sc_.activation(yt_hi[:, LRU_TILES + h, :], hp[:], ACT.Copy).then_inc(s("ycat_hi"), 1)
                split_hi(c + 2)
            ln_act(act, "mix0")
            route_act(act, 0)
            experts_act(act, 0)
            ln_act(act, "ffn0")
            s5_act(act)
            route_act(act, 1)
            experts_act(act, 1)
            ln_act(act, "ffn1")

        @block.vector
        def _(dve):
            v = nc.vector
            n_link = [0]

            def link(ins):
                n_link[0] += 1
                ins.then_inc(s("dve_chain"), 1)
                dve.wait_ge(s("dve_chain"), n_link[0])

            def split_lo(c):
                dve.wait_ge(s("hi_done"), c + 1)
                v.tensor_tensor(wlo[c % 2][:], raw[c % 2][:], whi[c % 2][:].bitcast(F32),
                                ALU.subtract).then_inc(s("lo_done"), 1)

            dve.wait_ge(s("params"), 16 * len(param_dmas))
            link(v.tensor_scalar(sp[:, 2, :], lam[:], -1.0, None, ALU.mult))
            link(v.tensor_tensor(sp[:, 0, :], sp[:, 2, :], lam[:], ALU.max))
            link(v.tensor_tensor(lbs[:, 2, :], lbl[:, 0, :], lbl[:, 1, :], ALU.max))
            link(v.tensor_tensor(lbs[:, 3, :], lbl[:, 1, :], lbs[:, 2, :], ALU.subtract))
            link(v.tensor_tensor(lbs[:, 2, :], lbl[:, 0, :], lbs[:, 2, :], ALU.subtract))
            v.tensor_scalar(sp[:, 2, :], sp[:, 2, :], 0.0, None, ALU.max).then_inc(s("prep"), 1)
            dve.wait_ge(s("prep_a"), 2)
            link(v.tensor_scalar(sp[:, 3, :], sp[:, 1, :], 2.0, None, ALU.add))
            link(v.reciprocal(sp[:, 4, :], sp[:, 3, :]))
            link(v.tensor_tensor(sp[:, 3, :], sp[:, 1, :], sp[:, 4, :], ALU.mult))
            link(v.tensor_tensor(sp[:, 4, :], sp[:, 3, :], sp[:, 3, :], ALU.mult))
            link(v.tensor_scalar(sp[:, 1, :], sp[:, 4, :], 1.0 / 15, 1.0 / 13, ALU.mult, ALU.add))
            for q in (11, 9, 7, 5, 3, 1):
                link(v.tensor_tensor(sp[:, 1, :], sp[:, 1, :], sp[:, 4, :], ALU.mult))
                link(v.tensor_scalar(sp[:, 1, :], sp[:, 1, :], 1.0 / q, None, ALU.add))
            link(v.tensor_tensor(sp[:, 1, :], sp[:, 1, :], sp[:, 3, :], ALU.mult))
            link(v.scalar_tensor_tensor(out=sp[:, 1, :], in0=sp[:, 1, :], scalar=2.0, in1=sp[:, 2, :],
                                        op0=ALU.mult, op1=ALU.add))
            v.tensor_scalar(spl4[:], sp[:, 1, :], 4.0, None, ALU.mult).then_inc(s("spl"), 1)
            link(v.tensor_tensor(lbs[:, 2, :], lbs[:, 0, :], lbs[:, 1, :], ALU.add))
            link(v.reciprocal(lbs[:, 3, :], lbs[:, 2, :]))
            link(v.tensor_tensor(lb[:], lbs[:, 0, :], lbs[:, 3, :], ALU.mult))
            link(v.tensor_scalar(omlb[:], lb[:], -1.0, 1.0, ALU.mult, ALU.add))
            link(v.tensor_scalar(nomlb[:], omlb[:], -1.0, None, ALU.mult))
            for i, (t0, n) in enumerate(TILES):
                for hf_ in range(2):
                    b = 2 * (i % 2) + hf_
                    dve.wait_ge(s("xt_hi"), 2 * i + hf_ + 1)
                    ins = v.tensor_tensor(ft_lo[:, 4 * hf_:4 * hf_ + 4, t0:t0 + n],
                                          ps[:, b, :].rearrange("p (k t) -> p k t", t=P)[:, :, 0:n],
                                          ft_hi[:, 4 * hf_:4 * hf_ + 4, t0:t0 + n].bitcast(F32), ALU.subtract)
                ins.then_inc(s("x_split"), 1)
                if i < 2:
                    split_lo(i)

            for j in range(LRU_TILES):
                x = zx[j % 2]
                dve.wait_ge(s("z_free"), 4 * (j // 2) + j % 2 + 1)
                dve.wait_ge(s("wri"), 80 * (j + 1))
                if j:
                    dve.wait_ge(s("ri"), j)
                link(v.tensor_scalar(lu[:], x[:, 0:LRU_U], convw[:, j, 0:1], convb[:, j:j + 1], ALU.mult, ALU.add))
                for k in range(1, CONV):
                    ins = v.scalar_tensor_tensor(out=lu[:], in0=x[:, k:k + LRU_U], scalar=convw[:, j, k:k + 1],
                                                 in1=lu[:], op0=ALU.mult, op1=ALU.add)
                    if k < CONV - 1:
                        link(ins)
                ins.then_inc(s("u_done"), 1)
                dve.wait_ge(s("u_done"), j + 1)
                dve.wait_ge(s("lru_act"), 4 * j + 3)
                if j:
                    dve.wait_ge(s("ycat_hi"), j)
                link(v.tensor_scalar(ld[:], lt[:], 1.0, None, ALU.add))
                link(v.reciprocal(ld[:], ld[:]))
                v.tensor_scalar(la[:], ld[:], 2.0, -1.0, ALU.mult, ALU.add).then_inc(s("la"), 1)
                dve.wait_ge(s("lru_act"), 4 * j + 4)
                link(v.scalar_tensor_tensor(out=lq[:], in0=lq[:], scalar=2.0, in1=ld[:], op0=ALU.mult, op1=ALU.mult))
                dve.wait_ge(s("lru_act"), 4 * j + 2)
                link(v.tensor_tensor(lq[:], lq[:], li[:], ALU.mult))
                link(v.tensor_tensor(lq[:], lq[:], lu[:], ALU.mult))
                dve.wait_ge(s("la"), j + 1)
                v.tensor_tensor_scan(lr[:, 0:T_PROMPT], la[:, 0:T_PROMPT], lq[:, 0:T_PROMPT], 0.0,
                                     ALU.mult, ALU.add).then_inc(s("scan"), 1)
                v.tensor_tensor_scan(lr[:, S0_AT:S0_AT + T_SAMPLE], la[:, S0_AT:S0_AT + T_SAMPLE],
                                     lq[:, S0_AT:S0_AT + T_SAMPLE], h0[:, j:j + 1], ALU.mult, ALU.add).then_inc(s("scan"), 1)
                dve.wait_ge(s("scan"), 2 * (j + 1))
                dve.wait_ge(s("z_free"), 4 * (j // 2) + 3 + j % 2)
                v.tensor_tensor(ld[:, 0:T_PROMPT], lr[:, 0:T_PROMPT], gz[j % 2][:, 0:T_PROMPT], ALU.mult)
                v.tensor_tensor(ld[:, T_PROMPT:T], lr[:, S0_AT:S0_AT + T_SAMPLE], gz[j % 2][:, T_PROMPT:T],
                                ALU.mult).then_inc(s("lru_y"), 1)
                dve.wait_ge(s("ycat_hi"), j + 1)
                v.tensor_tensor(yt_lo[:, j, :], ld[:, 0:T], yt_hi[:, j, :].bitcast(F32),
                                ALU.subtract).then_inc(s("ycat_lo"), 1)
                if j % 2:
                    split_lo(2 + j // 2)
            n_state = 0
            dve.wait_ge(s("ycat_lo"), LRU_TILES)
            blocks = lambda x: x.rearrange("p (b i) -> p b i", i=BLK)
            for h in range(HEADS):
                zbase = 8 + 4 * h
                dve.wait_ge(s("z_free"), zbase + 1)
                v.tensor_scalar(hk[:], hf[:], nomlb[:, h:h + 1], omlb[:, h:h + 1], ALU.mult, ALU.add).then_inc(s("hg_dve"), 1)
                dve.wait_ge(s("hg_dve"), 4 * h + 1)
                link(v.tensor_scalar(hf[:], hf[:], omlb[:, h:h + 1], lb[:, h:h + 1], ALU.mult, ALU.add))
                m0b = m0[:].rearrange("p (x i) -> p x i", x=1).to_broadcast([P, NBLK, BLK])
                link(v.tensor_tensor(blocks(ha[:]), blocks(hf[:]), m0b, ALU.mult))
                link(v.tensor_tensor(hb[:], hf[:], ha[:], ALU.subtract))
                link(v.tensor_tensor_scan(hp[:], ha[:], hb[:], 0.0, ALU.mult, ALU.add))
                link(v.reciprocal(hf[:], hp[:]))
                dve.wait_ge(s("z_free"), zbase + 2)
                v.tensor_tensor(ha[:], hq[:], hp[:], ALU.mult).then_inc(s("hg_dve"), 1)
                v.tensor_tensor(hb[:], hk[:], hf[:], ALU.mult).then_inc(s("hg_dve"), 1)
                dve.wait_ge(s("hg_dve"), 4 * h + 2)
                dve.wait_ge(s("hg_dve"), 4 * h + 3)
                last = blocks(hp[:])[:, :, BLK - 1:BLK].to_broadcast([P, NBLK, BLK])
                v.tensor_tensor(blocks(hq[:]), blocks(hb[:]), last, ALU.mult).then_inc(s("hg_dve"), 1)
                if h:
                    dve.wait_ge(s("st_out"), 32 * h)
                link(v.memset(srn[:, 0, :], 0.0))
                for tt, (t0, n) in enumerate(HTILES):
                    i = 5 * h + tt
                    dve.wait_ge(s("score"), i + 1)
                    if i:
                        dve.wait_ge(s("o_done"), i)
                    v.tensor_tensor(sc[0:n, 0:n], ps[0:n, 5, 0:n], causal[0:n, 0:n], ALU.mult).then_inc(s("scm"), 1)
                    dve.wait_ge(s("uinc"), i + 1)
                    if tt == 4:
                        dve.wait_ge(s("st_in"), 16 * (h + 1))
                    for b in range(n // BLK):
                        g_ = t0 // BLK + b
                        k = g_ + (tt == 4)
                        if n_state:
                            dve.wait_ge(s("state"), n_state)
                        v.scalar_tensor_tensor(out=srn[:, (k + 1) % SRING, :], in0=srn[:, k % SRING, :],
                                               scalar=hp[:, BLK * g_ + BLK - 1:BLK * g_ + BLK],
                                               in1=ps[:, 6 + b // 4, P * (b % 4):P * (b % 4) + P],
                                               op0=ALU.mult, op1=ALU.add).then_inc(s("state"), 1)
                        n_state += 1
                dve.wait_ge(s("hrs"), h + 1)
                link(v.reciprocal(hr[:], hr[:]))
                link(v.scalar_tensor_tensor(out=hp[:], in0=ho[:], scalar=hg_g[:, h:h + 1], in1=hr[:],
                                            op0=ALU.mult, op1=ALU.mult))
                dve.wait_ge(s("z_free"), zbase + 4)
                v.tensor_tensor(hp[:], hp[:], hg[:], ALU.mult).then_inc(s("head_y"), 1)
                dve.wait_ge(s("ycat_hi"), LRU_TILES + h + 1)
                v.tensor_tensor(yt_lo[:, LRU_TILES + h, :], hp[:], yt_hi[:, LRU_TILES + h, :].bitcast(F32),
                                ALU.subtract).then_inc(s("ycat_lo"), 1)
                split_lo(4 + h)
            dve.wait_ge(s("res_landed"), 16 * (NT + 1))
            for i, (t0, n) in enumerate(TILES):
                dve.wait_ge(s("y"), i + 1)
                x = xtok[0:n, i, :]
                b = 2 * (i % 2)
                v.scalar_tensor_tensor(out=x.rearrange("p (a c) -> p a c", a=2),
                                       in0=x.rearrange("p (a c) -> p a c", a=2), scalar=ALPHA,
                                       in1=ps[0:n, b:b + 2, :], op0=ALU.mult, op1=ALU.add).then_inc(s("mix0_sum"), 1)
                dve.wait_ge(s("mix0_sum"), i + 1)
                ln_dve(dve, link, "mix0", i)
            route_dve(dve, link, 0)
            experts_dve(dve, 0)
            combine_dve(dve, link, 0)
            s5_dve(dve, link, split_lo)
            route_dve(dve, link, 1)
            experts_dve(dve, 1)
            combine_dve(dve, link, 1)

        @block.tensor
        def _(pe):
            te = nc.tensor
            pe.wait_ge(s("pc"), 36)
            for i, (t0, n) in enumerate(TILES):
                pe.wait_ge(s(f"x_landed{i % 2}"), 16 * (i // 2 + 1) + (16 if i == 4 else 0))
                if i >= 2:
                    pe.wait_ge(s("x_split"), i - 1)
                for k in range(KT):
                    b = 2 * (i % 2) + k // 4
                    ins = te.transpose(ps[:, b, P * (k % 4):P * (k % 4) + n], xin[i % 2][0:n, P * k:P * k + P],
                                       ident[0:n, 0:n])
                    if k % 4 == 3:
                        ins.then_inc(s("xt"), 1)

            def mm3(out, l_hi, l_lo, r_hi, r_lo, first, last):
                te.matmul(out, l_lo, r_hi, start=first, stop=False)
                te.matmul(out, l_hi, r_lo, start=False, stop=False)
                return te.matmul(out, l_hi, r_hi, start=False, stop=last)

            zi = 0

            def z_tile(c, m):
                nonlocal zi
                if m == 0:
                    pe.wait_ge(s("lo_done"), c + 1)
                if c == 0 and m == 0:
                    pe.wait_ge(s("x_split"), NT)
                if zi >= 2:
                    pe.wait_ge(s("z_free"), zi - 1)
                whc = whi[c % 2][:].rearrange("p (k n) -> p k n", n=512)
                wlc = wlo[c % 2][:].rearrange("p (k n) -> p k n", n=512)
                for half in range(2):
                    for k in range(KT):
                        cols = slice(P * m, P * m + P)
                        tk = slice(HALF * half, HALF * half + HALF)
                        ins = mm3(ps[:, 2 * (zi % 2) + half, 0:HALF], whc[:, k, cols], wlc[:, k, cols],
                                  ft_hi[:, k, tk], ft_lo[:, k, tk], k == 0, k == KT - 1)
                ins.then_inc(s("z"), 1)
                zi += 1

            for jp in range(LRU_TILES // 2):
                for m in range(4):
                    z_tile(jp, m)
                for jj in range(2):
                    j = 2 * jp + jj
                    pe.wait_ge(s("wri"), 80 * (j + 1))
                    pe.wait_ge(s("u_done"), j + 1)
                    if j:
                        pe.wait_ge(s("lru_act"), 4 * j - 4 + 2)
                    h2 = LRU_U // 2
                    for w, b in ((wr, 4), (wi, 6)):
                        for half in range(2):
                            ins = te.matmul(ps[:, b + half, 0:h2], w[:], lu[:, h2 * half:h2 * half + h2],
                                            start=True, stop=True)
                    ins.then_inc(s("ri"), 1)
            for h in range(HEADS):
                for m in range(4):
                    z_tile(2 + h, m)
                if h == 0:
                    pe.wait_ge(s("lru_act"), 4 * LRU_TILES - 4 + 2)
                else:
                    pe.wait_ge(s("ho"), 5 * h)
                    pe.wait_ge(s("hrs"), h)
                    pe.wait_ge(s("scm"), 5 * h)
                pe.wait_ge(s("z_free"), 8 + 4 * h + 3)
                for src, nm in ((hv, "vT"), (hq, "kT")):
                    if nm == "kT":
                        pe.wait_ge(s("hg_dve"), 4 * h + 4)
                        pe.wait_ge(s("hg_tok"), 4 * h + 2)
                    for tt, (t0, n) in enumerate(HTILES):
                        out = ps[0:n, 4, P * tt:P * tt + P] if tt < 4 else ps[0:n, 5, 0:P]
                        ins = te.transpose(out, src[:, t0:t0 + n], ident[:])
                    ins.then_inc(s("hg_T"), 1)
                pe.wait_ge(s("hg_tok"), 4 * h + 4)
                for tt, (t0, n) in enumerate(HTILES):
                    i = 5 * h + tt
                    if i:
                        pe.wait_ge(s("scm"), i)
                    te.matmul(ps[0:n, 5, 0:n], hb[:, t0:t0 + n], ha[:, t0:t0 + n], start=True,
                              stop=True).then_inc(s("score"), 1)
                    pe.wait_ge(s("vmask"), i + 1)
                    if i:
                        pe.wait_ge(s("state"), (NBLK * h + 8 * tt) if tt else NBLK * h)
                    for u in range(n // 64 if n < P else 2):
                        if n < P and u:
                            break
                        ins = te.matmul(ps[:, 6 + u, :], ktok[0:n, tt, :],
                                        vmask[0:n, 4 * u:4 * u + 4, :].rearrange("p b d -> p (b d)"),
                                        start=True, stop=True)
                    ins.then_inc(s("uinc"), 1)
                    pe.wait_ge(s("scm"), i + 1)
                    if tt:
                        pe.wait_ge(s("ho"), i)
                    te.matmul(ps[:, 4, 0:n], vtok[0:n, tt, :], sc[0:n, 0:n], start=True, stop=False)
                    if tt == 4:
                        pe.wait_ge(s("st_in"), 16 * (h + 1))
                    nb = n // BLK
                    for b in range(nb):
                        g_ = t0 // BLK + b
                        k = g_ + (tt == 4)
                        if b:
                            pe.wait_ge(s("state"), NBLK * h + g_)
                        elif tt < 4 and tt:
                            pe.wait_ge(s("state"), NBLK * h + g_)
                        ins = te.matmul(ps[:, 4, BLK * b:BLK * b + BLK], srn[:, k % SRING, :],
                                        ha[:, BLK * g_:BLK * g_ + BLK], start=False, stop=(b == nb - 1))
                    ins.then_inc(s("o_done"), 1)
                pe.wait_ge(s("hsq"), h + 1)
                pe.wait_ge(s("state"), NBLK * (h + 1))
                for half in range(2):
                    ins = te.matmul(ps[:, 6 + half, 0:HALF], ones[:], hv[:, HALF * half:HALF * half + HALF],
                                    start=True, stop=True)
                ins.then_inc(s("rms"), 1)
            pe.wait_ge(s("ycat_lo"), KT)
            pe.wait_ge(s("lo_done"), 8)
            pe.wait_ge(s("z_free"), 24)
            for i, (t0, n) in enumerate(TILES):
                if i >= 2:
                    pe.wait_ge(s("mix0_sum"), i - 1)
                for half in range(2):
                    wh = whi[half][:].rearrange("p (k n) -> p k n", n=512)
                    wl = wlo[half][:].rearrange("p (k n) -> p k n", n=512)
                    for k in range(KT):
                        ins = mm3(ps[0:n, 2 * (i % 2) + half, :], yt_hi[:, k, t0:t0 + n], yt_lo[:, k, t0:t0 + n],
                                  wh[:, k, :], wl[:, k, :], k == 0, k == KT - 1)
                ins.then_inc(s("y"), 1)
            route_pe(pe, 0)
            experts_pe(pe, mm3, 0)
            s5_pe(pe, mm3)
            route_pe(pe, 1)
            experts_pe(pe, mm3, 1)


_OUTS = {
    "y_prompt": (1, 512, 1024), "y_sample": (1, 64, 1024),
    "p_lru_h": (1, 1, 512), "p_lru_conv": (1, 1, 3, 512), "p_hgrn2": (1, 1, 4, 128, 128),
    "p_s5_re": (1, 1, 64, 64), "p_s5_im": (1, 1, 64, 64),
    "s_lru_h": (1, 1, 512), "s_lru_conv": (1, 1, 3, 512), "s_hgrn2": (1, 1, 4, 128, 128),
    "s_s5_re": (1, 1, 64, 64), "s_s5_im": (1, 1, 64, 64),
}


def kernel(**inputs):
    import numpy as _np
    import concourse.bacc as _bacc
    from concourse.bass_utils import run_bass_kernel_spmd as _run

    nc = _bacc.Bacc("TRN2", target_bir_lowering=False, num_devices=1)
    arrays, ins, outs = {}, {}, {}
    for name, value in inputs.items():
        value = _np.ascontiguousarray(value)
        arrays[f"in_{name}"] = value
        ins[name] = nc.dram_tensor(f"in_{name}", value.shape, mybir.dt.from_np(value.dtype), kind="ExternalInput").ap()
    for name, shape in _OUTS.items():
        outs[name] = nc.dram_tensor(f"out_{name}", shape, F32, kind="ExternalOutput").ap()
    stream_kernel(nc, ins, outs)
    r = _run(nc, [arrays], core_ids=[0])
    return tuple(r.results[0][f"out_{name}"] for name in _OUTS)
```

```python
import concourse.bass as bass
from concourse import mybir
from contextlib import ExitStack

F32 = mybir.dt.float32
F32R = mybir.dt.float32r
I32 = mybir.dt.int32
U32 = mybir.dt.uint32
ALU = mybir.AluOpType
ACT = mybir.ActivationFunctionType
AX_X = mybir.AxisListType.X

P = 128
D = 1024
KT = D // P
T_PROMPT, T_SAMPLE = 512, 64
T = T_PROMPT + T_SAMPLE
TT = 120
TILES = [(t, min(TT, T - t)) for t in range(0, T, TT)]
NT = len(TILES)
HALF = T // 2
LRU = 512
LRU_TILES = LRU // P
CONV = 4
LRU_W = T + 2 * (CONV - 1) + 1
LRU_U = LRU_W - (CONV - 1)
S0_AT = T_PROMPT + CONV - 1
HEADS = 4
BLK = 16
NBLK_P, NBLK_S = T_PROMPT // BLK, T_SAMPLE // BLK
NBLK = NBLK_P + NBLK_S
SRING = 9
HTILES = [(t, min(P, T - t)) for t in range(0, T, P)]
ALPHA = 4.0 ** 0.25
LN_EPS = 1e-5
RMS_EPS = 1e-6
E = 16
GROUPS, PER_GROUP = 4, 4
F_EXP = 512
CAP = 128
ROUNDS_MAX = -(-T // CAP)
SLOTS = E * CAP
DUMP = SLOTS

CHUNK = 4096
SB0 = 16512
RAW_AT = [SB0, SB0 + 16384]
SPL_AT = [SB0 + 32768, SB0 + 65536]
FT_AT = SB0 + 98304
YT_AT = FT_AT + 2 * KT * T * 4
XTOK_AT = YT_AT + 2 * KT * T * 4
TEMP_AT = XTOK_AT + NT * D * 4
SB_END = 229344


def stream_kernel(nc, a, o):
    with ExitStack() as ctx:
        taken = [TEMP_AT]

        def at(name, shape, offset, dt=F32):
            return nc.alloc_sbuf_tensor_at(name, shape, dt, offset=offset)

        def small(name, cols, dt=F32, parts=P):
            t = at(name, [parts] + (cols if isinstance(cols, list) else [cols]), taken[0], dt)
            n = 4
            for c in (cols if isinstance(cols, list) else [cols]):
                n *= c
            taken[0] += -(-n // 32) * 32
            assert taken[0] <= SB_END, name
            return t

        def sem(name):
            return ctx.enter_context(nc.semaphore(name))

        ps = ctx.enter_context(nc.psum_tensor("ps", [P, 8, 512], F32))

        raw = [at(f"raw{i}", [P, CHUNK], RAW_AT[i]) for i in range(2)]
        whi = [at(f"whi{i}", [P, CHUNK], SPL_AT[i], F32R) for i in range(2)]
        wlo = [at(f"wlo{i}", [P, CHUNK], SPL_AT[i] + 4 * CHUNK, F32R) for i in range(2)]
        ft_hi = at("ft_hi", [P, KT, T], FT_AT, F32R)
        ft_lo = at("ft_lo", [P, KT, T], FT_AT + 4 * KT * T, F32R)
        yt_hi = at("yt_hi", [P, KT, T], YT_AT, F32R)
        yt_lo = at("yt_lo", [P, KT, T], YT_AT + 4 * KT * T, F32R)
        xtok = at("xtok", [P, NT, D], XTOK_AT)

        ident = small("ident", P)
        ones = small("ones", P)
        lstrict = small("lstrict", P)
        wt4 = small("wt4", PER_GROUP)
        e128 = small("e128", E)
        eps = small("eps", 2)
        lnst = small("lnst", [2, 2, 6])
        lnmv = small("lnmv", [2, 4])
        gate = small("gate", [2, NT])
        slot = small("slot", [2, NT], U32)
        nstep = small("nstep", 1, I32)
        shared_end = taken[0]
        causal = small("causal", P)
        blkmask = small("blkmask", 8)
        m0 = small("m0", BLK)
        convw = small("convw", [LRU_TILES, CONV])
        convb = small("convb", LRU_TILES)
        b_r = small("b_r", LRU_TILES)
        b_i = small("b_i", LRU_TILES)
        lam = small("lam", LRU_TILES)
        h0 = small("h0", LRU_TILES)
        spl4 = small("spl4", LRU_TILES)
        sp = small("sp", [6, LRU_TILES])
        lbl = small("lbl", [2, HEADS])
        lbs = small("lbs", [4, HEADS])
        lb = small("lb", HEADS)
        omlb = small("omlb", HEADS)
        nomlb = small("nomlb", HEADS)
        hg_g = small("hg_g", HEADS)
        past = small("past", [CONV - 1, LRU_TILES])
        convst = small("convst", [2, CONV - 1, LRU_TILES])
        hst = small("hst", [2, LRU_TILES])
        consts_end = taken[0]

        l0_at = [consts_end]
        l0b_at = [XTOK_AT]

        def l0(name, cols, low=False):
            cols = cols if isinstance(cols, list) else [cols]
            n = 4
            for c in cols:
                n *= c
            n = -(-n // 32) * 32
            where = l0b_at if low else l0_at
            t = at(name, [P] + cols, where[0])
            where[0] += n
            assert where[0] <= (TEMP_AT if low else SB_END), name
            return t

        zx = [l0(f"zx{i}", LRU_W, True) for i in range(2)]
        gz = [l0(f"gz{i}", T, True) for i in range(2)]
        lr = l0("lr", LRU_U, True)
        li = l0("li", LRU_U, True)
        lt = l0("lt", LRU_U, True)
        ld = l0("ld", LRU_U, True)
        lu = [l0(f"lu{i}", LRU_U) for i in range(2)]
        la = l0("la", LRU_U)
        lq = l0("lq", LRU_U)
        l0_at_lru_end = l0_at[0]
        xin = [at(f"xin{i}", [P, D], YT_AT + 4 * D * i) for i in range(NT)]
        SLOT = 4 * T
        gate_w_at = YT_AT + 4 * KT * T + 4 * SLOT
        wr = at("wr", [P, LRU_TILES, P], gate_w_at)
        wi = at("wi", [P, LRU_TILES, P], gate_w_at + 4 * LRU_TILES * P)
        assert 8 * LRU_TILES * P <= 2 * SLOT
        l0_at[0], l0b_at[0] = consts_end, XTOK_AT
        in_yt = [YT_AT + (KT - 2) * SLOT, YT_AT + (2 * KT - 2) * SLOT, YT_AT + (KT - 1) * SLOT, YT_AT + (2 * KT - 1) * SLOT]
        hf, hq, hv, hg = ([at(f"{nm}0", [P, T], in_yt[i]), l0(f"{nm}1", T, True)]
                          for i, nm in enumerate(("hf", "hq", "hv", "hg")))
        hk = l0("hk", T, True)
        ha = l0("ha", T, True)
        hb = l0("hb", T, True)
        hp = l0("hp", T, True)
        vtok = l0("vtok", [5, P])
        ktok = l0("ktok", [5, P])
        srn = l0("srn", [SRING, P])
        vmask = l0("vmask", [8, P])
        sc = l0("sc", P)
        s_in = l0("s_in", P)
        ho = hq
        hr = hf
        zeros = at("zeros", [P, D], SB_END - 4 * D)
        assert l0_at_lru_end <= SB_END - 4 * D

        taken[0] = shared_end
        lng = small("lng", D)
        lnb = small("lnb", D)
        x1t = small("x1t", [KT, TT])
        rw = small("rw", [KT, E])
        rb = small("rb", E)
        R = {n: small("r_" + n, [NT, E]) for n in ("l", "p", "m1", "m2", "w", "x", "s1")}
        Rg = {n: small("rg_" + n, [NT, GROUPS]) for n in ("a", "b", "c", "d", "e")}
        Rt = {n: small("rt_" + n, NT) for n in ("mx", "z", "p1", "p2")}
        nrow = small("nrow", 4)

        taken[0] = shared_end
        xe = small("xe", D)
        xet_hi = small("xet_hi", [KT, P], F32R)
        xet_lo = small("xet_lo", [KT, P], F32R)
        hx = at("hx", [P, F_EXP], YT_AT + 8 * CHUNK)
        ht_hi = small("ht_hi", [4, P], F32R)
        ht_lo = small("ht_lo", [4, P], F32R)
        raw.append(at("raw2", [P, CHUNK], YT_AT))
        whi.append(at("whi2", [P, CHUNK], FT_AT, F32R))
        wlo.append(at("wlo2", [P, CHUNK], FT_AT + 4 * CHUNK, F32R))
        ysb = at("ysb", [P, D], FT_AT + 8 * CHUNK)
        ygat = [[at(f"ygat{i}{k}", [P, D], YT_AT + 4 * CHUNK + 4 * D * (2 * i + k)) for k in range(2)] for i in range(2)]

        xg = nc.dram_tensor("xg", (ROUNDS_MAX * SLOTS, D), F32, kind="Internal").ap()
        yg = nc.dram_tensor("yg", (ROUNDS_MAX * SLOTS, D), F32, kind="Internal").ap()

        S = {}

        def s(name):
            if name not in S:
                S[name] = sem(name)
            return S[name]

        w_in = a["w_in_ab"][0].rearrange("(k p) n -> p k n", p=P)
        w_out = a["w_out_ab"][0].rearrange("(k p) n -> p k n", p=P)

        chunks0 = []
        for jp in range(LRU_TILES // 2):
            chunks0.append([(w_in[:, :, LRU + 256 * jp:LRU + 256 * jp + 256], 0, 256),
                            (w_in[:, :, 256 * jp:256 * jp + 256], 256, 256)])
        Q_AT, F_AT, V_AT, G_AT = (2 * LRU + 512 * i for i in range(4))
        for h in range(HEADS):
            chunks0.append([(w_in[:, :, b + P * h:b + P * h + P], P * i, P)
                            for i, b in enumerate((F_AT, Q_AT, V_AT, G_AT))])
        for n in range(2):
            chunks0.append([(w_out[:, :, 512 * n:512 * n + 512], 0, 512)])
        n_in = 6
        landed = {}
        count = [0, 0]
        for c, pieces in enumerate(chunks0):
            count[c % 2] += 16 * len(pieces)
            landed[c] = count[c % 2]
        param_dmas = [
            *[(convw[:, :, k], a["lru_conv_w"][0, k].rearrange("(j p) -> p j", p=P)) for k in range(CONV)],
            (convb[:], a["lru_conv_b"][0].rearrange("(j p) -> p j", p=P)),
            (b_r[:], a["lru_b_r"][0].rearrange("(j p) -> p j", p=P)),
            (b_i[:], a["lru_b_i"][0].rearrange("(j p) -> p j", p=P)),
            (lam[:], a["lru_lam"][0].rearrange("(j p) -> p j", p=P)),
            (h0[:], a["state_lru_h"][0, 0].rearrange("(j p) -> p j", p=P)),
            *[(lbl[:, r], a["hgrn_lb_logits"][r].rearrange("(j p) -> p j", p=P)) for r in range(2)],
            (hg_g[:], a["hgrn_norm_g"][0].rearrange("(j p) -> p j", p=P)),
            *[(past[:, k], a["state_lru_conv"][0, 0, k].rearrange("(j p) -> p j", p=P)) for k in range(CONV - 1)],
        ]

        def x_rows(t0, n):
            xp, xs = a["x_prompt"][0], a["x_sample"][0]
            if t0 + n <= T_PROMPT:
                return [(0, n, xp[t0:t0 + n])]
            m = T_PROMPT - t0
            return [(0, m, xp[t0:T_PROMPT]), (m, n - m, xs[0:n - m])]

        x_group = [0, 1, 1, 2, 2]
        x_loads = [16, 32, 16 * 3]

        ln_no = {"mix0": 0, "ffn0": 1, "mix1": 2, "ffn1": 3}

        def ln_gains_pool(pool, tag):
            ln, l = tag[:3], int(tag[3])
            for dst, src in ((lng, a[f"ln_{ln}_g"]), (lnb, a[f"ln_{ln}_b"])):
                pool.dma_start(dst[:], src[l:l + 1, :].to_broadcast([P, D])).then_inc(s("ln_gains"), 16)

        def ln_act(act, tag, tiles=range(NT)):
            for i in tiles:
                n = TILES[i][1]
                act.wait_ge(s("ln_mv"), NT * ln_no[tag] + i + 1)
                nc.scalar.activation(lnmv[0:n, i % 2, 2:3], lnmv[0:n, i % 2, 1:2], ACT.Sqrt,
                                     bias=eps[0:n, 1:2]).then_inc(s("ln_sd"), 1)

        def ln_dve(dve, link, tag, i):
            v, n = nc.vector, TILES[i][1]
            x, st, mv = xtok[0:n, i, :], lnst[0:n, i % 2], lnmv[0:n, i % 2]
            v.bn_stats(st[:, 0, :], x[:, 0:512])
            link(v.bn_stats(st[:, 1, :], x[:, 512:D]))
            v.bn_aggr(mv[:, 0:2], st).then_inc(s("ln_mv"), 1)
            dve.wait_ge(s("ln_sd"), NT * ln_no[tag] + i + 1)
            link(v.reciprocal(mv[:, 3:4], mv[:, 2:3]))
            link(v.tensor_scalar(x, x, mv[:, 0:1], mv[:, 3:4], ALU.subtract, ALU.mult))
            dve.wait_ge(s("ln_gains"), 32 * ln_no[tag] + 32)
            link(v.tensor_tensor(x, x, lng[0:n, :], ALU.mult))
            v.tensor_tensor(x, x, lnb[0:n, :], ALU.add).then_inc(s("ln_x"), 1)

        def route_pool(pool, l):
            L = f"_{l}"
            pool.dma_start(rw[:], a["router_w"].rearrange("(k p) e -> p k e", p=P)).then_inc(s("rw"), 16)
            pool.dma_start(rb[:], a["router_b"].rearrange("(x e) -> x e", x=1).to_broadcast([P, E])
                           ).then_inc(s("rw"), 16)
            pool.wait_ge(s("routed"), 1 * l + 1)
            steps = pool.value_load(nstep[0:1, 0:1], min_val=E, max_val=E * ROUNDS_MAX)
            with pool.If(steps > E):
                nc.gpsimd.memset(ysb[:], 0.0).then_inc(s("rest_zero" + L), 1)
                pool.wait_ge(s("rest_zero" + L), 1)
                with pool.Fori(1, ROUNDS_MAX) as rr:
                    for q in range(E):
                        for buf in (xg, yg):
                            pool.dma_start(buf[bass.ds(rr * SLOTS + CAP * q, CAP)], ysb[:]).then_inc(s("xg_rest" + L), 16)
                pool.wait_ge(s("xg_rest" + L), 32 * E * (ROUNDS_MAX - 1))
            for i, (t0, n) in enumerate(TILES):
                for k in range(2):
                    pool.indirect_dma_start(out=xg, out_offset=bass.IndirectOffsetOnAxis(ap=slot[0:n, k, i:i + 1], axis=0),
                                            in_=xtok[0:n, i, :], in_offset=None).then_inc(s("sent"), 16)
            pool.wait_ge(s("sent"), 32 * NT * l + 32 * NT)

        def route_act(act, l):
            L = f"_{l}"
            for i, (t0, n) in enumerate(TILES):
                act.wait_ge(s("x1T"), NT * l + i + 1)
                if i:
                    act.wait_ge(s("logit"), NT * l + i)
                nc.scalar.activation(x1t[:, :, 0:n].rearrange("p (a k) t -> p a k t", a=2),
                                     ps[:, 4:6, :].rearrange("p a (k t) -> p a k t", t=P)[:, :, :, 0:n],
                                     ACT.Copy).then_inc(s("x1t"), 1)
            act.wait_ge(s("r_shift"), 1 * l + 1)
            nc.scalar.activation(R["p"][0:TT], R["w"][0:TT], ACT.Exp).then_inc(s("r_exp"), 1)

        def route_pe(pe, l):
            L, te = f"_{l}", nc.tensor
            pe.wait_ge(s("rw"), 32 * l + 32)
            for i, (t0, n) in enumerate(TILES):
                pe.wait_ge(s("ln_x"), NT * (2 * l) + i + 1)
                if i:
                    pe.wait_ge(s("x1t"), NT * l + i)
                for k in range(KT):
                    ins = te.transpose(ps[:, 4 + k // 4, P * (k % 4):P * (k % 4) + n], xtok[0:n, i, P * k:P * k + P],
                                       ident[0:n, 0:n])
                ins.then_inc(s("x1T"), 1)
                pe.wait_ge(s("x1t"), NT * l + i + 1)
                for k in range(KT):
                    ins = te.matmul(ps[0:n, 6, E * i:E * i + E], x1t[:, k, 0:n], rw[:, k, :],
                                    start=(k == 0), stop=(k == KT - 1))
                ins.then_inc(s("logit"), 1)
            pe.wait_ge(s("chosen"), 1 * l + 1)
            m = R["x"]
            for i, (t0, n) in enumerate(TILES):
                for q in range(i + 1):
                    nq = TILES[q][1]
                    te.matmul(ps[0:n, 7, E * i:E * i + E], (lstrict if q == i else ones)[0:nq, 0:n], m[0:nq, q, :],
                              start=(q == 0), stop=(q == i))
            for q in range(NT):
                nq = TILES[q][1]
                ins = te.matmul(ps[:, 7, E * NT:E * NT + E], ones[0:nq, :], m[0:nq, q, :],
                                start=(q == 0), stop=(q == NT - 1))
            ins.then_inc(s("ranked"), 1)

        def route_dve(dve, link, l):
            L, v = f"_{l}", nc.vector
            n = TT
            lg, pr, m1, m2, w, x, s1 = (R[q][0:n] for q in ("l", "p", "m1", "m2", "w", "x", "s1"))
            ga, gb, gc, gd, ge = (Rg[q][0:n] for q in ("a", "b", "c", "d", "e"))
            mx, z, p1, p2 = (Rt[q][0:n] for q in ("mx", "z", "p1", "p2"))
            col = lambda q: q.rearrange("p (i x) -> p i x", x=1)
            grp = lambda q: q.rearrange("p i (g j) -> p (i g) j", j=PER_GROUP)
            flat_g = lambda q: q.rearrange("p i g -> p (i g)")
            over16 = lambda q: col(q).to_broadcast([n, NT, E])
            over4 = lambda q: col(q).to_broadcast([n, NT, GROUPS])
            wide = lambda q: flat_g(q).rearrange("p (i x) -> p i x", x=1).to_broadcast([n, NT * GROUPS, PER_GROUP])
            tt, rdc = v.tensor_tensor, v.tensor_reduce
            link(v.memset(R["l"][:], 0.0))
            dve.wait_ge(s("rw"), 32 * l + 32)
            dve.wait_ge(s("logit"), NT * l + NT)
            nl = TILES[-1][1]
            tt(R["l"][0:n, 0:NT - 1, :], ps[0:n, 6, 0:E * (NT - 1)].rearrange("p (i e) -> p i e", e=E),
               rb[0:n, :].rearrange("p (x e) -> p x e", x=1).to_broadcast([n, NT - 1, E]), ALU.add)
            link(tt(R["l"][0:nl, NT - 1, :], ps[0:nl, 6, E * (NT - 1):E * NT], rb[0:nl, :], ALU.add))
            link(rdc(mx, lg, AX_X, ALU.max))
            tt(w, lg, over16(mx), ALU.subtract).then_inc(s("r_shift"), 1)
            dve.wait_ge(s("r_exp"), 1 * l + 1)
            link(rdc(z, pr, AX_X, ALU.add))
            link(v.reciprocal(z, z))
            link(tt(pr, pr, over16(z), ALU.mult))
            g4 = grp(pr)
            c4 = [g4[:, :, q] for q in range(4)]
            f = flat_g
            tt(f(ga), c4[0], c4[1], ALU.max)
            tt(f(gb), c4[0], c4[1], ALU.min)
            tt(f(gc), c4[2], c4[3], ALU.max)
            link(tt(f(gd), c4[2], c4[3], ALU.min))
            tt(f(ge), f(ga), f(gc), ALU.max)
            link(tt(f(gb), f(gb), f(gd), ALU.max))
            link(tt(f(gd), f(ga), f(gc), ALU.min))
            link(tt(f(gb), f(gb), f(gd), ALU.max))
            link(tt(f(ga), f(ge), f(gb), ALU.add))
            wt_g = wt4[0:n, :].rearrange("p (x g) -> p x g", x=1).to_broadcast([n, NT, GROUPS])
            wt_j = wt4[0:n, :].rearrange("p (x g) -> p x g", x=1).to_broadcast([n, NT * GROUPS, PER_GROUP])
            link(rdc(mx, ga, AX_X, ALU.max))
            link(tt(gb, ga, over4(mx), ALU.is_equal))
            link(tt(gb, gb, wt_g, ALU.mult))
            link(rdc(mx, gb, AX_X, ALU.max))
            link(tt(ge, gb, over4(mx), ALU.is_equal))
            cur = lg
            for dst in (m1, m2):
                link(rdc(f(ga), grp(cur), AX_X, ALU.max))
                link(tt(grp(w), grp(cur), wide(ga), ALU.is_equal))
                link(tt(grp(w), grp(w), wt_j, ALU.mult))
                link(rdc(f(gb), grp(w), AX_X, ALU.max))
                link(tt(grp(dst), grp(w), wide(gb), ALU.is_equal))
                if dst is m1:
                    link(v.scalar_tensor_tensor(out=s1, in0=dst, scalar=-3.0e38, in1=lg, op0=ALU.mult, op1=ALU.add))
                    cur = s1
            link(tt(grp(m1), grp(m1), wide(ge), ALU.mult))
            link(tt(grp(m2), grp(m2), wide(ge), ALU.mult))
            tt(x, m1, m2, ALU.add).then_inc(s("chosen"), 1)
            for m, p in ((m1, p1), (m2, p2)):
                link(tt(w, pr, m, ALU.mult))
                link(rdc(p, w, AX_X, ALU.add))
            link(tt(z, p1, p2, ALU.add))
            link(v.reciprocal(z, z))
            tt(gate[0:n, 0, :], p1, z, ALU.mult)
            link(tt(gate[0:n, 1, :], p2, z, ALU.mult))
            dve.wait_ge(s("ranked"), 1 * l + 1)
            nl = TILES[-1][1]
            link(v.memset(R["l"][:], 0.0))
            v.tensor_copy(R["l"][0:n, 0:NT - 1, :], ps[0:n, 7, 0:E * (NT - 1)].rearrange("p (i e) -> p i e", e=E))
            link(v.tensor_copy(R["l"][0:nl, NT - 1, :], ps[0:nl, 7, E * (NT - 1):E * NT]))
            link(v.tensor_scalar(w, lg, float(CAP), None, ALU.is_ge))
            for q in range(2, ROUNDS_MAX):
                link(v.scalar_tensor_tensor(out=w, in0=lg, scalar=float(CAP * q), in1=w, op0=ALU.is_ge, op1=ALU.add))
            link(v.scalar_tensor_tensor(out=w, in0=w, scalar=float(SLOTS - CAP), in1=lg, op0=ALU.mult, op1=ALU.add))
            link(tt(w, w, e128[0:n, :].rearrange("p (x e) -> p x e", x=1).to_broadcast([n, NT, E]), ALU.add))
            for k, (m, p) in enumerate(((m1, p1), (m2, p2))):
                link(tt(m, w, m, ALU.mult))
                link(rdc(p, m, AX_X, ALU.add))
                link(v.tensor_copy(slot[0:n, k, :], p))
            link(rdc(nrow[0:1, 0:1], ps[0:1, 7, E * NT:E * NT + E], AX_X, ALU.max))
            link(v.tensor_scalar(nrow[0:1, 1:2], nrow[0:1, 0:1], float(CAP), 1.0, ALU.is_gt, ALU.add))
            for q in range(2, ROUNDS_MAX):
                link(v.scalar_tensor_tensor(out=nrow[0:1, 1:2], in0=nrow[0:1, 0:1], scalar=float(CAP * q),
                                            in1=nrow[0:1, 1:2], op0=ALU.is_gt, op1=ALU.add))
            v.tensor_scalar(nstep[0:1, 0:1], nrow[0:1, 1:2], float(E), None, ALU.mult).then_inc(s("routed"), 1)

        mixed = ((s("y"), NT), (s("y"), 3 * NT))

        def step_count(eng, l):
            eng.wait_ge(s("routed"), l + 1)
            return eng.value_load(nstep[0:1, 0:1], min_val=E, max_val=E * ROUNDS_MAX)

        def experts_sp(sp_, l):
            L = f"_{l}"
            w3 = [a["moe_w_gate"][l].rearrange("e (k p) n -> p e k n", p=P),
                  a["moe_w_up"][l].rearrange("e (k p) n -> p e k n", p=P),
                  a["moe_w_down"][l].rearrange("e (k p) n -> p e k n", p=P)]

            def load(q, e, it):
                if isinstance(it, int) and it == 0:
                    if q < 2:
                        sp_.wait_ge(s("lo_done"), (7, 13)[l] + q)
                    else:
                        sp_.wait_ge(*mixed[l])
                else:
                    sp_.wait_ge(s(f"lo{q}" + L), it)
                src = w3[q][:, e:e + 1] if isinstance(e, int) else w3[q][:, bass.ds(e, 1)]
                src = src.rearrange("p e k n -> p (e k) n")
                sp_.dma_start(raw[q][:].rearrange("p (k n) -> p k n", k=src.shape[1]), src
                              ).then_inc(s(f"ld{q}" + L), 16)

            for q in range(3):
                load(q, 0, 0)
            load(0, 1, 1)
            load(1, 1, 1)
            with sp_.Fori(1, E - 1) as e:
                load(0, e + 1, e + 1)
                load(1, e + 1, e + 1)
                load(2, e, e)
            load(2, E - 1, E - 1)
            steps = step_count(sp_, l)
            with sp_.If(steps > E):
                with sp_.Fori(E, steps) as it:
                    for q in range(3):
                        load(q, it % E, it)

        def experts_pool(pool, l):
            L = f"_{l}"

            def load_x(it):
                if not (isinstance(it, int) and it == 0):
                    pool.wait_ge(s("p_xt" + L), it)
                rows = xg[bass.ds(it * CAP, CAP)] if not isinstance(it, int) else xg[it * CAP:it * CAP + CAP]
                pool.dma_start(xe[:], rows).then_inc(s("xe" + L), 16)

            def store_y(it):
                pool.wait_ge(s("y_ev" + L), it + 1)
                rows = yg[bass.ds((it + 1) * CAP - CAP, CAP)] if not isinstance(it, int) else yg[it * CAP:it * CAP + CAP]
                pool.dma_start(rows, ysb[:]).then_inc(s("y_st" + L), 16)

            load_x(0)
            load_x(1)
            load_x(2)
            with pool.Fori(2, E - 1) as it:
                load_x(it + 1)
                store_y(it - 2)
            for it in range(E - 3, E):
                store_y(it)
            steps = step_count(pool, l)
            with pool.If(steps > E):
                with pool.Fori(E, steps) as it:
                    load_x(it)
                    store_y(it)
                    pool.wait_ge(s("y_st" + L), it * 16 + 16)

        def experts_act(act, l):
            L, sa = f"_{l}", nc.scalar

            def hi(q, it, done):
                act.wait_ge(s(f"ld{q}" + L), it * 16 + 16)
                if not (isinstance(it, int) and it == 0):
                    act.wait_ge(s(done + L), it)
                sa.activation(whi[q][:], raw[q][:], ACT.Copy).then_inc(s(f"hi{q}" + L), 1)

            def xt_hi(it):
                act.wait_ge(s("p_xt" + L), it + 1)
                if not (isinstance(it, int) and it == 0):
                    act.wait_ge(s("p_u" + L), it)
                sa.activation(xet_hi[:].rearrange("p (a k) t -> p a (k t)", a=2), ps[:, 4:6, :],
                              ACT.Copy).then_inc(s("xth" + L), 1)

            def silu(it):
                act.wait_ge(s("p_g" + L), it + 1)
                if not (isinstance(it, int) and it == 0):
                    act.wait_ge(s("p_ht" + L), it)
                sa.activation(hx[:], ps[:, 0, :], ACT.Silu).then_inc(s("silu" + L), 1)

            def ht_hi_(it):
                act.wait_ge(s("p_ht" + L), it + 1)
                if not (isinstance(it, int) and it == 0):
                    act.wait_ge(s("p_d" + L), it)
                sa.activation(ht_hi[:].rearrange("p k t -> p (k t)"), ps[:, 6, :], ACT.Copy).then_inc(s("hth" + L), 1)

            def y_ev(it):
                act.wait_ge(s("p_d" + L), it + 1)
                if not (isinstance(it, int) and it == 0):
                    act.wait_ge(s("y_st" + L), it * 16)
                sa.activation(ysb[:].rearrange("p (a c) -> p a c", a=2), ps[:, 2:4, :], ACT.Copy).then_inc(s("y_ev" + L), 1)

            def step(it, prev=True, prev2=True, nxt=True):
                if prev:
                    silu(it - 1)
                    hi(2, it - 1, "p_d")
                if prev2:
                    y_ev(it - 2)
                if prev:
                    ht_hi_(it - 1)
                if nxt:
                    hi(0, it + 1, "p_g")
                    xt_hi(it + 1)
                    hi(1, it + 1, "p_u")

            act.wait_ge(*mixed[l])
            hi(0, 0, "")
            hi(1, 0, "")
            xt_hi(0)
            step(0, prev=False, prev2=False)
            step(1, prev2=False)
            with act.Fori(2, E - 1) as it:
                step(it)
            step(E - 1, nxt=False)
            step(E, nxt=False)
            y_ev(E - 1)
            steps = step_count(act, l)
            with act.If(steps > E):
                with act.Fori(E, steps) as it:
                    xt_hi(it)
                    hi(0, it, "p_g")
                    hi(1, it, "p_u")
                    silu(it)
                    ht_hi_(it)
                    hi(2, it, "p_d")
                    y_ev(it)

        def experts_dve(dve, l):
            L, v = f"_{l}", nc.vector

            def lo(q, it):
                dve.wait_ge(s(f"hi{q}" + L), it + 1)
                v.tensor_tensor(wlo[q][:], raw[q][:], whi[q][:].bitcast(F32), ALU.subtract).then_inc(s(f"lo{q}" + L), 1)

            def xt_lo(it):
                dve.wait_ge(s("xth" + L), it + 1)
                v.tensor_tensor(xet_lo[:].rearrange("p (a k) t -> p a (k t)", a=2), ps[:, 4:6, :],
                                xet_hi[:].bitcast(F32).rearrange("p (a k) t -> p a (k t)", a=2),
                                ALU.subtract).then_inc(s("xtl" + L), 1)

            def h(it):
                dve.wait_ge(s("silu" + L), it + 1)
                dve.wait_ge(s("p_u" + L), it + 1)
                v.tensor_tensor(hx[:], hx[:], ps[:, 1, :], ALU.mult).then_inc(s("h" + L), 1)

            def ht_lo_(it):
                dve.wait_ge(s("hth" + L), it + 1)
                v.tensor_tensor(ht_lo[:].rearrange("p k t -> p (k t)"), ps[:, 6, :],
                                ht_hi[:].bitcast(F32).rearrange("p k t -> p (k t)"), ALU.subtract).then_inc(s("htl" + L), 1)

            def step(it, prev=True, nxt=True):
                if prev:
                    h(it - 1)
                    lo(2, it - 1)
                    ht_lo_(it - 1)
                if nxt:
                    lo(0, it + 1)
                    xt_lo(it + 1)
                    lo(1, it + 1)

            lo(0, 0)
            lo(1, 0)
            xt_lo(0)
            step(0, prev=False)
            with dve.Fori(1, E - 1) as it:
                step(it)
            step(E - 1, nxt=False)
            step(E, nxt=False)
            steps = step_count(dve, l)
            with dve.If(steps > E):
                with dve.Fori(E, steps) as it:
                    xt_lo(it)
                    lo(0, it)
                    lo(1, it)
                    h(it)
                    ht_lo_(it)
                    lo(2, it)

        def experts_pe(pe, mm3, l):
            L, te = f"_{l}", nc.tensor
            first = lambda it: isinstance(it, int) and it == 0

            def xt(it):
                pe.wait_ge(s("xe" + L), it * 16 + 16)
                if not first(it):
                    pe.wait_ge(s("xtl" + L), it)
                for k in range(KT):
                    ins = te.transpose(ps[:, 4 + k // 4, P * (k % 4):P * (k % 4) + P], xe[:, P * k:P * k + P], ident[:])
                ins.then_inc(s("p_xt" + L), 1)

            def up(q, it, done):
                pe.wait_ge(s(f"lo{q}" + L), it + 1)
                pe.wait_ge(s("xtl" + L), it + 1)
                if not first(it):
                    pe.wait_ge(s(("silu" if q == 0 else "h") + L), it)
                wh = whi[q][:].rearrange("p (k n) -> p k n", k=KT)
                wl = wlo[q][:].rearrange("p (k n) -> p k n", k=KT)
                for k in range(KT):
                    ins = mm3(ps[:, q, :], xet_hi[:, k, :], xet_lo[:, k, :], wh[:, k, :], wl[:, k, :], k == 0, k == KT - 1)
                ins.then_inc(s(done + L), 1)

            def ht(it):
                pe.wait_ge(s("h" + L), it + 1)
                if not first(it):
                    pe.wait_ge(s("htl" + L), it)
                for k in range(4):
                    ins = te.transpose(ps[:, 6, P * k:P * k + P], hx[:, P * k:P * k + P], ident[:])
                ins.then_inc(s("p_ht" + L), 1)

            def down(it):
                pe.wait_ge(s("lo2" + L), it + 1)
                pe.wait_ge(s("htl" + L), it + 1)
                if not first(it):
                    pe.wait_ge(s("y_ev" + L), it)
                wh = whi[2][:].rearrange("p (k n) -> p k n", k=4)
                wl = wlo[2][:].rearrange("p (k n) -> p k n", k=4)
                for half in range(2):
                    cols = slice(512 * half, 512 * half + 512)
                    for k in range(4):
                        ins = mm3(ps[:, 2 + half, :], ht_hi[:, k, :], ht_lo[:, k, :], wh[:, k, cols], wl[:, k, cols],
                                  k == 0, k == 3)
                ins.then_inc(s("p_d" + L), 1)

            def step(it, prev=True, nxt=True):
                up(0, it, "p_g")
                if prev:
                    ht(it - 1)
                up(1, it, "p_u")
                if nxt:
                    xt(it + 1)
                if prev:
                    down(it - 1)

            xt(0)
            step(0, prev=False)
            with pe.Fori(1, E - 1) as it:
                step(it)
            step(E - 1, nxt=False)
            ht(E - 1)
            down(E - 1)
            steps = step_count(pe, l)
            with pe.If(steps > E):
                with pe.Fori(E, steps) as it:
                    xt(it)
                    up(0, it, "p_g")
                    up(1, it, "p_u")
                    ht(it)
                    down(it)

        def combine_pool(pool, l):
            L = f"_{l}"
            pool.wait_ge(s("y_st" + L), 16 * E)
            ln_gains_pool(pool, f"ffn{l}")

            def gather(rows):
                for i, (t0, n) in enumerate(TILES):
                    if i >= 2:
                        pool.wait_ge(s("comb"), NT * l + i - 1)
                    for k in range(2):
                        pool.indirect_dma_start(out=ygat[i % 2][k][0:n, :], out_offset=None, in_=rows,
                                                in_offset=bass.IndirectOffsetOnAxis(ap=slot[0:n, k, i:i + 1], axis=0)
                                                ).then_inc(s(f"got{i % 2}"), 16)

            steps = step_count(pool, l)
            with pool.If(steps > E):
                gather(yg)
            with pool.Else():
                gather(yg[0:SLOTS])

        def combine_dve(dve, link, l):
            L, v = f"_{l}", nc.vector
            for i, (t0, n) in enumerate(TILES):
                x = xtok[0:n, i, :]
                dve.wait_ge(s("sent"), 32 * NT * l + 32 * NT)
                link(v.tensor_scalar(x, x, ALPHA, None, ALU.mult))
                dve.wait_ge(s(f"got{i % 2}"), 32 * (l * (3 - i % 2) + i // 2 + 1))
                link(v.scalar_tensor_tensor(out=x, in0=ygat[i % 2][0][0:n, :], scalar=gate[0:n, 0, i:i + 1], in1=x,
                                            op0=ALU.mult, op1=ALU.add))
                v.scalar_tensor_tensor(out=x, in0=ygat[i % 2][1][0:n, :], scalar=gate[0:n, 1, i:i + 1], in1=x,
                                       op0=ALU.mult, op1=ALU.add).then_inc(s("comb"), 1)
                dve.wait_ge(s("comb"), NT * l + i + 1)
                ln_dve(dve, link, f"ffn{l}", i)

        def store_tokens(sp_, tag):
            yp, ys = o["y_prompt"][0], o["y_sample"][0]
            for i, (t0, n) in enumerate(TILES):
                sp_.wait_ge(s("ln_x"), NT * ln_no[tag] + i + 1)
                if t0 + n <= T_PROMPT:
                    parts = [(0, n, yp[t0:t0 + n])]
                else:
                    m = T_PROMPT - t0
                    parts = [(0, m, yp[t0:T_PROMPT]), (m, n - m, ys[0:n - m])]
                for r, m, rows in parts:
                    sp_.dma_start(rows, xtok[r:r + m, i, :]).then_inc(s("tokens_out"), 16)
            sp_.wait_ge(s("tokens_out"), 16 * (NT + 1))


        G, SP_, GC, CL = 64, 64, 16, 8
        NC_P, NC_S = T_PROMPT // CL, T_SAMPLE // CL
        NCH = NC_P + NC_S
        PAIRS = G // 2
        ar0 = SB0
        Z_AT, UT_AT = ar0, ar0 + (NCH + 2) * 2 * PAIRS * 4
        SPAD_AT = UT_AT + G * NCH * 4
        UB_AT = RAW_AT[1]
        QP = 8
        W_AT = SPAD_AT + 2 * 2 * QP * 2 * NCH * 4
        CH_AT = W_AT + PAIRS * 2 * P * 4
        assert CH_AT + 2 * 4 * P * 8 <= FT_AT
        zst = at("s5_z", [P, NCH + 2, 2, PAIRS], Z_AT)
        ut = at("s5_ut", [P, G, NCH], UT_AT)
        spad = [at(f"s5_spad{i}", [P, 2, QP, 2, NCH], SPAD_AT + 4 * 2 * QP * 2 * NCH * i) for i in range(2)]
        wt = at("s5_wt", [P, PAIRS, CL, GC], SPAD_AT)
        assert PAIRS * P * 4 <= W_AT - SPAD_AT
        wl = at("s5_w", [P, 2, PAIRS, P], W_AT)
        u_g = at("s5_ug", [P, G, CL, GC], W_AT)
        mm_ = at("s5_m", [P, G, P], W_AT)
        ych = [at(f"s5_y{i}", [P, CL, P], CH_AT + 4096 * i) for i in range(2)]
        craw = at("s5_craw", [P, 2, 4, P], UB_AT + 8192)
        ct = at("s5_ct", [P, 2, PAIRS, GC], UB_AT + 12288)
        u72 = at("s5_u", [P, CL, D], FT_AT)
        ksb = at("s5_k", [P, PAIRS, P], FT_AT)
        ox = at("s5_o", [P, 2, CL + 1, PAIRS, GC], YT_AT)
        q_at = [Z_AT]

        def pre(name):
            x = at("q_" + name, [P, P], q_at[0])
            q_at[0] += 512
            return x[0:PAIRS, :]
        q = {n: pre(n) for n in ("are", "aim", "x", "y", "t", "e", "ex", "r", "k", "sn", "sh", "cm", "co", "nr", "den",
                                 "ar", "ai", "fr", "fi", "w1", "w2", "sre", "sim")}
        qdt = at("q_dt", [P, 3, 2], q_at[0])[0:PAIRS]
        qd = at("q_d", [P, 2 * GC], q_at[0] + 32)[0:PAIRS]
        qdi = at("q_di", [P, 2], q_at[0] + 32 + 128, I32)[0:PAIRS]
        q_at[0] += 32
        taken[0] = shared_end
        bb0 = small("s5_b", [2, PAIRS, GC])
        bb = small("s5_bb", [2, PAIRS, GC])
        bd = small("s5_bd", [2, PAIRS, 2 * GC])
        otmp = bd
        t4 = small("s5_t4", [4, PAIRS])
        pw = at("s5_pw", [P, 2, CL + 1, PAIRS], q_at[0] + 160)
        assert q_at[0] + 160 + 8 * (CL + 1) * PAIRS <= UB_AT
        dk = at("s5_dk", [P, PAIRS], FT_AT + PAIRS * P * 4)
        eye = at("s5_eye", [P, GC], FT_AT + PAIRS * P * 4 + 128)
        stf = at("s5_stf", [P, 4, P], FT_AT + PAIRS * P * 4 + 256)
        pr_ = at("s5_pr", [P, 2, CL, PAIRS], CH_AT)
        a8 = at("s5_a8", [P, 2, 2, PAIRS], CH_AT + 2048)
        sctmp = at("s5_tmp", [P, 2, 2, PAIRS], CH_AT + 2048 + 512)
        sg = [at(f"sg{i}", [P, 512], YT_AT + 4 * CHUNK + 2048 * i) for i in range(2)]
        ub = [at(f"ub{i}", [P, D], UB_AT + 4096 * i) for i in range(2)]
        u_d = nc.dram_tensor("u_d", (T, D), F32, kind="Internal").ap()
        wis = a["w_in_s5"][0].rearrange("(k p) n -> p k n", p=P)
        wos = a["w_out_s5"][0].rearrange("(k p) n -> p k n", p=P)
        chunks1 = [wis[:, :, 0:512], wis[:, :, 512:D], wos[:, :, 0:512], wos[:, :, D:D + 512],
                   wos[:, :, 512:D], wos[:, :, D + 512:2 * D]]

        def pairs_of(x):
            return x.rearrange("(a b) p -> a (b p)", b=2)

        def s5_sp(sp_):
            def load(c):
                if c >= 2:
                    sp_.wait_ge(s("lo_done"), 8 + c - 1)
                sp_.dma_start(raw[c % 2][:].rearrange("p (k n) -> p k n", n=512), chunks1[c]).then_inc(s(f"w_landed{c % 2}"), 16)
            steps = step_count(sp_, 0)
            sp_.wait_ge(s("comb"), 1)
            load(0)
            load(1)
            sp_.wait_ge(s("lo_done"), 10)
            for dst, src in ((q["are"], pairs_of(a["s5_a_re"][0])), (q["aim"], pairs_of(a["s5_a_im"][0])),
                             (q["sre"], pairs_of(a["state_s5_re"][0, 0])), (q["sim"], pairs_of(a["state_s5_im"][0, 0])),
                             (qdt[:, 0, :], a["s5_log_dt"][0].rearrange("(a b) -> a b", b=2)),
                             (qd, a["s5_d"][0].rearrange("(a b) -> a b", b=2 * GC))):
                sp_.dma_start(dst, src).then_inc(s("s5_par"), 16)
            sp_.wait_ge(s("ln_x"), 2 * NT)
            for ri, nm in enumerate(("re", "im")):
                b_src = a[f"s5_b_{nm}"][0].rearrange("(a b) p c -> (b p) a c", b=2)
                sp_.dma_start(bb0[:, ri], b_src).then_inc(s("s5_bc"), 16)
                c_src = a[f"s5_c_{nm}"][0].rearrange("(q j b) c p -> q b j c p", b=2, j=8)
                for qq in range(4):
                    for b in range(2):
                        sp_.dma_start(craw[:, ri, qq, 64 * b:64 * b + 64], c_src[qq, b]).then_inc(s("s5_bc"), 16)
            for i, (t0, n) in enumerate(TILES):
                sp_.wait_ge(s("ub"), i + 1)
                sp_.dma_start(u_d[t0:t0 + n], ub[i % 2][0:n, :]).then_inc(s(f"u_out{i % 2}"), 16)
            sp_.wait_ge(s("u_out0"), 16 * 3)
            sp_.wait_ge(s("u_out1"), 16 * 2)
            sp_.wait_ge(s("u1"), NT)
            sp_.dma_start(u72[0:NCH].rearrange("n s c -> n (s c)"), u_d.rearrange("(n s) c -> n (s c)", s=CL)
                          ).then_inc(s("u72"), 16)
            sp_.wait_ge(s("kd"), 1)
            sp_.wait_ge(s("m_zero"), 1)
            for st in range(CL):
                for b in range(2):
                    sp_.dma_start(mm_[GC * st:GC * st + GC, b::2, GC * st:P],
                                  ksb[GC * b:GC * b + GC, :, 0:P - GC * st]).then_inc(s("s5_m"), 16)
            sp_.wait_ge(s("stf"), 1)
            for i, nm in enumerate(("p_s5_re", "p_s5_im", "s_s5_re", "s_s5_im")):
                sp_.dma_start(pairs_of(o[nm][0, 0]), stf[0:PAIRS, i, :]).then_inc(s("s5_so"), 16)
            sp_.wait_ge(s("yt_s5"), 8)
            sp_.wait_ge(s("ytl_s5"), 8)
            load(2)
            load(3)
            load(4)
            load(5)
            sp_.wait_ge(s("s5_so"), 64)

        def by_group(i):
            return (u_g[0:NCH, 16 * i:16 * i + 16].rearrange("n g t c -> n t g c"),
                    u72[0:NCH, :, 256 * i:256 * i + 256].rearrange("n t (g c) -> n t g c", c=GC))

        def s5_pool(pool):
            g = nc.gpsimd
            pool.wait_ge(s("u1"), NT)
            pool.wait_ge(s("u72"), 16)
            for i in (1, 3):
                dst, src = by_group(i)
                g.tensor_copy(dst, src).then_inc(s("ug_pool"), 1)
            pool.wait_ge(s("bbar"), 1)
            pool.wait_ge(s("o_c"), 6 * (CL + 1))
            g.memset(bd[:], 0.0).then_inc(s("bd"), 1)
            pool.wait_ge(s("bd"), 1)
            for b in range(2):
                r_ = slice(64 * b, 64 * b + 64)
                g.tensor_copy(bd[r_, :, :, GC * b:GC * b + GC], bb[r_]).then_inc(s("bd"), 1)
            pool.wait_ge(s("bd"), 3)
            pool.wait_ge(s("x_done"), 16)
            g.memset(mm_[:], 0.0).then_inc(s("m_zero"), 1)
            for i in range(2):
                if i == 0:
                    pool.wait_ge(s("s5_fill"), 16 + 16)
                g.memset(spad[i][:], 0.0).then_inc(s("spad0"), 1)
            ln_gains_after(pool)

        def ln_gains_after(pool):
            pool.wait_ge(s("yt_s5"), 8)
            ln_gains_pool(pool, "mix1")

        def s5_act(act):
            sa = nc.scalar
            def hi(c):
                act.wait_ge(s(f"w_landed{c % 2}"), count[c % 2] + 16 * (c // 2 + 1))
                if c >= 4:
                    act.wait_ge(s("y"), 2 * NT)
                sa.activation(whi[c % 2][:], raw[c % 2][:], ACT.Copy).then_inc(s("hi_done"), 1)
            for i, (t0, n) in enumerate(TILES):
                for hf_ in range(2):
                    b = 2 * (i % 2) + hf_
                    act.wait_ge(s("xt"), 2 * NT + 2 * i + hf_ + 1)
                    sa.activation(ft_hi[:, 4 * hf_:4 * hf_ + 4, t0:t0 + n],
                                  ps[:, b, :].rearrange("p (k t) -> p k t", t=P)[:, :, 0:n],
                                  ACT.Copy).then_inc(s("xt_hi"), 1)
                if i < 2:
                    hi(i)
            act.wait_ge(s("s5d"), 1)
            sa.activation(qdt[:, 1, :], qdt[:, 0, :], ACT.Tanh, scale=0.5).then_inc(s("s5a"), 1)
            act.wait_ge(s("s5d"), 2)
            sa.activation(q["t"], q["x"], ACT.Tanh, scale=0.5).then_inc(s("s5a"), 1)
            act.wait_ge(s("s5d"), 3)
            sa.activation(q["sn"], q["r"], ACT.Sin).then_inc(s("s5a"), 1)
            sa.activation(q["sh"], q["r"], ACT.Sin, scale=0.5).then_inc(s("s5a"), 1)
            for i, (t0, n) in enumerate(TILES):
                act.wait_ge(s("u1"), i + 1)
                if i >= 2:
                    act.wait_ge(s(f"u_out{i % 2}"), 16 * (i // 2))
                b = 2 * (i % 2)
                sa.activation(ub[i % 2][0:n, :].rearrange("p (a c) -> p a c", a=2), ps[0:n, b:b + 2, :],
                              ACT.Copy).then_inc(s("ub"), 1)
                if i == 1:
                    act.wait_ge(s("s5_pt"), 2)
                    sa.activation(t4[:].rearrange("p a b -> p (a b)"), ps[:, 4, 0:4 * PAIRS], ACT.Copy).then_inc(s("t4"), 1)
                    sa.activation(ct[:].rearrange("p a b c -> p a (b c)"), ps[:, 5:7, :], ACT.Copy).then_inc(s("t4"), 1)
            act.wait_ge(s("u72"), 16)
            for i in (0, 2):
                dst, src = by_group(i)
                sa.activation(dst, src, ACT.Copy).then_inc(s("ug_act"), 1)
            act.wait_ge(s("u_out0"), 16 * 3)
            act.wait_ge(s("u_out1"), 16 * 2)
            sa.activation(zst[:, NC_P + 1].rearrange("p a b -> p (a b)"), ps[:, 4, 4 * PAIRS:6 * PAIRS],
                          ACT.Copy).then_inc(s("t4"), 1)
            act.wait_ge(s("o_c"), 6 * (CL + 1))
            for i in range(G // 4):
                act.wait_ge(s("s5_fill"), i + 1)
                sa.activation(ut[:, 4 * i:4 * i + 4, :].rearrange("p g n -> p (g n)"), ps[:, 3 + i % 2, 0:4 * NCH],
                              ACT.Copy).then_inc(s("s5_drain"), 1)
            for ri in range(2):
                for i in range(8):
                    act.wait_ge(s("s5_fill"), 16 + 8 * ri + i + 1)
                    sa.activation(wl[:, ri, 4 * i:4 * i + 4, :].rearrange("p a b -> p (a b)"), ps[:, 3 + i % 2, :],
                                  ACT.Copy).then_inc(s("s5_drain"), 1)
            for i in range(16):
                act.wait_ge(s("x_done"), i + 1)
                for ri in range(2):
                    for sl, n0, n1 in ((1, 0, NC_P), (2, NC_P, NCH)):
                        ins = sa.activation(zst[:, n0 + sl:n1 + sl, ri, 2 * i:2 * i + 2],
                                            ps[:, 5 + i % 2, 0:4 * NCH].rearrange("p (r a n) -> p r n a", r=2, a=2)[:, ri, n0:n1],
                                            ACT.Copy)
                ins.then_inc(s("x_in"), 1)
            for i in range(8):
                act.wait_ge(s("s5_fill"), 32 + i + 1)
                sa.activation(ksb[0:2 * GC, 4 * i:4 * i + 4, :].rearrange("p a b -> p (a b)"), ps[0:2 * GC, 3 + i % 2, :],
                              ACT.Copy).then_inc(s("s5_drain"), 1)
            sa.activation(dk[0:2 * GC, :], ps[0:2 * GC, 7, 0:PAIRS], ACT.Copy).then_inc(s("s5_drain"), 1)
            act.wait_ge(s("z_done"), NCH)
            act.wait_ge(s("spad0"), 2)
            act.wait_ge(s("s5_pt"), 3)
            sa.activation(stf[0:PAIRS].rearrange("p a b -> p (a b)"), ps[0:PAIRS, 0, :], ACT.Copy).then_inc(s("stf"), 1)

            def pad_states(c):
                if c >= 2:
                    act.wait_ge(s("y_mm"), 2 * (c - 1))
                for b in range(2):
                    r_ = slice(64 * b, 64 * b + 64)
                    for n0, n1, sl in ((0, NC_P, 0), (NC_P, NCH, 1)):
                        ins = sa.activation(spad[c % 2][r_, :, :, b, n0:n1],
                                            zst[r_, n0 + sl:n1 + sl, :, QP * c:QP * c + QP].rearrange("p n r a -> p r a n"),
                                            ACT.Copy)
                ins.then_inc(s("spad"), 1)

            def y_gelu(i):
                act.wait_ge(s("y_mm"), i + 1)
                if i >= 2:
                    act.wait_ge(s("yt_s5"), i - 1)
                for hb_ in range(2):
                    ins = sa.activation(ych[i % 2][0:NCH, :, 64 * hb_:64 * hb_ + 64].rearrange("n t (g c) -> n g t c", c=GC),
                                        ps[0:NCH, 2 * (i % 2) + hb_, :].rearrange("n (g t c) -> n g t c", g=4, c=GC),
                                        ACT.Gelu_apprx_tanh)
                ins.then_inc(s("y_gelu"), 1)

            def y_hi(i):
                act.wait_ge(s("yt_s5"), i + 1)
                for hb_ in range(2):
                    ins = sa.activation(ft_hi[:, i, :].rearrange("p (n t) -> p t n", t=CL)[:, 4 * hb_:4 * hb_ + 4, :],
                                        ps[:, 4 + 2 * (i % 2) + hb_, 0:4 * NCH].rearrange("p (t n) -> p t n", n=NCH), ACT.Copy)
                ins.then_inc(s("yth_s5"), 1)

            pad_states(0)
            pad_states(1)
            for i in range(8):
                y_gelu(i)
                if i in (1, 3):
                    pad_states(2 + i // 2)
                if i:
                    y_hi(i - 1)
            y_hi(7)
            hi(2)
            hi(3)
            for ph in range(2):
                for i, (t0, n) in enumerate(TILES):
                    j = NT * ph + i
                    act.wait_ge(s("y"), NT + j + 1)
                    if j >= 2:
                        act.wait_ge(s("mix1_glu"), 2 * j - 2)
                    sa.activation(sg[j % 2][0:n, :], ps[0:n, 2 * (j % 2) + 1, :], ACT.Sigmoid).then_inc(s("sg"), 1)
                    if ph and i:
                        ln_act(act, "mix1", [i - 1])
                if ph == 0:
                    hi(4)
                    hi(5)
            ln_act(act, "mix1", [NT - 1])

        def s5_dve(dve, link, split_lo):
            v = nc.vector
            tt, ts = v.tensor_tensor, v.tensor_scalar
            def lo(c):
                dve.wait_ge(s("hi_done"), 8 + c + 1)
                tt(wlo[c % 2][:], raw[c % 2][:], whi[c % 2][:].bitcast(F32), ALU.subtract).then_inc(s("lo_done"), 1)
            for i, (t0, n) in enumerate(TILES):
                for hf_ in range(2):
                    b = 2 * (i % 2) + hf_
                    dve.wait_ge(s("xt_hi"), 2 * NT + 2 * i + hf_ + 1)
                    ins = tt(ft_lo[:, 4 * hf_:4 * hf_ + 4, t0:t0 + n],
                             ps[:, b, :].rearrange("p (k t) -> p k t", t=P)[:, :, 0:n],
                             ft_hi[:, 4 * hf_:4 * hf_ + 4, t0:t0 + n].bitcast(F32), ALU.subtract)
                ins.then_inc(s("x_split"), 1)
                if i < 2:
                    lo(i)
            M, A_, S_ = ALU.mult, ALU.add, ALU.subtract
            MAGIC = 12582912.0
            LN2_HI = 0.693145751953125
            LN2_LO = 0.6931471805599453 - LN2_HI
            d0, d1, d2 = (qdt[:, i, :] for i in range(3))
            dve.wait_ge(s("s5_par"), 16 * 6)
            link(ts(d2, d0, 1.0 / 0.6931471805599453, MAGIC, M, A_))
            link(ts(d2, d2, MAGIC, None, S_))
            link(v.scalar_tensor_tensor(out=d0, in0=d2, scalar=-LN2_HI, in1=d0, op0=M, op1=A_))
            v.scalar_tensor_tensor(out=d0, in0=d2, scalar=-LN2_LO, in1=d0, op0=M, op1=A_).then_inc(s("s5d"), 1)
            link(ts(d2, d2, 127.0, 8388608.0, A_, M))
            link(v.tensor_copy(qdi, d2))
            dve.wait_ge(s("s5a"), 1)
            link(ts(d2, d1, -1.0, 1.0, M, A_))
            link(v.reciprocal(d2, d2))
            link(ts(d1, d1, 1.0, None, A_))
            link(tt(d0, d1, d2, M))
            link(tt(d0, d0, qdi.bitcast(F32), M))
            two = lambda x: x.rearrange("p (b k) -> p b k", b=2)
            dtb = d0.rearrange("p (b x) -> p b x", x=1).to_broadcast([PAIRS, 2, SP_])
            tt(two(q["y"]), two(q["aim"]), dtb, M)
            tt(two(q["x"]), two(q["are"]), dtb, M).then_inc(s("s5d"), 1)
            dve.wait_ge(s("s5d"), 2)
            C1 = 6.28125
            C2 = 0.0019350051879882812
            C3 = 6.283185307179586 - C1 - C2
            link(ts(q["k"], q["y"], 1.0 / 6.283185307179586, MAGIC, M, A_))
            link(ts(q["k"], q["k"], MAGIC, None, S_))
            link(v.scalar_tensor_tensor(out=q["r"], in0=q["k"], scalar=-C1, in1=q["y"], op0=M, op1=A_))
            link(v.scalar_tensor_tensor(out=q["r"], in0=q["k"], scalar=-C2, in1=q["r"], op0=M, op1=A_))
            link(v.scalar_tensor_tensor(out=q["r"], in0=q["k"], scalar=-C3, in1=q["r"], op0=M, op1=A_))
            ts(q["r"], q["r"], 3.1415925, -3.1415925, ALU.min, ALU.max).then_inc(s("s5d"), 1)
            dve.wait_ge(s("s5a"), 2)
            link(ts(q["w1"], q["t"], -1.0, 1.0, M, A_))
            link(v.reciprocal(q["w1"], q["w1"]))
            link(v.scalar_tensor_tensor(out=q["e"], in0=q["t"], scalar=2.0, in1=q["w1"], op0=M, op1=M))
            link(ts(q["ex"], q["e"], 1.0, None, A_))
            dve.wait_ge(s("s5a"), 4)
            link(tt(q["cm"], q["sh"], q["sh"], M))
            link(ts(q["co"], q["cm"], -2.0, 1.0, M, A_))
            link(tt(q["ar"], q["ex"], q["co"], M))
            link(tt(q["ai"], q["ex"], q["sn"], M))
            link(tt(q["nr"], q["e"], q["co"], M))
            link(v.scalar_tensor_tensor(out=q["nr"], in0=q["cm"], scalar=-2.0, in1=q["nr"], op0=M, op1=A_))
            link(tt(q["w1"], q["are"], q["are"], M))
            link(tt(q["w2"], q["aim"], q["aim"], M))
            link(tt(q["den"], q["w1"], q["w2"], A_))
            link(v.reciprocal(q["den"], q["den"]))
            link(tt(q["w1"], q["nr"], q["are"], M))
            link(tt(q["w2"], q["ai"], q["aim"], M))
            link(tt(q["w1"], q["w1"], q["w2"], A_))
            link(tt(q["fr"], q["w1"], q["den"], M))
            link(tt(q["w1"], q["ai"], q["are"], M))
            link(tt(q["w2"], q["nr"], q["aim"], M))
            link(tt(q["w1"], q["w1"], q["w2"], S_))
            tt(q["fi"], q["w1"], q["den"], M).then_inc(s("s5d"), 1)
            dve.wait_ge(s("t4"), 2)
            link(v.memset(pw[:, 1, 0, :], 0.0))
            link(v.memset(pw[:, 0, 0, :], 1.0))
            link(v.tensor_copy(pw[:, :, 1, :], t4[:, 0:2, :]))
            ot = otmp[:].rearrange("p a b c -> p (a b c)")
            tm = ot[:, 0:4 * PAIRS].rearrange("p (a n) -> p a n", n=PAIRS)

            def cmul(lo_, n, by):
                ar_, ai_ = (pw[:, r_, lo_:lo_ + n, :] for r_ in range(2))
                br_, bi_ = (pw[:, r_, by:by + 1, :].to_broadcast([P, n, PAIRS]) for r_ in range(2))
                out = slice(lo_ + by, lo_ + by + n)
                tr = tm[:, 0:n, :]
                link(tt(pw[:, 0, out, :], ar_, br_, M))
                link(tt(tr, ai_, bi_, M))
                link(tt(pw[:, 0, out, :], pw[:, 0, out, :], tr, S_))
                link(tt(pw[:, 1, out, :], ar_, bi_, M))
                link(tt(tr, ai_, br_, M))
                link(tt(pw[:, 1, out, :], pw[:, 1, out, :], tr, A_))
            cmul(1, 1, 1)
            cmul(1, 2, 2)
            cmul(1, 4, 4)
            dve.wait_ge(s("s5_bc"), 16 * 18)
            over = lambda x: x.rearrange("p (a x) -> p a x", x=1).to_broadcast([P, PAIRS, GC])
            fr, fi = over(t4[:, 2, :]), over(t4[:, 3, :])
            tb = ot[:, 0:PAIRS * GC].rearrange("p (a c) -> p a c", c=GC)
            link(tt(bb[:, 0], bb0[:, 0], fr, M))
            link(tt(tb, bb0[:, 1], fi, M))
            link(tt(bb[:, 0], bb[:, 0], tb, S_))
            link(tt(bb[:, 1], bb0[:, 1], fr, M))
            link(tt(tb, bb0[:, 0], fi, M))
            tt(bb[:, 1], bb[:, 1], tb, A_).then_inc(s("bbar"), 1)
            dve.wait_ge(s("bbar"), 1)
            cr, ci = ct[:, 0], ct[:, 1]
            for tau in range(CL + 1):
                pr0, pi0 = over(pw[:, 0, tau, :]), over(pw[:, 1, tau, :])
                ta, tb_ = (ot[:, 512 * (2 * (tau % 2) + x):512 * (2 * (tau % 2) + x) + 512].rearrange("p (a c) -> p a c", c=GC) for x in range(2))
                tt(ta, ci, pi0, M).then_inc(s("o_c"), 1)
                tt(tb_, ci, pr0, M).then_inc(s("o_c"), 1)
                tt(ox[:, 0, tau], cr, pr0, M).then_inc(s("o_c"), 1)
                tt(ox[:, 1, tau], cr, pi0, M).then_inc(s("o_c"), 1)
                dve.wait_ge(s("o_c"), 6 * tau + 3)
                tt(ox[:, 0, tau], ox[:, 0, tau], ta, S_).then_inc(s("o_c"), 1)
                dve.wait_ge(s("o_c"), 6 * tau + 4)
                v.scalar_tensor_tensor(out=ox[:, 1, tau].rearrange("p a c -> p (a c)"),
                                       in0=ox[:, 1, tau].rearrange("p a c -> p (a c)"), scalar=-1.0,
                                       in1=tb_.rearrange("p a c -> p (a c)"), op0=M, op1=S_).then_inc(s("o_c"), 1)
                dve.wait_ge(s("o_c"), 6 * tau + 6)
            dve.wait_ge(s("u1"), NT)
            for st in range(CL):
                v.tensor_copy(pr_[:, :, st, :], pw[:, :, CL - 1 - st, :])
            for r_ in range(2):
                link(v.tensor_copy(a8[:, 0, r_, :], pw[:, 0, CL, :]))
            link(v.tensor_copy(a8[:, 1, 0, :], pw[:, 1, CL, :]))
            link(ts(a8[:, 1, 1, :], pw[:, 1, CL, :], -1.0, None, M))
            for ri in range(2):
                if ri:
                    dve.wait_ge(s("s5_fill"), 16 + 8)
                for st in range(CL):
                    x0, x1 = over(pr_[:, 0, st, :]), over(pr_[:, 1, st, :])
                    first, second = (x0, x1) if ri == 0 else (x1, x0)
                    dst = wt[:, :, st, :]
                    tmp = bb0[:, st % 2]
                    tt(dst, bb[:, 0], first, M).then_inc(s("w_m"), 1)
                    tt(tmp, bb[:, 1], second, M).then_inc(s("w_m"), 1)
                    dve.wait_ge(s("w_m"), 3 * (8 * ri + st) + 2)
                    tt(dst, dst, tmp, S_ if ri == 0 else A_).then_inc(s("w_m"), 1)
                    dve.wait_ge(s("w_m"), 3 * (8 * ri + st) + 3)
            dve.wait_ge(s("x_in"), 16)
            link(v.memset(zst[:, 0], 0.0))
            nz = 0
            cnt = 0
            for n in range(NCH):
                sl = n + (n >= NC_P)
                z0, z1 = zst[:, sl], zst[:, sl + 1]
                ta, tb_ = sctmp[:, 0], sctmp[:, 1]
                if n:
                    dve.wait_ge(s("z_done"), n)
                tt(ta, z0, a8[:, 0], M).then_inc(s("z_a"), 1)
                for r_ in range(2):
                    ins = tt(tb_[:, 1 - r_, :], z0[:, r_, :], a8[:, 1, r_, :], M)
                ins.then_inc(s("z_a"), 1)
                dve.wait_ge(s("z_a"), 3 * n + 1)
                tt(z1, z1, ta, A_).then_inc(s("z_a"), 1)
                dve.wait_ge(s("z_a"), 3 * n + 3)
                tt(z1, z1, tb_, A_).then_inc(s("z_done"), 1)
            dve.wait_ge(s("z_done"), NCH)
            dve.wait_ge(s("s5_drain"), 32 + 9)
            g2 = 2 * GC
            link(tt(eye[0:g2, :], ident[0:g2, 0:GC], ident[0:g2, GC:g2], A_))
            tmp = bb0[0:g2, 0]
            link(tt(tmp, dk[0:g2, :].rearrange("p (a x) -> p a x", x=1).to_broadcast([g2, PAIRS, GC]),
                    eye[0:g2, :].rearrange("p (x c) -> p x c", x=1).to_broadcast([g2, PAIRS, GC]), M))
            tt(ksb[0:g2, :, 0:GC], ksb[0:g2, :, 0:GC], tmp, A_).then_inc(s("kd"), 1)
            dve.wait_ge(s("s5_so"), 64)
            for i in range(8):
                dve.wait_ge(s("yth_s5"), i + 1)
                for hb_ in range(2):
                    dst = ft_lo[:, i, :].rearrange("p (n t) -> p t n", t=CL)[:, 4 * hb_:4 * hb_ + 4, :]
                    ins = tt(dst, ps[:, 4 + 2 * (i % 2) + hb_, 0:4 * NCH].rearrange("p (t n) -> p t n", n=NCH),
                             ft_hi[:, i, :].bitcast(F32).rearrange("p (n t) -> p t n", t=CL)[:, 4 * hb_:4 * hb_ + 4, :], S_)
                ins.then_inc(s("ytl_s5"), 1)
            lo(2)
            lo(3)
            for ph in range(2):
                if ph:
                    lo(4)
                    lo(5)
                for i, (t0, n) in enumerate(TILES):
                    j = NT * ph + i
                    dve.wait_ge(s("sg"), j + 1)
                    x = xtok[0:n, i, 512 * ph:512 * ph + 512]
                    tt(sg[j % 2][0:n, :], sg[j % 2][0:n, :], ps[0:n, 2 * (j % 2), :], M).then_inc(s("mix1_glu"), 1)
                    dve.wait_ge(s("mix1_glu"), 2 * j + 1)
                    v.scalar_tensor_tensor(out=x, in0=x, scalar=ALPHA, in1=sg[j % 2][0:n, :], op0=M,
                                           op1=A_).then_inc(s("mix1_glu"), 1)
                    if ph:
                        dve.wait_ge(s("mix1_glu"), 2 * j + 2)
                        ln_dve(dve, link, "mix1", i)

        def s5_pe(pe, mm3):
            te = nc.tensor
            for i, (t0, n) in enumerate(TILES):
                pe.wait_ge(s("ln_x"), NT + i + 1)
                if i >= 2:
                    pe.wait_ge(s("x_split"), NT + i - 1)
                for k in range(KT):
                    b = 2 * (i % 2) + k // 4
                    ins = te.transpose(ps[:, b, P * (k % 4):P * (k % 4) + n], xtok[0:n, i, P * k:P * k + P], ident[0:n, 0:n])
                    if k % 4 == 3:
                        ins.then_inc(s("xt"), 1)
            pe.wait_ge(s("x_split"), 2 * NT)
            pe.wait_ge(s("lo_done"), 10)

            def token_major(i, l_hi, l_lo, sem_):
                t0, n = TILES[i]
                for half in range(2):
                    wh = whi[half][:].rearrange("p (k n) -> p k n", n=512)
                    wl_ = wlo[half][:].rearrange("p (k n) -> p k n", n=512)
                    for k in range(KT):
                        ins = mm3(ps[0:n, 2 * (sem_[1] % 2) + half, :], l_hi[:, k, t0:t0 + n], l_lo[:, k, t0:t0 + n],
                                  wh[:, k, :], wl_[:, k, :], k == 0, k == KT - 1)
                ins.then_inc(s(sem_[0]), 1)

            for i in range(NT):
                if i == 2:
                    pe.wait_ge(s("s5d"), 4)
                    pe.wait_ge(s("s5_bc"), 16 * 18)
                    for m, nm in enumerate(("ar", "ai", "fr", "fi", "sre", "sim")):
                        te.transpose(ps[:, 4, PAIRS * m:PAIRS * m + PAIRS], q[nm], ident[0:PAIRS, 0:PAIRS])
                    te.transpose(ps[0:2 * GC, 7, 0:PAIRS], qd, ident[0:PAIRS, 0:PAIRS]).then_inc(s("s5_pt"), 1)
                    for ri in range(2):
                        for qq in range(4):
                            ins = te.transpose(ps[:, 5 + ri, P * qq:P * qq + P], craw[:, ri, qq, :], ident[:])
                    ins.then_inc(s("s5_pt"), 1)
                if i >= 2:
                    pe.wait_ge(s("ub"), i - 1)
                token_major(i, ft_hi, ft_lo, ("u1", i))
            pe.wait_ge(s("ub"), NT)
            pe.wait_ge(s("t4"), 3)
            for i in range(G // 4):
                if i % 4 == 0:
                    pe.wait_ge(s("ug_pool" if i % 8 else "ug_act"), i // 8 + 1)
                if i >= 2:
                    pe.wait_ge(s("s5_drain"), i - 1)
                for j in range(4):
                    g_ = 4 * i + j
                    ins = te.transpose(ps[:, 3 + i % 2, NCH * j:NCH * j + NCH], u_g[0:NCH, g_].rearrange("n t c -> n (t c)"),
                                       ident[0:NCH, 0:NCH])
                ins.then_inc(s("s5_fill"), 1)
            for ri in range(2):
                pe.wait_ge(s("w_m"), 24 * (ri + 1))
                for i in range(8):
                    pe.wait_ge(s("s5_drain"), 16 + 8 * ri + i - 1)
                    for j in range(4):
                        ins = te.transpose(ps[:, 3 + i % 2, P * j:P * j + P], wt[:, 4 * i + j].rearrange("p a b -> p (a b)"),
                                           ident[:])
                    ins.then_inc(s("s5_fill"), 1)
            pe.wait_ge(s("s5_drain"), 32)
            for i in range(16):
                if i >= 2:
                    pe.wait_ge(s("x_in"), i - 1)
                for ri in range(2):
                    for j in range(2):
                        for b in range(2):
                            pair = 2 * i + j
                            c0 = (2 * ri + j) * NCH
                            ins = te.matmul(ps[64 * b:64 * b + 64, 5 + i % 2, c0:c0 + NCH],
                                            wl[:, ri, pair, 64 * b:64 * b + 64], ut[:, 2 * pair + b, :], start=True, stop=True)
                ins.then_inc(s("x_done"), 1)
            pe.wait_ge(s("bd"), 3)
            for i in range(8):
                if i >= 2:
                    pe.wait_ge(s("s5_drain"), 32 + i - 1)
                for j in range(4):
                    pair = 4 * i + j
                    for ri in range(2):
                        ins = te.matmul(ps[0:2 * GC, 3 + i % 2, P * j:P * j + P], bd[:, ri, pair, :],
                                        ox[:, ri, 0:CL, pair, :], start=(ri == 0), stop=(ri == 1))
                ins.then_inc(s("s5_fill"), 1)
            pe.wait_ge(s("z_done"), NCH)
            for i, (sl, ri) in enumerate(((NC_P, 0), (NC_P, 1), (NCH + 1, 0), (NCH + 1, 1))):
                ins = te.transpose(ps[0:PAIRS, 0, P * i:P * i + P], zst[:, sl, ri, :], ident[:])
            ins.then_inc(s("s5_pt"), 1)
            pe.wait_ge(s("s5_m"), 16 * 16)
            pe.wait_ge(s("stf"), 1)
            pe.wait_ge(s("s5_drain"), 32 + 9)
            pe.wait_ge(s("x_in"), 16)
            def outputs(i):
                pe.wait_ge(s("spad"), i // 2 + 1)
                if i >= 2:
                    pe.wait_ge(s("y_gelu"), i - 1)
                for j in range(8):
                    g_ = 8 * i + j
                    pair, b = g_ // 2, g_ % 2
                    out = ps[0:NCH, 2 * (i % 2) + j // 4, P * (j % 4):P * (j % 4) + P]
                    te.matmul(out, ut[:, g_, :], mm_[:, g_, :], start=True, stop=False)
                    for ri in range(2):
                        ins = te.matmul(out, spad[(i // 2) % 2][:, ri, pair % QP, b, :], ox[:, ri, 1:CL + 1, pair, :],
                                        start=False, stop=(ri == 1))
                ins.then_inc(s("y_mm"), 1)

            def outputs_t(i):
                pe.wait_ge(s("y_gelu"), i + 1)
                if i >= 2:
                    pe.wait_ge(s("ytl_s5"), i - 1)
                for st in range(CL):
                    ins = te.transpose(ps[:, 4 + 2 * (i % 2) + st // 4, NCH * (st % 4):NCH * (st % 4) + NCH],
                                       ych[i % 2][0:NCH, st, :], ident[0:NCH, 0:NCH])
                ins.then_inc(s("yt_s5"), 1)

            for i in range(8):
                outputs(i)
                if i:
                    outputs_t(i - 1)
            outputs_t(7)
            pe.wait_ge(s("ytl_s5"), 8)
            for ph in range(2):
                pe.wait_ge(s("lo_done"), 12 + 2 * ph)
                for i in range(NT):
                    j = NT * ph + i
                    if j >= 2:
                        pe.wait_ge(s("mix1_glu"), 2 * j - 2)
                    token_major(i, ft_hi, ft_lo, ("y", j))

        block = ctx.enter_context(nc.Block())

        @block.sync
        def _(sp_):
            def load_chunk(c):
                if c >= 2:
                    sp_.wait_ge(s("lo_done"), c - 1)
                for src, col, n in chunks0[c]:
                    dst = raw[c % 2][:].rearrange("p (k n) -> p k n", n=512)[:, :, col:col + n]
                    sp_.dma_start(dst, src).then_inc(s(f"w_landed{c % 2}"), 16)

            for i, (t0, n) in enumerate(TILES):
                for r, m, rows in x_rows(t0, n):
                    sp_.dma_start(xin[i][r:r + m, :], rows).then_inc(s(f"x_landed{x_group[i]}"), 16)
            load_chunk(0)
            load_chunk(1)
            for c in range(2, len(chunks0)):
                load_chunk(c)
            for i, (t0, n) in enumerate(TILES):
                sp_.wait_ge(s("ycat_lo"), KT)
                for r, m, rows in x_rows(t0, n):
                    sp_.dma_start(xtok[r:r + m, i, :], rows).then_inc(s("res_landed"), 16)
            sp_.wait_ge(s("res_landed"), 16 * (NT + 1))
            experts_sp(sp_, 0)
            s5_sp(sp_)
            experts_sp(sp_, 1)
            store_tokens(sp_, "ffn1")

        @block.gpsimd
        def _(pool):
            g = nc.gpsimd
            g.memset(ident[:], 0.0).then_inc(s("pc"), 1)
            pool.wait_ge(s("pc"), 1)
            g.affine_select(out=ident[:], in_=ident[:], compare_op=ALU.not_equal, fill=1.0, base=0,
                            pattern=[[-1, P]], channel_multiplier=1).then_inc(s("pc"), 1)
            for dst, src in param_dmas:
                with nc.allow_non_contiguous_dma(reason="per-channel parameters, one word to a partition"):
                    pool.dma_start(dst, src).then_inc(s("params"), 16)
            g.memset(wr[:], 0.0).then_inc(s("wz"), 1)
            g.memset(wi[:], 0.0).then_inc(s("wz"), 1)
            for i in range(2):
                g.memset(zx[i][:, 0:CONV - 1], 0.0).then_inc(s("wz"), 1)
                g.memset(zx[i][:, LRU_W - 1:LRU_W], 0.0).then_inc(s("wz"), 1)
            pool.wait_ge(s("wz"), 6)
            for hh in range(2):
                r = slice(64 * hh, 64 * hh + 64)
                for dst, nm in ((wr, "lru_w_r"), (wi, "lru_w_i")):
                    pool.dma_start(dst[r, :, 64 * hh:64 * hh + 64],
                                   a[nm][0].rearrange("(j b) k n -> b k j n", b=2)[hh]).then_inc(s("wri"), 16)
            g.memset(causal[:], 1.0).then_inc(s("pc"), 1)
            g.memset(blkmask[:], 1.0).then_inc(s("pc"), 1)
            g.memset(ones[:], 1.0).then_inc(s("pc"), 1)
            g.memset(m0[:], 1.0).then_inc(s("pc"), 1)
            g.memset(eps[:, 0:1], RMS_EPS).then_inc(s("pc"), 1)
            g.memset(eps[:, 1:2], LN_EPS).then_inc(s("pc"), 1)
            g.memset(lstrict[:], 1.0).then_inc(s("pc"), 1)
            for q in range(PER_GROUP):
                g.memset(wt4[:, q:q + 1], float(PER_GROUP - q)).then_inc(s("pc"), 1)
            for q in range(E):
                g.memset(e128[:, q:q + 1], float(CAP * q)).then_inc(s("pc"), 1)
            g.memset(zeros[:], 0.0).then_inc(s("pc"), 1)
            pool.wait_ge(s("pc"), 30)
            g.affine_select(out=lstrict[:], in_=lstrict[:], compare_op=ALU.is_ge, fill=0.0, base=-1,
                            pattern=[[1, P]], channel_multiplier=-1).then_inc(s("pc"), 1)
            g.affine_select(out=causal[:], in_=causal[:], compare_op=ALU.is_ge, fill=0.0, base=0,
                            pattern=[[1, P]], channel_multiplier=-1).then_inc(s("pc"), 1)
            g.affine_select(out=blkmask[:], in_=blkmask[:], compare_op=ALU.is_ge, fill=0.0, base=0,
                            pattern=[[-BLK, 8]], channel_multiplier=1).then_inc(s("pc"), 1)
            g.memset(m0[:, 0:1], 0.0).then_inc(s("pc"), 1)
            pool.wait_ge(s("pc"), 34)
            g.affine_select(out=blkmask[:], in_=blkmask[:], compare_op=ALU.is_ge, fill=0.0, base=BLK - 1,
                            pattern=[[BLK, 8]], channel_multiplier=-1).then_inc(s("pc"), 1)
            g.affine_select(out=causal[:].rearrange("p (b i) -> p b i", i=BLK),
                            in_=causal[:].rearrange("p (b i) -> p b i", i=BLK),
                            compare_op=ALU.is_ge, fill=0.0, base=0, pattern=[[-BLK, 8], [0, BLK]],
                            channel_multiplier=1).then_inc(s("pc"), 1)
            pool.wait_ge(s("lo_done"), 2)
            for q in range(4):
                pool.dma_start(xg[CAP * 4 * q:CAP * 4 * q + CAP * 4].rearrange("(q p) d -> p q d", p=P),
                               zeros[:].rearrange("p (q d) -> p q d", q=1).to_broadcast([P, 4, D])
                               ).then_inc(s("xg_zero"), 16)
            pool.wait_ge(s("lru_st"), 4 * LRU_TILES)
            for i, tag in enumerate(("p", "s")):
                with nc.allow_non_contiguous_dma(reason="states, one word to a channel"):
                    for k in range(CONV - 1):
                        pool.dma_start(o[tag + "_lru_conv"][0, 0, k].rearrange("(j p) -> p j", p=P),
                                       convst[:, i, k]).then_inc(s("lru_out"), 16)
                    pool.dma_start(o[tag + "_lru_h"][0, 0].rearrange("(j p) -> p j", p=P),
                                   hst[:, i]).then_inc(s("lru_out"), 16)
            pool.wait_ge(s("ycat_lo"), LRU_TILES)
            pool.wait_ge(s("xg_zero"), 16 * 4)
            pool.dma_start(s_in[:], a["state_hgrn2"][0, 0, 0]).then_inc(s("st_in"), 16)
            for h in range(HEADS):
                for tt, (t0, n) in enumerate(HTILES):
                    i = 5 * h + tt
                    nb = n // BLK
                    pool.wait_ge(s("hg_tok"), 4 * h + 2)
                    if i:
                        pool.wait_ge(s("uinc"), 9 * h + 2 * tt)
                    g.tensor_tensor(vmask[0:n, 0:nb, :],
                                    vtok[0:n, tt:tt + 1, :].to_broadcast([n, nb, P]),
                                    blkmask[0:n, 0:nb].rearrange("p (b x) -> p b x", x=1).to_broadcast([n, nb, P]),
                                    ALU.mult).then_inc(s("vmask"), 1)
                pool.wait_ge(s("state"), NBLK * h + NBLK_P)
                pool.dma_start(o["p_hgrn2"][0, 0, h], srn[:, NBLK_P % SRING, :]).then_inc(s("st_out"), 16)
                pool.wait_ge(s("state"), NBLK * (h + 1))
                pool.dma_start(o["s_hgrn2"][0, 0, h], srn[:, (NBLK + 1) % SRING, :]).then_inc(s("st_out"), 16)
                if h + 1 < HEADS:
                    pool.wait_ge(s("o_done"), 5 * (h + 1))
                    pool.dma_start(s_in[:], a["state_hgrn2"][0, 0, h + 1]).then_inc(s("st_in"), 16)
            pool.wait_ge(s("st_out"), 32 * HEADS)
            pool.wait_ge(s("lru_out"), 16 * 8)
            pool.wait_ge(s("ycat_lo"), KT)
            ln_gains_pool(pool, "mix0")
            route_pool(pool, 0)
            experts_pool(pool, 0)
            combine_pool(pool, 0)
            s5_pool(pool)
            route_pool(pool, 1)
            experts_pool(pool, 1)
            combine_pool(pool, 1)

        @block.scalar
        def _(act):
            sc_ = nc.scalar
            n_link = [0]

            def link(ins):
                n_link[0] += 1
                ins.then_inc(s("act_chain"), 1)
                act.wait_ge(s("act_chain"), n_link[0])

            def split_hi(c):
                act.wait_ge(s(f"w_landed{c % 2}"), landed[c])
                if c >= 2:
                    act.wait_ge(s("z"), 4 * (c - 1))
                sc_.activation(whi[c % 2][:], raw[c % 2][:], ACT.Copy).then_inc(s("hi_done"), 1)

            for i, (t0, n) in enumerate(TILES):
                for hf_ in range(2):
                    b = 2 * (i % 2) + hf_
                    act.wait_ge(s("xt"), 2 * i + hf_ + 1)
                    sc_.activation(ft_hi[:, 4 * hf_:4 * hf_ + 4, t0:t0 + n],
                                   ps[:, b, :].rearrange("p (k t) -> p k t", t=P)[:, :, 0:n],
                                   ACT.Copy).then_inc(s("xt_hi"), 1)
            split_hi(0)
            act.wait_ge(s("prep"), 1)
            sc_.activation(sp[:, 1, :], sp[:, 0, :], ACT.Exp, scale=-1.0).then_inc(s("prep_a"), 1)
            sc_.activation(lbs[:, 0:2, :], lbs[:, 2:4, :], ACT.Exp).then_inc(s("prep_a"), 1)
            split_hi(1)

            def conv_input(j):
                zi, x = 4 * (j // 2) + j % 2, zx[j % 2]
                act.wait_ge(s("z"), zi + 1)
                b = 2 * (zi % 2)
                if j >= 2:
                    act.wait_ge(s("u_done"), j - 1)
                    act.wait_ge(s("lru_st"), 8 * (j // 2 - 1) + 2 * (j % 2) + 2)
                else:
                    act.wait_ge(s("wz"), 6)
                    act.wait_ge(s("params"), 16 * len(param_dmas))
                sc_.activation(x[:, S0_AT:S0_AT + CONV - 1], past[:, :, j], ACT.Copy)
                sc_.activation(x[:, 3:3 + HALF], ps[:, b, 0:HALF], ACT.Copy)
                sc_.activation(x[:, 3 + HALF:3 + T_PROMPT], ps[:, b + 1, 0:T_PROMPT - HALF], ACT.Copy)
                sc_.activation(x[:, S0_AT + 3:S0_AT + 3 + T_SAMPLE],
                               ps[:, b + 1, T_PROMPT - HALF:HALF], ACT.Copy).then_inc(s("z_free"), 1)

            def gates(j):
                h2 = LRU_U // 2
                act.wait_ge(s("ri"), j + 1)
                if j:
                    act.wait_ge(s("lru_y"), j)
                sc_.activation(lr[:].rearrange("p (a t) -> p a t", a=2), ps[:, 4:6, 0:h2], ACT.Sigmoid,
                               bias=b_r[:, j:j + 1]).then_inc(s("lru_act"), 1)
                sc_.activation(li[:].rearrange("p (a t) -> p a t", a=2), ps[:, 6:8, 0:h2], ACT.Sigmoid,
                               bias=b_i[:, j:j + 1]).then_inc(s("lru_act"), 1)
                act.wait_ge(s("lru_act"), 4 * j + 1)
                act.wait_ge(s("spl"), 1)
                sc_.activation(lt[:], lr[:], ACT.Tanh, scale=spl4[:, j:j + 1]).then_inc(s("lru_act"), 1)
                act.wait_ge(s("lru_act"), 4 * j + 3)
                sc_.activation(lq[:], lt[:], ACT.Sqrt).then_inc(s("lru_act"), 1)

            def gelu_gate(j):
                zi = 4 * (j // 2) + 2 + j % 2
                act.wait_ge(s("z"), zi + 1)
                if j >= 2:
                    act.wait_ge(s("lru_y"), j - 1)
                b = 2 * (zi % 2)
                sc_.activation(gz[j % 2][:].rearrange("p (a t) -> p a t", a=2), ps[:, b:b + 2, 0:HALF],
                               ACT.Gelu_apprx_tanh).then_inc(s("z_free"), 1)

            def lru_y_hi(j):
                act.wait_ge(s("lru_y"), j + 1)
                sc_.activation(yt_hi[:, j, :], ld[:, 0:T], ACT.Copy).then_inc(s("ycat_hi"), 1)

            for jp in range(LRU_TILES // 2):
                j = 2 * jp
                conv_input(j)
                conv_input(j + 1)
                if jp:
                    lru_y_hi(j - 1)
                gates(j)
                gelu_gate(j)
                lru_y_hi(j)
                gates(j + 1)
                gelu_gate(j + 1)
                split_hi(jp + 2)
            lru_y_hi(LRU_TILES - 1)

            def head_input(h, m):
                zi = 8 + 4 * h + m
                dst, fn = ((hf, ACT.Sigmoid), (hq, ACT.Copy), (hv, ACT.Copy), (hg, ACT.Silu))[m]
                if h == 1:
                    act.wait_ge(s("ycat_lo"), LRU_TILES)
                if h >= 2:
                    act.wait_ge(s("head_y"), h - 1)
                    act.wait_ge(s("ycat_lo"), LRU_TILES + h - 1 if m == 3 else LRU_TILES)
                act.wait_ge(s("z"), zi + 1)
                b = 2 * (zi % 2)
                sc_.activation(dst[h % 2][:].rearrange("p (a t) -> p a t", a=2), ps[:, b:b + 2, 0:HALF],
                               fn).then_inc(s("z_free"), 1)

            def head_y_hi(h):
                act.wait_ge(s("head_y"), h + 1)
                sc_.activation(yt_hi[:, LRU_TILES + h, :], hg[h % 2][:], ACT.Copy).then_inc(s("ycat_hi"), 1)

            act.wait_ge(s("pc"), 36)
            for m in range(4):
                head_input(0, m)
            for h in range(HEADS):
                if h:
                    act.wait_ge(s("vmask"), 5 * h)
                    act.wait_ge(s("o_done"), 5 * h)
                for k, dst in enumerate((vtok, ktok)):
                    act.wait_ge(s("hg_T"), 2 * h + 1 + k)
                    sc_.activation(dst[:, 0:4, :], ps[:, 4, :].rearrange("p (a t) -> p a t", a=4),
                                   ACT.Copy).then_inc(s("hg_tok"), 1)
                    sc_.activation(dst[0:64, 4, :], ps[0:64, 5, 0:P], ACT.Copy).then_inc(s("hg_tok"), 1)
                if h:
                    head_y_hi(h - 1)
                split_hi(4 + h)
                for tt, (t0, n) in enumerate(HTILES):
                    if h + 1 < HEADS and tt < 2:
                        head_input(h + 1, tt)
                    act.wait_ge(s("o_done"), 5 * h + tt + 1)
                    sc_.activation(ho[h % 2][:, t0:t0 + n], ps[:, 4, 0:n], ACT.Copy).then_inc(s("ho"), 1)
                act.wait_ge(s("ho"), 5 * (h + 1))
                sc_.activation(hv[h % 2][:], ho[h % 2][:], ACT.Square).then_inc(s("hsq"), 1)
                act.wait_ge(s("rms"), h + 1)
                sc_.activation(hr[h % 2][:].rearrange("p (a t) -> p a t", a=2), ps[:, 6:8, 0:HALF], ACT.Sqrt,
                               bias=eps[:, 0:1], scale=1.0 / P).then_inc(s("hrs"), 1)
                if h + 1 < HEADS:
                    head_input(h + 1, 2)
                    head_input(h + 1, 3)
            head_y_hi(HEADS - 1)
            ln_act(act, "mix0")
            route_act(act, 0)
            experts_act(act, 0)
            ln_act(act, "ffn0")
            s5_act(act)
            route_act(act, 1)
            experts_act(act, 1)
            ln_act(act, "ffn1")

        @block.vector
        def _(dve):
            v = nc.vector
            n_link = [0]

            def link(ins):
                n_link[0] += 1
                ins.then_inc(s("dve_chain"), 1)
                dve.wait_ge(s("dve_chain"), n_link[0])

            def split_lo(c):
                dve.wait_ge(s("hi_done"), c + 1)
                v.tensor_tensor(wlo[c % 2][:], raw[c % 2][:], whi[c % 2][:].bitcast(F32),
                                ALU.subtract).then_inc(s("lo_done"), 1)

            for i, (t0, n) in enumerate(TILES):
                for hf_ in range(2):
                    b = 2 * (i % 2) + hf_
                    dve.wait_ge(s("xt_hi"), 2 * i + hf_ + 1)
                    ins = v.tensor_tensor(ft_lo[:, 4 * hf_:4 * hf_ + 4, t0:t0 + n],
                                          ps[:, b, :].rearrange("p (k t) -> p k t", t=P)[:, :, 0:n],
                                          ft_hi[:, 4 * hf_:4 * hf_ + 4, t0:t0 + n].bitcast(F32), ALU.subtract)
                ins.then_inc(s("x_split"), 1)
            split_lo(0)
            dve.wait_ge(s("params"), 16 * len(param_dmas))
            link(v.tensor_scalar(sp[:, 2, :], lam[:], -1.0, None, ALU.mult))
            link(v.tensor_tensor(sp[:, 0, :], sp[:, 2, :], lam[:], ALU.max))
            link(v.tensor_tensor(lbs[:, 2, :], lbl[:, 0, :], lbl[:, 1, :], ALU.max))
            link(v.tensor_tensor(lbs[:, 3, :], lbl[:, 1, :], lbs[:, 2, :], ALU.subtract))
            link(v.tensor_tensor(lbs[:, 2, :], lbl[:, 0, :], lbs[:, 2, :], ALU.subtract))
            v.tensor_scalar(sp[:, 2, :], sp[:, 2, :], 0.0, None, ALU.max).then_inc(s("prep"), 1)
            split_lo(1)
            dve.wait_ge(s("prep_a"), 2)
            link(v.tensor_scalar(sp[:, 3, :], sp[:, 1, :], 2.0, None, ALU.add))
            link(v.reciprocal(sp[:, 4, :], sp[:, 3, :]))
            link(v.tensor_tensor(sp[:, 3, :], sp[:, 1, :], sp[:, 4, :], ALU.mult))
            link(v.tensor_tensor(sp[:, 4, :], sp[:, 3, :], sp[:, 3, :], ALU.mult))
            link(v.tensor_scalar(sp[:, 1, :], sp[:, 4, :], 1.0 / 15, 1.0 / 13, ALU.mult, ALU.add))
            for q in (11, 9, 7, 5, 3, 1):
                link(v.tensor_tensor(sp[:, 1, :], sp[:, 1, :], sp[:, 4, :], ALU.mult))
                link(v.tensor_scalar(sp[:, 1, :], sp[:, 1, :], 1.0 / q, None, ALU.add))
            link(v.tensor_tensor(sp[:, 1, :], sp[:, 1, :], sp[:, 3, :], ALU.mult))
            link(v.scalar_tensor_tensor(out=sp[:, 1, :], in0=sp[:, 1, :], scalar=2.0, in1=sp[:, 2, :],
                                        op0=ALU.mult, op1=ALU.add))
            v.tensor_scalar(spl4[:], sp[:, 1, :], 4.0, None, ALU.mult).then_inc(s("spl"), 1)
            link(v.tensor_tensor(lbs[:, 2, :], lbs[:, 0, :], lbs[:, 1, :], ALU.add))
            link(v.reciprocal(lbs[:, 3, :], lbs[:, 2, :]))
            link(v.tensor_tensor(lb[:], lbs[:, 0, :], lbs[:, 3, :], ALU.mult))
            link(v.tensor_scalar(omlb[:], lb[:], -1.0, 1.0, ALU.mult, ALU.add))
            link(v.tensor_scalar(nomlb[:], omlb[:], -1.0, None, ALU.mult))

            def conv(j):
                x, u = zx[j % 2], lu[j % 2]
                dve.wait_ge(s("z_free"), 4 * (j // 2) + j % 2 + 1)
                if j >= 2:
                    dve.wait_ge(s("ri"), j - 1)
                v.tensor_copy(convst[:, 0, :, j], x[:, T_PROMPT:T_PROMPT + 3]).then_inc(s("lru_st"), 1)
                v.tensor_copy(convst[:, 1, :, j], x[:, S0_AT + T_SAMPLE:S0_AT + T_SAMPLE + 3]).then_inc(s("lru_st"), 1)
                link(v.tensor_scalar(u[:], x[:, 0:LRU_U], convw[:, j, 0:1], convb[:, j:j + 1], ALU.mult, ALU.add))
                for k in range(1, CONV):
                    ins = v.scalar_tensor_tensor(out=u[:], in0=x[:, k:k + LRU_U], scalar=convw[:, j, k:k + 1],
                                                 in1=u[:], op0=ALU.mult, op1=ALU.add)
                    if k < CONV - 1:
                        link(ins)
                ins.then_inc(s("u_done"), 1)

            def recur(j):
                dve.wait_ge(s("u_done"), j + 1)
                dve.wait_ge(s("lru_act"), 4 * j + 3)
                if j:
                    dve.wait_ge(s("ycat_lo"), j)
                link(v.tensor_scalar(ld[:], lt[:], 1.0, None, ALU.add))
                link(v.reciprocal(ld[:], ld[:]))
                v.tensor_scalar(la[:], ld[:], 2.0, -1.0, ALU.mult, ALU.add).then_inc(s("la"), 1)
                dve.wait_ge(s("lru_act"), 4 * j + 4)
                link(v.scalar_tensor_tensor(out=lq[:], in0=lq[:], scalar=2.0, in1=ld[:], op0=ALU.mult, op1=ALU.mult))
                link(v.tensor_tensor(lq[:], lq[:], li[:], ALU.mult))
                link(v.tensor_tensor(lq[:], lq[:], lu[j % 2][:], ALU.mult))
                dve.wait_ge(s("la"), j + 1)
                v.tensor_tensor_scan(lr[:, 0:T_PROMPT], la[:, 0:T_PROMPT], lq[:, 0:T_PROMPT], 0.0,
                                     ALU.mult, ALU.add).then_inc(s("scan"), 1)
                v.tensor_tensor_scan(lr[:, S0_AT:S0_AT + T_SAMPLE], la[:, S0_AT:S0_AT + T_SAMPLE],
                                     lq[:, S0_AT:S0_AT + T_SAMPLE], h0[:, j:j + 1], ALU.mult, ALU.add).then_inc(s("scan"), 1)
                dve.wait_ge(s("scan"), 2 * (j + 1))
                v.tensor_copy(hst[:, 0, j:j + 1], lr[:, T_PROMPT - 1:T_PROMPT]).then_inc(s("lru_st"), 1)
                v.tensor_copy(hst[:, 1, j:j + 1], lr[:, S0_AT + T_SAMPLE - 1:S0_AT + T_SAMPLE]).then_inc(s("lru_st"), 1)
                dve.wait_ge(s("z_free"), 4 * (j // 2) + 3 + j % 2)
                v.tensor_tensor(ld[:, 0:T_PROMPT], lr[:, 0:T_PROMPT], gz[j % 2][:, 0:T_PROMPT], ALU.mult)
                v.tensor_tensor(ld[:, T_PROMPT:T], lr[:, S0_AT:S0_AT + T_SAMPLE], gz[j % 2][:, T_PROMPT:T],
                                ALU.mult).then_inc(s("lru_y"), 1)
                dve.wait_ge(s("ycat_hi"), j + 1)
                v.tensor_tensor(yt_lo[:, j, :], ld[:, 0:T], yt_hi[:, j, :].bitcast(F32),
                                ALU.subtract).then_inc(s("ycat_lo"), 1)

            dve.wait_ge(s("params"), 16 * len(param_dmas))
            for jp in range(LRU_TILES // 2):
                conv(2 * jp)
                conv(2 * jp + 1)
                recur(2 * jp)
                recur(2 * jp + 1)
                split_lo(2 + jp)
            n_state = 0
            dve.wait_ge(s("pc"), 36)
            dve.wait_ge(s("xg_zero"), 16 * 4)
            dve.wait_ge(s("ycat_lo"), LRU_TILES)
            blocks = lambda x: x.rearrange("p (b i) -> p b i", i=BLK)

            def decays(h):
                zbase = 8 + 4 * h
                f_, q_ = hf[h % 2], hq[h % 2]
                dve.wait_ge(s("z_free"), zbase + 1)
                v.tensor_scalar(hk[:], f_[:], nomlb[:, h:h + 1], omlb[:, h:h + 1], ALU.mult, ALU.add).then_inc(s("hg_dve"), 1)
                dve.wait_ge(s("hg_dve"), 4 * h + 1)
                if h:
                    dve.wait_ge(s("o_done"), 5 * h)
                link(v.tensor_scalar(f_[:], f_[:], omlb[:, h:h + 1], lb[:, h:h + 1], ALU.mult, ALU.add))
                m0b = m0[:].rearrange("p (x i) -> p x i", x=1).to_broadcast([P, NBLK, BLK])
                link(v.tensor_tensor(blocks(ha[:]), blocks(f_[:]), m0b, ALU.mult))
                link(v.tensor_tensor(hb[:], f_[:], ha[:], ALU.subtract))
                link(v.tensor_tensor_scan(hp[:], ha[:], hb[:], 0.0, ALU.mult, ALU.add))
                link(v.reciprocal(f_[:], hp[:]))
                dve.wait_ge(s("z_free"), zbase + 2)
                v.tensor_tensor(ha[:], q_[:], hp[:], ALU.mult).then_inc(s("hg_dve"), 1)
                v.tensor_tensor(hb[:], hk[:], f_[:], ALU.mult).then_inc(s("hg_dve"), 1)
                dve.wait_ge(s("hg_dve"), 4 * h + 3)
                last = blocks(hp[:])[:, :, BLK - 1:BLK].to_broadcast([P, NBLK, BLK])
                v.tensor_tensor(blocks(q_[:]), blocks(hb[:]), last, ALU.mult).then_inc(s("hg_dve"), 1)

            def head_end(h):
                r_, o_, g_ = hr[h % 2], ho[h % 2], hg[h % 2]
                dve.wait_ge(s("hrs"), h + 1)
                link(v.reciprocal(r_[:], r_[:]))
                link(v.scalar_tensor_tensor(out=o_[:], in0=o_[:], scalar=hg_g[:, h:h + 1], in1=r_[:],
                                            op0=ALU.mult, op1=ALU.mult))
                v.tensor_tensor(g_[:], o_[:], g_[:], ALU.mult).then_inc(s("head_y"), 1)

            def head_y_lo(h):
                dve.wait_ge(s("ycat_hi"), LRU_TILES + h + 1)
                v.tensor_tensor(yt_lo[:, LRU_TILES + h, :], hg[h % 2][:], yt_hi[:, LRU_TILES + h, :].bitcast(F32),
                                ALU.subtract).then_inc(s("ycat_lo"), 1)

            decays(0)
            for h in range(HEADS):
                if h:
                    dve.wait_ge(s("st_out"), 32 * h)
                link(v.memset(srn[:, 0, :], 0.0))
                for tt, (t0, n) in enumerate(HTILES):
                    i = 5 * h + tt
                    if i:
                        dve.wait_ge(s("o_done"), i)
                    if tt == 4:
                        dve.wait_ge(s("st_in"), 16 * (h + 1))
                    for b in range(n // BLK):
                        g_ = t0 // BLK + b
                        k = g_ + (tt == 4)
                        if b % 4 == 0:
                            dve.wait_ge(s("uinc"), 9 * h + 2 * tt + b // 4 + 1)
                        if n_state:
                            dve.wait_ge(s("state"), n_state)
                        v.scalar_tensor_tensor(out=srn[:, (k + 1) % SRING, :],
                                               in0=s_in[:] if g_ == NBLK_P else srn[:, k % SRING, :],
                                               scalar=hp[:, BLK * g_ + BLK - 1:BLK * g_ + BLK],
                                               in1=ps[:, 6 + b // 4, P * (b % 4):P * (b % 4) + P],
                                               op0=ALU.mult, op1=ALU.add).then_inc(s("state"), 1)
                        n_state += 1
                        if b == 3:
                            dve.wait_ge(s("score"), i + 1)
                            v.tensor_tensor(sc[0:n, 0:n], ps[0:n, 5, 0:n], causal[0:n, 0:n], ALU.mult).then_inc(s("scm"), 1)
                    if tt == 0:
                        if h:
                            head_y_lo(h - 1)
                        split_lo(4 + h)
                if h + 1 < HEADS:
                    decays(h + 1)
                head_end(h)
            head_y_lo(HEADS - 1)
            dve.wait_ge(s("res_landed"), 16 * (NT + 1))
            for i, (t0, n) in enumerate(TILES):
                dve.wait_ge(s("y"), i + 1)
                x = xtok[0:n, i, :]
                b = 2 * (i % 2)
                v.scalar_tensor_tensor(out=x.rearrange("p (a c) -> p a c", a=2),
                                       in0=x.rearrange("p (a c) -> p a c", a=2), scalar=ALPHA,
                                       in1=ps[0:n, b:b + 2, :], op0=ALU.mult, op1=ALU.add).then_inc(s("mix0_sum"), 1)
                dve.wait_ge(s("mix0_sum"), i + 1)
                ln_dve(dve, link, "mix0", i)
            route_dve(dve, link, 0)
            experts_dve(dve, 0)
            combine_dve(dve, link, 0)
            s5_dve(dve, link, split_lo)
            route_dve(dve, link, 1)
            experts_dve(dve, 1)
            combine_dve(dve, link, 1)

        @block.tensor
        def _(pe):
            te = nc.tensor
            pe.wait_ge(s("pc"), 2)
            for i, (t0, n) in enumerate(TILES):
                pe.wait_ge(s(f"x_landed{x_group[i]}"), x_loads[x_group[i]])
                if i >= 2:
                    pe.wait_ge(s("x_split"), i - 1)
                for k in range(KT):
                    b = 2 * (i % 2) + k // 4
                    ins = te.transpose(ps[:, b, P * (k % 4):P * (k % 4) + n], xin[i][0:n, P * k:P * k + P],
                                       ident[0:n, 0:n])
                    if k % 4 == 3:
                        ins.then_inc(s("xt"), 1)

            def mm3(out, l_hi, l_lo, r_hi, r_lo, first, last):
                te.matmul(out, l_lo, r_hi, start=first, stop=False)
                te.matmul(out, l_hi, r_lo, start=False, stop=False)
                return te.matmul(out, l_hi, r_hi, start=False, stop=last)

            zi = 0

            def z_tile(c, m):
                nonlocal zi
                if m == 0:
                    pe.wait_ge(s("lo_done"), c + 1)
                if c == 0 and m == 0:
                    pe.wait_ge(s("x_split"), NT)
                if zi >= 2:
                    pe.wait_ge(s("z_free"), zi - 1)
                whc = whi[c % 2][:].rearrange("p (k n) -> p k n", n=512)
                wlc = wlo[c % 2][:].rearrange("p (k n) -> p k n", n=512)
                for half in range(2):
                    for k in range(KT):
                        cols = slice(P * m, P * m + P)
                        tk = slice(HALF * half, HALF * half + HALF)
                        ins = mm3(ps[:, 2 * (zi % 2) + half, 0:HALF], whc[:, k, cols], wlc[:, k, cols],
                                  ft_hi[:, k, tk], ft_lo[:, k, tk], k == 0, k == KT - 1)
                ins.then_inc(s("z"), 1)
                zi += 1

            def lru_gates(j):
                pe.wait_ge(s("wri"), 16 * 4)
                pe.wait_ge(s("u_done"), j + 1)
                if j:
                    pe.wait_ge(s("lru_act"), 4 * j - 2)
                h2 = LRU_U // 2
                for w, b in ((wr, 4), (wi, 6)):
                    for half in range(2):
                        ins = te.matmul(ps[:, b + half, 0:h2], w[:, j, :], lu[j % 2][:, h2 * half:h2 * half + h2],
                                        start=True, stop=True)
                ins.then_inc(s("ri"), 1)

            for jp in range(LRU_TILES // 2):
                z_tile(jp, 0)
                z_tile(jp, 1)
                lru_gates(2 * jp)
                z_tile(jp, 2)
                lru_gates(2 * jp + 1)
                z_tile(jp, 3)
            for m in range(4):
                z_tile(2, m)
            pe.wait_ge(s("pc"), 36)
            for h in range(HEADS):
                if h == 0:
                    pe.wait_ge(s("lru_act"), 4 * LRU_TILES - 2)
                else:
                    pe.wait_ge(s("ho"), 5 * h)
                    pe.wait_ge(s("hrs"), h)
                    pe.wait_ge(s("scm"), 5 * h)
                pe.wait_ge(s("z_free"), 8 + 4 * h + 3)
                for src, nm in ((hv[h % 2], "vT"), (hq[h % 2], "kT")):
                    if nm == "kT":
                        pe.wait_ge(s("hg_dve"), 4 * h + 4)
                        pe.wait_ge(s("hg_tok"), 4 * h + 2)
                    for tt, (t0, n) in enumerate(HTILES):
                        out = ps[0:n, 4, P * tt:P * tt + P] if tt < 4 else ps[0:n, 5, 0:P]
                        ins = te.transpose(out, src[:, t0:t0 + n], ident[:])
                    ins.then_inc(s("hg_T"), 1)
                pe.wait_ge(s("hg_tok"), 4 * h + 4)

                def score(tt):
                    t0, n = HTILES[tt]
                    if 5 * h + tt:
                        pe.wait_ge(s("scm"), 5 * h + tt)
                    te.matmul(ps[0:n, 5, 0:n], hb[:, t0:t0 + n], ha[:, t0:t0 + n], start=True,
                              stop=True).then_inc(s("score"), 1)

                def increments(tt, u):
                    n = HTILES[tt][1]
                    pe.wait_ge(s("vmask"), 5 * h + tt + 1)
                    if h or tt:
                        pe.wait_ge(s("state"), NBLK * h + (8 * (tt - 1) + 4 * (u + 1) if tt else 0))
                    te.matmul(ps[:, 6 + u, :], ktok[0:n, tt, :], vmask[0:n, 4 * u:4 * u + 4, :].rearrange("p b d -> p (b d)"),
                              start=True, stop=True).then_inc(s("uinc"), 1)

                score(0)
                increments(0, 0)
                increments(0, 1)
                for tt, (t0, n) in enumerate(HTILES):
                    i = 5 * h + tt
                    if h + 1 < HEADS and tt < 2:
                        z_tile(3 + h, tt)
                    pe.wait_ge(s("scm"), i + 1)
                    if i:
                        pe.wait_ge(s("ho"), i)
                    te.matmul(ps[:, 4, 0:n], vtok[0:n, tt, :], sc[0:n, 0:n], start=True, stop=False)
                    nb = n // BLK
                    for b in range(nb):
                        g_ = t0 // BLK + b
                        k = g_ + (tt == 4)
                        if b == 4 and tt < 4:
                            increments(tt + 1, 0)
                        if g_ == NBLK_P:
                            pe.wait_ge(s("st_in"), 16 * (h + 1))
                        elif g_:
                            pe.wait_ge(s("state"), NBLK * h + g_)
                        ins = te.matmul(ps[:, 4, BLK * b:BLK * b + BLK], s_in[:] if g_ == NBLK_P else srn[:, k % SRING, :],
                                        ha[:, BLK * g_:BLK * g_ + BLK], start=False, stop=(b == nb - 1))
                    ins.then_inc(s("o_done"), 1)
                    if tt < 4:
                        score(tt + 1)
                        if HTILES[tt + 1][1] == P:
                            increments(tt + 1, 1)
                pe.wait_ge(s("hsq"), h + 1)
                pe.wait_ge(s("state"), NBLK * (h + 1))
                for half in range(2):
                    ins = te.matmul(ps[:, 6 + half, 0:HALF], ones[:], hv[h % 2][:, HALF * half:HALF * half + HALF],
                                    start=True, stop=True)
                ins.then_inc(s("rms"), 1)
                if h + 1 < HEADS:
                    z_tile(3 + h, 2)
                    z_tile(3 + h, 3)
            pe.wait_ge(s("ycat_lo"), KT)
            pe.wait_ge(s("lo_done"), 8)
            pe.wait_ge(s("z_free"), 24)
            for i, (t0, n) in enumerate(TILES):
                if i >= 2:
                    pe.wait_ge(s("mix0_sum"), i - 1)
                for half in range(2):
                    wh = whi[half][:].rearrange("p (k n) -> p k n", n=512)
                    wl = wlo[half][:].rearrange("p (k n) -> p k n", n=512)
                    for k in range(KT):
                        ins = mm3(ps[0:n, 2 * (i % 2) + half, :], yt_hi[:, k, t0:t0 + n], yt_lo[:, k, t0:t0 + n],
                                  wh[:, k, :], wl[:, k, :], k == 0, k == KT - 1)
                ins.then_inc(s("y"), 1)
            route_pe(pe, 0)
            experts_pe(pe, mm3, 0)
            s5_pe(pe, mm3)
            route_pe(pe, 1)
            experts_pe(pe, mm3, 1)


_OUTS = {
    "y_prompt": (1, 512, 1024), "y_sample": (1, 64, 1024),
    "p_lru_h": (1, 1, 512), "p_lru_conv": (1, 1, 3, 512), "p_hgrn2": (1, 1, 4, 128, 128),
    "p_s5_re": (1, 1, 64, 64), "p_s5_im": (1, 1, 64, 64),
    "s_lru_h": (1, 1, 512), "s_lru_conv": (1, 1, 3, 512), "s_hgrn2": (1, 1, 4, 128, 128),
    "s_s5_re": (1, 1, 64, 64), "s_s5_im": (1, 1, 64, 64),
}


def kernel(**inputs):
    import numpy as _np
    import concourse.bacc as _bacc
    from concourse.bass_utils import run_bass_kernel_spmd as _run

    nc = _bacc.Bacc("TRN2", target_bir_lowering=False, num_devices=1)
    arrays, ins, outs = {}, {}, {}
    for name, value in inputs.items():
        value = _np.ascontiguousarray(value)
        arrays[f"in_{name}"] = value
        ins[name] = nc.dram_tensor(f"in_{name}", value.shape, mybir.dt.from_np(value.dtype), kind="ExternalInput").ap()
    for name, shape in _OUTS.items():
        outs[name] = nc.dram_tensor(f"out_{name}", shape, F32, kind="ExternalOutput").ap()
    stream_kernel(nc, ins, outs)
    r = _run(nc, [arrays], core_ids=[0])
    return tuple(r.results[0][f"out_{name}"] for name in _OUTS)
```

```python
import concourse.bass as bass
from concourse import mybir
from contextlib import ExitStack

F32 = mybir.dt.float32
F32R = mybir.dt.float32r
I32 = mybir.dt.int32
U32 = mybir.dt.uint32
ALU = mybir.AluOpType
ACT = mybir.ActivationFunctionType
AX_X = mybir.AxisListType.X

P = 128
D = 1024
KT = D // P
T_PROMPT, T_SAMPLE = 512, 64
T = T_PROMPT + T_SAMPLE
TT = 120
TILES = [(t, min(TT, T - t)) for t in range(0, T, TT)]
NT = len(TILES)
HALF = T // 2
LRU = 512
LRU_TILES = LRU // P
CONV = 4
LRU_W = T + 2 * (CONV - 1) + 1
LRU_U = LRU_W - (CONV - 1)
S0_AT = T_PROMPT + CONV - 1
HEADS = 4
BLK = 16
NBLK_P, NBLK_S = T_PROMPT // BLK, T_SAMPLE // BLK
NBLK = NBLK_P + NBLK_S
SRING = 9
HTILES = [(t, min(P, T - t)) for t in range(0, T, P)]
ALPHA = 4.0 ** 0.25
LN_EPS = 1e-5
RMS_EPS = 1e-6
E = 16
GROUPS, PER_GROUP = 4, 4
F_EXP = 512
CAP = 96
ROUNDS_MAX = -(-T // CAP)
SLOTS = E * CAP
DUMP = SLOTS

CHUNK = 4096
SB0 = 16512
RAW_AT = [SB0, SB0 + 16384]
SPL_AT = [SB0 + 32768, SB0 + 65536]
FT_AT = SB0 + 98304
YT_AT = FT_AT + 2 * KT * T * 4
XTOK_AT = YT_AT + 2 * KT * T * 4
TEMP_AT = XTOK_AT + NT * D * 4
SB_END = 229344


def stream_kernel(nc, a, o):
    with ExitStack() as ctx:
        taken = [TEMP_AT]

        def at(name, shape, offset, dt=F32):
            return nc.alloc_sbuf_tensor_at(name, shape, dt, offset=offset)

        def small(name, cols, dt=F32, parts=P):
            t = at(name, [parts] + (cols if isinstance(cols, list) else [cols]), taken[0], dt)
            n = 4
            for c in (cols if isinstance(cols, list) else [cols]):
                n *= c
            taken[0] += -(-n // 32) * 32
            assert taken[0] <= SB_END, name
            return t

        def sem(name):
            return ctx.enter_context(nc.semaphore(name))

        ps = ctx.enter_context(nc.psum_tensor("ps", [P, 8, 512], F32))

        raw = [at(f"raw{i}", [P, CHUNK], RAW_AT[i]) for i in range(2)]
        whi = [at(f"whi{i}", [P, CHUNK], SPL_AT[i], F32R) for i in range(2)]
        wlo = [at(f"wlo{i}", [P, CHUNK], SPL_AT[i] + 4 * CHUNK, F32R) for i in range(2)]
        ft_hi = at("ft_hi", [P, KT, T], FT_AT, F32R)
        ft_lo = at("ft_lo", [P, KT, T], FT_AT + 4 * KT * T, F32R)
        yt_hi = at("yt_hi", [P, KT, T], YT_AT, F32R)
        yt_lo = at("yt_lo", [P, KT, T], YT_AT + 4 * KT * T, F32R)
        xtok = at("xtok", [P, NT, D], XTOK_AT)

        ident = small("ident", P)
        ones = small("ones", P)
        lstrict = small("lstrict", P)
        wt4 = small("wt4", PER_GROUP)
        e128 = small("e128", E)
        eps = small("eps", 2)
        lnst = small("lnst", [2, 2, 6])
        lnmv = small("lnmv", [2, 4])
        gate = small("gate", [2, NT])
        slot = small("slot", [2, NT], U32)
        nstep = small("nstep", 1, I32)
        round_mark = small("round_mark", 1)
        shared_end = taken[0]
        causal = small("causal", P)
        blkmask = small("blkmask", 8)
        m0 = small("m0", BLK)
        convw = small("convw", [LRU_TILES, CONV])
        convb = small("convb", LRU_TILES)
        b_r = small("b_r", LRU_TILES)
        b_i = small("b_i", LRU_TILES)
        lam = small("lam", LRU_TILES)
        h0 = small("h0", LRU_TILES)
        spl4 = small("spl4", LRU_TILES)
        sp = small("sp", [6, LRU_TILES])
        lbl = small("lbl", [2, HEADS])
        lbs = small("lbs", [4, HEADS])
        lb = small("lb", HEADS)
        omlb = small("omlb", HEADS)
        nomlb = small("nomlb", HEADS)
        hg_g = small("hg_g", HEADS)
        past = small("past", [CONV - 1, LRU_TILES])
        convst = small("convst", [2, CONV - 1, LRU_TILES])
        hst = small("hst", [2, LRU_TILES])
        consts_end = taken[0]

        l0_at = [consts_end]
        l0b_at = [XTOK_AT]

        def l0(name, cols, low=False):
            cols = cols if isinstance(cols, list) else [cols]
            n = 4
            for c in cols:
                n *= c
            n = -(-n // 32) * 32
            where = l0b_at if low else l0_at
            t = at(name, [P] + cols, where[0])
            where[0] += n
            assert where[0] <= (TEMP_AT if low else SB_END), name
            return t

        zx = [l0(f"zx{i}", LRU_W, True) for i in range(2)]
        gz = [l0(f"gz{i}", T, True) for i in range(2)]
        lr = l0("lr", LRU_U, True)
        li = l0("li", LRU_U, True)
        lt = l0("lt", LRU_U, True)
        ld = l0("ld", LRU_U, True)
        lu = [l0(f"lu{i}", LRU_U) for i in range(2)]
        la = l0("la", LRU_U)
        lq = l0("lq", LRU_U)
        l0_at_lru_end = l0_at[0]
        xin = [at(f"xin{i}", [P, D], YT_AT + 4 * D * i) for i in range(NT)]
        SLOT = 4 * T
        gate_w_at = YT_AT + 4 * KT * T + 4 * SLOT
        wr = at("wr", [P, LRU_TILES, P], gate_w_at)
        wi = at("wi", [P, LRU_TILES, P], gate_w_at + 4 * LRU_TILES * P)
        assert 8 * LRU_TILES * P <= 2 * SLOT
        l0_at[0], l0b_at[0] = consts_end, XTOK_AT
        in_yt = [YT_AT + (KT - 2) * SLOT, YT_AT + (2 * KT - 2) * SLOT, YT_AT + (KT - 1) * SLOT, YT_AT + (2 * KT - 1) * SLOT]
        hf, hq, hv, hg = ([at(f"{nm}0", [P, T], in_yt[i]), l0(f"{nm}1", T, True)]
                          for i, nm in enumerate(("hf", "hq", "hv", "hg")))
        hk = l0("hk", T, True)
        ha = l0("ha", T, True)
        hb = l0("hb", T, True)
        hp = l0("hp", T, True)
        vtok = l0("vtok", [5, P])
        ktok = l0("ktok", [5, P])
        srn = l0("srn", [SRING, P])
        vmask = l0("vmask", [8, P])
        sc = l0("sc", P)
        s_in = l0("s_in", P)
        ho = hq
        hr = hf
        zeros = at("zeros", [P, D], SB_END - 4 * D)
        assert l0_at_lru_end <= SB_END - 4 * D

        taken[0] = shared_end
        lng = small("lng", D)
        lnb = small("lnb", D)
        x1t = small("x1t", [KT, TT])
        rw = small("rw", [KT, E])
        rb = small("rb", E)
        R = {n: small("r_" + n, [NT, E]) for n in ("l", "p", "m1", "m2", "w", "x", "s1")}
        Rg = {n: small("rg_" + n, [NT, GROUPS]) for n in ("a", "b", "c", "d", "e", "f", "g")}
        Rt = {n: small("rt_" + n, NT) for n in ("mx", "z", "p1", "p2")}
        nrow = small("nrow", 4)

        taken[0] = shared_end
        xe = small("xe", D)
        xet_hi = small("xet_hi", [KT, P], F32R)
        xet_lo = small("xet_lo", [KT, P], F32R)
        hx = at("hx", [P, F_EXP], YT_AT + 8 * CHUNK)
        ht_hi = small("ht_hi", [4, P], F32R)
        ht_lo = small("ht_lo", [4, P], F32R)
        raw.append(at("raw2", [P, CHUNK], YT_AT))
        whi.append(at("whi2", [P, CHUNK], FT_AT, F32R))
        wlo.append(at("wlo2", [P, CHUNK], FT_AT + 4 * CHUNK, F32R))
        ysb = at("ysb", [P, D], FT_AT + 8 * CHUNK)
        ygat = [[at(f"ygat{i}{k}", [P, D], YT_AT + 4 * D * (2 * i + k)) for k in range(2)] for i in range(4)]

        xg = nc.dram_tensor("xg", (ROUNDS_MAX * SLOTS, D), F32, kind="Internal").ap()
        yg = nc.dram_tensor("yg", (ROUNDS_MAX * SLOTS, D), F32, kind="Internal").ap()

        S = {}

        def s(name):
            if name not in S:
                S[name] = sem(name)
            return S[name]

        w_in = a["w_in_ab"][0].rearrange("(k p) n -> p k n", p=P)
        w_out = a["w_out_ab"][0].rearrange("(k p) n -> p k n", p=P)

        chunks0 = []
        for jp in range(LRU_TILES // 2):
            chunks0.append([(w_in[:, :, LRU + 256 * jp:LRU + 256 * jp + 256], 0, 256),
                            (w_in[:, :, 256 * jp:256 * jp + 256], 256, 256)])
        Q_AT, F_AT, V_AT, G_AT = (2 * LRU + 512 * i for i in range(4))
        for h in range(HEADS):
            chunks0.append([(w_in[:, :, b + P * h:b + P * h + P], P * i, P)
                            for i, b in enumerate((F_AT, Q_AT, V_AT, G_AT))])
        for n in range(2):
            chunks0.append([(w_out[:, :, 512 * n:512 * n + 512], 0, 512)])
        n_in = 6
        landed = {}
        count = [0, 0]
        for c, pieces in enumerate(chunks0):
            count[c % 2] += 16 * len(pieces)
            landed[c] = count[c % 2]
        param_dmas = [
            *[(convw[:, :, k], a["lru_conv_w"][0, k].rearrange("(j p) -> p j", p=P)) for k in range(CONV)],
            (convb[:], a["lru_conv_b"][0].rearrange("(j p) -> p j", p=P)),
            (b_r[:], a["lru_b_r"][0].rearrange("(j p) -> p j", p=P)),
            (b_i[:], a["lru_b_i"][0].rearrange("(j p) -> p j", p=P)),
            (lam[:], a["lru_lam"][0].rearrange("(j p) -> p j", p=P)),
            (h0[:], a["state_lru_h"][0, 0].rearrange("(j p) -> p j", p=P)),
            *[(lbl[:, r], a["hgrn_lb_logits"][r].rearrange("(j p) -> p j", p=P)) for r in range(2)],
            (hg_g[:], a["hgrn_norm_g"][0].rearrange("(j p) -> p j", p=P)),
            *[(past[:, k], a["state_lru_conv"][0, 0, k].rearrange("(j p) -> p j", p=P)) for k in range(CONV - 1)],
        ]

        def x_rows(t0, n):
            xp, xs = a["x_prompt"][0], a["x_sample"][0]
            if t0 + n <= T_PROMPT:
                return [(0, n, xp[t0:t0 + n])]
            m = T_PROMPT - t0
            return [(0, m, xp[t0:T_PROMPT]), (m, n - m, xs[0:n - m])]

        x_group = [0, 1, 1, 2, 2]
        x_loads = [16, 32, 16 * 3]

        ln_no = {"mix0": 0, "ffn0": 1, "mix1": 2, "ffn1": 3}

        ln_sd_base = {"mix0": 0, "ffn0": NT, "mix1": 3 * NT, "ffn1": 4 * NT}

        def ln_gains_pool(pool, tag):
            ln, l = tag[:3], int(tag[3])
            for dst, src in ((lng, a[f"ln_{ln}_g"]), (lnb, a[f"ln_{ln}_b"])):
                pool.dma_start(dst[:], src[l:l + 1, :].to_broadcast([P, D])).then_inc(s("ln_gains"), 16)

        def ln_act(act, tag, tiles=range(NT)):
            for i in tiles:
                n = TILES[i][1]
                act.wait_ge(s("ln_mv"), NT * ln_no[tag] + i + 1)
                nc.scalar.activation(lnmv[0:n, i % 2, 2:3], lnmv[0:n, i % 2, 1:2], ACT.Sqrt,
                                     bias=eps[0:n, 1:2]).then_inc(s("ln_sd"), 1)

        def ln_stats(dve, link, tag, i):
            v, n = nc.vector, TILES[i][1]
            x, st, mv = xtok[0:n, i, :], lnst[0:n, i % 2], lnmv[0:n, i % 2]
            v.bn_stats(st[:, 0, :], x[:, 0:512])
            link(v.bn_stats(st[:, 1, :], x[:, 512:D]))
            v.bn_aggr(mv[:, 0:2], st).then_inc(s("ln_mv"), 1)

        def ln_root(dve, link, tag, i):
            mv = lnmv[0:TILES[i][1], i % 2]
            dve.wait_ge(s("ln_sd"), ln_sd_base[tag] + (1 if tag[:3] == "mix" else 2) * i + 1)
            link(nc.vector.reciprocal(mv[:, 3:4], mv[:, 2:3]))

        def ln_dve(dve, link, tag, i):
            v, n = nc.vector, TILES[i][1]
            x, mv = xtok[0:n, i, :], lnmv[0:n, i % 2]
            ln_stats(dve, link, tag, i)
            ln_root(dve, link, tag, i)
            link(v.tensor_scalar(x, x, mv[:, 0:1], mv[:, 3:4], ALU.subtract, ALU.mult))
            dve.wait_ge(s("ln_gains"), 32 * ln_no[tag] + 32)
            link(v.tensor_tensor(x, x, lng[0:n, :], ALU.mult))
            v.tensor_tensor(x, x, lnb[0:n, :], ALU.add).then_inc(s("ln_x"), 1)

        def route_pool(pool, l):
            L = f"_{l}"
            pool.dma_start(rw[:], a["router_w"].rearrange("(k p) e -> p k e", p=P)).then_inc(s("rw"), 16)
            pool.dma_start(rb[:], a["router_b"].rearrange("(x e) -> x e", x=1).to_broadcast([P, E])
                           ).then_inc(s("rw"), 16)
            pool.wait_ge(s("routed"), 1 * l + 1)
            steps = pool.value_load(nstep[0:1, 0:1], min_val=E, max_val=E * ROUNDS_MAX)
            with pool.If(steps > E):
                nc.gpsimd.memset(ysb[:], 0.0).then_inc(s("rest_zero" + L), 1)
                pool.wait_ge(s("rest_zero" + L), 1)
                with pool.Fori(1, ROUNDS_MAX) as rr:
                    for q in range(E):
                        for buf in (xg, yg):
                            pool.dma_start(buf[bass.ds(rr * SLOTS + CAP * q, CAP)], ysb[0:CAP, :]).then_inc(s("xg_rest" + L), 16)
                pool.wait_ge(s("xg_rest" + L), 32 * E * (ROUNDS_MAX - 1))
            for i, (t0, n) in enumerate(TILES):
                for k in range(2):
                    pool.indirect_dma_start(out=xg, out_offset=bass.IndirectOffsetOnAxis(ap=slot[0:n, k, i:i + 1], axis=0),
                                            in_=xtok[0:n, i, :], in_offset=None).then_inc(s("sent"), 16)
            pool.wait_ge(s("sent"), 32 * NT * l + 32 * NT)

        def x1t_copy(act, l, i):
            n = TILES[i][1]
            act.wait_ge(s("x1T"), NT * l + i + 1)
            if i:
                act.wait_ge(s("logit"), NT * l + i)
            nc.scalar.activation(x1t[:, :, 0:n].rearrange("p (a k) t -> p a k t", a=2),
                                 ps[:, 4:6, :].rearrange("p a (k t) -> p a k t", t=P)[:, :, :, 0:n],
                                 ACT.Copy).then_inc(s("x1t"), 1)

        def route_act(act, l):
            act.wait_ge(*mixed[l])
            act.wait_ge(s(f"ld0_{l}"), 16)
            nc.scalar.activation(whi[0][:], raw[0][:], ACT.Copy).then_inc(s(f"hi0_{l}"), 1)
            x1t_copy(act, l, NT - 1)
            act.wait_ge(s("r_shift"), l + 1)
            nc.scalar.activation(R["p"][0:TT], R["w"][0:TT], ACT.Exp).then_inc(s("r_exp"), 1)

        def x1_transpose(pe, l, i):
            n, te = TILES[i][1], nc.tensor
            pe.wait_ge(s("ln_x"), NT * (2 * l) + i + 1)
            if i:
                pe.wait_ge(s("x1t"), NT * l + i)
            for k in range(KT):
                ins = te.transpose(ps[:, 4 + k // 4, P * (k % 4):P * (k % 4) + n], xtok[0:n, i, P * k:P * k + P],
                                   ident[0:n, 0:n])
            ins.then_inc(s("x1T"), 1)

        def logits(pe, l, i):
            n, te = TILES[i][1], nc.tensor
            if i == 0:
                pe.wait_ge(s("rw"), 32 * l + 32)
            pe.wait_ge(s("x1t"), NT * l + i + 1)
            for k in range(KT):
                ins = te.matmul(ps[0:n, 6, E * i:E * i + E], x1t[:, k, 0:n], rw[:, k, :],
                                start=(k == 0), stop=(k == KT - 1))
            ins.then_inc(s("logit"), 1)

        def route_early(pe, l, i):
            if i >= 3:
                logits(pe, l, i - 3)
            if i >= 2:
                x1_transpose(pe, l, i - 2)

        def route_pe(pe, l):
            te = nc.tensor
            logits(pe, l, NT - 3)
            x1_transpose(pe, l, NT - 2)
            logits(pe, l, NT - 2)
            x1_transpose(pe, l, NT - 1)
            logits(pe, l, NT - 1)
            pe.wait_ge(s("chosen"), l + 1)
            m = R["x"][0:TT].rearrange("p i e -> p (i e)")
            te.matmul(ps[0:TT, 7, 0:E * NT], lstrict[0:TT, 0:TT], m, start=True, stop=True)
            te.matmul(ps[0:TT, 7, E * NT:2 * E * NT], ones[0:TT, 0:TT], m, start=True, stop=True
                      ).then_inc(s("ranked"), 1)

        def route_dve(dve, link, l):
            L, v = f"_{l}", nc.vector
            n = TT
            lg, pr, m1, m2, w, x, s1 = (R[q][0:n] for q in ("l", "p", "m1", "m2", "w", "x", "s1"))
            ga, gb, gc, gd, ge = (Rg[q][0:n] for q in ("a", "b", "c", "d", "e"))
            mx, z, p1, p2 = (Rt[q][0:n] for q in ("mx", "z", "p1", "p2"))
            col = lambda q: q.rearrange("p (i x) -> p i x", x=1)
            grp = lambda q: q.rearrange("p i (g j) -> p (i g) j", j=PER_GROUP)
            flat_g = lambda q: q.rearrange("p i g -> p (i g)")
            over16 = lambda q: col(q).to_broadcast([n, NT, E])
            over4 = lambda q: col(q).to_broadcast([n, NT, GROUPS])
            wide = lambda q: flat_g(q).rearrange("p (i x) -> p i x", x=1).to_broadcast([n, NT * GROUPS, PER_GROUP])
            tt, rdc = v.tensor_tensor, v.tensor_reduce
            dve.wait_ge(s(f"hi0_{l}"), 1)
            v.tensor_tensor(wlo[0][:], raw[0][:], whi[0][:].bitcast(F32), ALU.subtract).then_inc(s(f"lo0_{l}"), 1)
            link(v.memset(R["l"][:], 0.0))
            dve.wait_ge(s("rw"), 32 * l + 32)
            dve.wait_ge(s("logit"), NT * l + NT)
            nl = TILES[-1][1]
            tt(R["l"][0:n, 0:NT - 1, :], ps[0:n, 6, 0:E * (NT - 1)].rearrange("p (i e) -> p i e", e=E),
               rb[0:n, :].rearrange("p (x e) -> p x e", x=1).to_broadcast([n, NT - 1, E]), ALU.add)
            link(tt(R["l"][0:nl, NT - 1, :], ps[0:nl, 6, E * (NT - 1):E * NT], rb[0:nl, :], ALU.add))
            link(rdc(mx, lg, AX_X, ALU.max))
            tt(w, lg, over16(mx), ALU.subtract).then_inc(s("r_shift"), 1)
            f = flat_g
            gf, gg = Rg["f"][0:n], Rg["g"][0:n]
            wt_j = wt4[0:n, :].rearrange("p (x g) -> p x g", x=1).to_broadcast([n, NT * GROUPS, PER_GROUP])

            s_max = lambda cur: link(rdc(f(gf), grp(cur), AX_X, ALU.max))
            s_equal = lambda cur: link(tt(grp(x), grp(cur), wide(gf), ALU.is_equal))
            s_weigh = lambda: link(tt(grp(x), grp(x), wt_j, ALU.mult))
            s_first = lambda: link(rdc(f(gg), grp(x), AX_X, ALU.max))
            s_mark = lambda dst: link(tt(grp(dst), grp(x), wide(gg), ALU.is_equal))
            s_max(lg)
            s_equal(lg)
            dve.wait_ge(s("r_exp"), 1 * l + 1)
            rdc(z, pr, AX_X, ALU.add)
            s_weigh()
            v.reciprocal(z, z)
            s_first()
            tt(pr, pr, over16(z), ALU.mult)
            s_mark(m1)
            g4 = grp(pr)
            c4 = [g4[:, :, q] for q in range(4)]
            tt(f(ga), c4[0], c4[1], ALU.max)
            tt(f(gb), c4[0], c4[1], ALU.min)
            tt(f(gc), c4[2], c4[3], ALU.max)
            tt(f(gd), c4[2], c4[3], ALU.min)
            link(v.scalar_tensor_tensor(out=s1, in0=m1, scalar=-3.0e38, in1=lg, op0=ALU.mult, op1=ALU.add))
            tt(f(ge), f(ga), f(gc), ALU.max)
            tt(f(gb), f(gb), f(gd), ALU.max)
            s_max(s1)
            tt(f(gd), f(ga), f(gc), ALU.min)
            s_equal(s1)
            tt(f(gb), f(gb), f(gd), ALU.max)
            s_weigh()
            tt(f(ga), f(ge), f(gb), ALU.add)
            s_first()
            wt_g = wt4[0:n, :].rearrange("p (x g) -> p x g", x=1).to_broadcast([n, NT, GROUPS])
            rdc(mx, ga, AX_X, ALU.max)
            s_mark(m2)
            link(tt(gb, ga, over4(mx), ALU.is_equal))
            link(tt(gb, gb, wt_g, ALU.mult))
            link(rdc(mx, gb, AX_X, ALU.max))
            link(tt(ge, gb, over4(mx), ALU.is_equal))
            tt(grp(m1), grp(m1), wide(ge), ALU.mult)
            link(tt(grp(m2), grp(m2), wide(ge), ALU.mult))
            link(tt(x, m1, m2, ALU.add))
            v.memset(R["x"][TILES[-1][1]:TT, NT - 1, :], 0.0).then_inc(s("chosen"), 1)
            tt(w, pr, m1, ALU.mult)
            link(tt(s1, pr, m2, ALU.mult))
            rdc(p1, w, AX_X, ALU.add)
            link(rdc(p2, s1, AX_X, ALU.add))
            link(tt(z, p1, p2, ALU.add))
            link(v.reciprocal(z, z))
            tt(gate[0:n, 0, :], p1, z, ALU.mult)
            link(tt(gate[0:n, 1, :], p2, z, ALU.mult))
            dve.wait_ge(s("ranked"), 1 * l + 1)
            total = ps[0:n, 7, E * NT:2 * E * NT].rearrange("p (i e) -> p i e", e=E)
            link(v.memset(s1[:, 0, :], 0.0))
            for i in range(1, NT):
                link(tt(s1[:, i, :], s1[:, i - 1, :], total[:, i - 1, :], ALU.add))
            tt(pr[:, 0, :], s1[:, NT - 1, :], total[:, NT - 1, :], ALU.add)
            link(tt(lg, ps[0:n, 7, 0:E * NT].rearrange("p (i e) -> p i e", e=E), s1, ALU.add))
            rdc(nrow[0:1, 0:1], pr[0:1, 0, :], AX_X, ALU.max)
            link(v.tensor_scalar(w, lg, float(CAP), None, ALU.is_ge))
            for q in range(1, ROUNDS_MAX):
                if q == 1:
                    v.tensor_scalar(nrow[0:1, 1:2], nrow[0:1, 0:1], float(CAP), 1.0, ALU.is_gt, ALU.add)
                else:
                    v.scalar_tensor_tensor(out=nrow[0:1, 1:2], in0=nrow[0:1, 0:1], scalar=float(CAP * q),
                                           in1=nrow[0:1, 1:2], op0=ALU.is_gt, op1=ALU.add)
                if q + 1 < ROUNDS_MAX:
                    link(v.scalar_tensor_tensor(out=w, in0=lg, scalar=float(CAP * (q + 1)), in1=w, op0=ALU.is_ge, op1=ALU.add))
                else:
                    link(v.scalar_tensor_tensor(out=w, in0=w, scalar=float(SLOTS - CAP), in1=lg, op0=ALU.mult, op1=ALU.add))
            v.tensor_scalar(nstep[0:1, 0:1], nrow[0:1, 1:2], float(E), None, ALU.mult)
            link(tt(w, w, e128[0:n, :].rearrange("p (x e) -> p x e", x=1).to_broadcast([n, NT, E]), ALU.add))
            tt(m1, w, m1, ALU.mult)
            link(tt(m2, w, m2, ALU.mult))
            rdc(p1, m1, AX_X, ALU.add)
            link(rdc(p2, m2, AX_X, ALU.add))
            v.tensor_copy(slot[0:n, 0, :], p1)
            v.tensor_copy(slot[0:n, 1, :], p2).then_inc(s("routed"), 1)

        mixed = ((s("y"), NT), (s("y"), 4 * NT))

        def step_count(eng, l):
            eng.wait_ge(s("routed"), l + 1)
            return eng.value_load(nstep[0:1, 0:1], min_val=E, max_val=E * ROUNDS_MAX)

        xe_rows = lambda x: x[:, :, 0:CAP].rearrange("p (a k) t -> p a k t", a=2)
        xe_banks = ps[:, 4:6, :].rearrange("p a (k t) -> p a k t", t=P)[:, :, :, 0:CAP]
        h_bank = ps[:, 6, :].rearrange("p (k t) -> p k t", t=P)[:, :, 0:CAP]

        def experts_sp(sp_, l):
            L = f"_{l}"
            w3 = [a["moe_w_gate"][l].rearrange("e (k p) n -> p e k n", p=P),
                  a["moe_w_up"][l].rearrange("e (k p) n -> p e k n", p=P),
                  a["moe_w_down"][l].rearrange("e (k p) n -> p e k n", p=P)]

            half = CHUNK // 2

            def load(q, e, it, further=0):
                if isinstance(it, int) and it == 0:
                    if q < 2:
                        sp_.wait_ge(s("lo_done"), (7 + q, 18 + 2 * q)[l])
                    else:
                        sp_.wait_ge(*mixed[l])
                else:
                    sp_.wait_ge(s(f"lo{q}" + L), it + further if q == 2 else it)
                src = w3[q][:, e:e + 1] if isinstance(e, int) else w3[q][:, bass.ds(e, 1)]
                src = src.rearrange("p e k n -> p (e k) n")
                sp_.dma_start(raw[q][:].rearrange("p (k n) -> p k n", k=src.shape[1]), src
                              ).then_inc(s(f"ld{q}" + L), 16)

            for q in range(3):
                load(q, 0, 0)
            load(0, 1, 1)
            sp_.wait_ge(s("xe" + L), 16)
            load(1, 1, 1)
            with sp_.Fori(1, E - 1) as e:
                load(0, e + 1, e + 1)
                load(1, e + 1, e + 1)
                load(2, e, e)
            sp_.wait_ge(s("lo2" + L), E - 1)
            for h_, name in enumerate(("ld2", "ld0")):
                sp_.dma_start(raw[2][:, half * h_:half * h_ + half].rearrange("p (k n) -> p k n", k=2),
                              w3[2][:, E - 1, 2 * h_:2 * h_ + 2]).then_inc(s(name + L), 16)
            steps = step_count(sp_, l)
            with sp_.If(steps > E):
                sp_.wait_ge(s("lo2" + L), E + 1)
                with sp_.Fori(E, steps) as it:
                    for q in range(3):
                        load(q, it % E, it, 1)
                sp_.wait_ge(*((s("rounds_over"), 1), (s("comb"), NT + 1))[l])

        def experts_pool(pool, l):
            L = f"_{l}"

            def load_x(it):
                if not (isinstance(it, int) and it == 0):
                    pool.wait_ge(s("p_xt" + L), it)
                rows = xg[bass.ds(it * CAP, CAP)] if not isinstance(it, int) else xg[it * CAP:it * CAP + CAP]
                pool.dma_start(xe[0:CAP, :], rows).then_inc(s("xe" + L), 16)

            def store_y(it):
                pool.wait_ge(s("y_ev" + L), it + 1)
                rows = yg[bass.ds((it + 1) * CAP - CAP, CAP)] if not isinstance(it, int) else yg[it * CAP:it * CAP + CAP]
                pool.dma_start(rows, ysb[0:CAP, :]).then_inc(s("y_st" + L), 16)

            load_x(0)
            load_x(1)
            for tiles, n in ((slice(0, NT - 1), TT), (slice(NT - 1, NT), TILES[-1][1])):
                x = xtok[0:n, tiles, :]
                nc.gpsimd.tensor_scalar(x, x, ALPHA, None, ALU.mult).then_inc(s("x_alpha"), 1)
            load_x(2)
            with pool.Fori(2, E - 1) as it:
                load_x(it + 1)
                store_y(it - 2)
            for it in range(E - 3, E):
                store_y(it)
            steps = step_count(pool, l)
            with pool.If(steps > E):
                with pool.Fori(E, steps) as it:
                    load_x(it)
                    store_y(it)
                    pool.wait_ge(s("y_st" + L), it * 16 + 16)

        def experts_act(act, l):
            L, sa = f"_{l}", nc.scalar

            def hi(q, it, done, further=0):
                act.wait_ge(s(f"ld{q}" + L), it * 16 + (16 + 16 * further if q == 0 else 16))
                if not (isinstance(it, int) and it == 0):
                    act.wait_ge(s(done + L), it)
                sa.activation(whi[q][:], raw[q][:], ACT.Copy).then_inc(s(f"hi{q}" + L), 1)

            def xt_hi(it):
                act.wait_ge(s("p_xt" + L), it + 1)
                if not (isinstance(it, int) and it == 0):
                    act.wait_ge(s("p_u" + L), it)
                sa.activation(xe_rows(xet_hi), xe_banks,
                              ACT.Copy).then_inc(s("xth" + L), 1)

            def silu(it):
                act.wait_ge(s("p_g" + L), it + 1)
                if not (isinstance(it, int) and it == 0):
                    act.wait_ge(s("p_ht" + L), it)
                sa.activation(hx[0:CAP, :], ps[0:CAP, 0, :], ACT.Silu).then_inc(s("silu" + L), 1)

            def ht_hi_(it):
                act.wait_ge(s("p_ht" + L), it + 1)
                if not (isinstance(it, int) and it == 0):
                    act.wait_ge(s("p_d" + L), it)
                sa.activation(ht_hi[:, :, 0:CAP], h_bank, ACT.Copy).then_inc(s("hth" + L), 1)

            def y_ev(it):
                act.wait_ge(s("p_d" + L), it + 1)
                if not (isinstance(it, int) and it == 0):
                    act.wait_ge(s("y_st" + L), it * 16)
                sa.activation(ysb[0:CAP, :].rearrange("p (a c) -> p a c", a=2), ps[0:CAP, 2:4, :],
                              ACT.Copy).then_inc(s("y_ev" + L), 1)

            def step(it, prev=True, prev2=True, nxt=True):
                if prev:
                    silu(it - 1)
                    hi(2, it - 1, "p_d")
                if prev2:
                    y_ev(it - 2)
                if prev:
                    ht_hi_(it - 1)
                if nxt:
                    hi(0, it + 1, "p_g")
                    xt_hi(it + 1)
                    hi(1, it + 1, "p_u")

            hi(1, 0, "")
            xt_hi(0)
            step(0, prev=False, prev2=False)
            step(1, prev2=False)
            with act.Fori(2, E - 1) as it:
                step(it)
            step(E - 1, nxt=False)
            silu(E - 1)
            act.wait_ge(s("p_d" + L), E - 1)
            for h_, name, count_ in ((0, "ld2", 16 * E), (1, "ld0", 16 * E + 16)):
                act.wait_ge(s(name + L), count_)
                half = slice(CHUNK // 2 * h_, CHUNK // 2 * h_ + CHUNK // 2)
                sa.activation(whi[2][:, half], raw[2][:, half], ACT.Copy).then_inc(s("hi2" + L), 1)
                if h_ == 0:
                    y_ev(E - 2)
                    ht_hi_(E - 1)
            y_ev(E - 1)
            steps = step_count(act, l)
            with act.If(steps > E):
                with act.Fori(E, steps) as it:
                    xt_hi(it)
                    hi(0, it, "p_g", 1)
                    hi(1, it, "p_u")
                    silu(it)
                    ht_hi_(it)
                    hi(2, it, "p_d")
                    y_ev(it)

        def experts_dve(dve, l):
            L, v = f"_{l}", nc.vector

            def lo(q, it, further=0):
                dve.wait_ge(s(f"hi{q}" + L), it + (1 + further if q == 2 else 1))
                v.tensor_tensor(wlo[q][:], raw[q][:], whi[q][:].bitcast(F32), ALU.subtract).then_inc(s(f"lo{q}" + L), 1)

            def xt_lo(it):
                dve.wait_ge(s("xth" + L), it + 1)
                v.tensor_tensor(xe_rows(xet_lo), xe_banks, xe_rows(xet_hi).bitcast(F32),
                                ALU.subtract).then_inc(s("xtl" + L), 1)

            def h(it):
                dve.wait_ge(s("silu" + L), it + 1)
                dve.wait_ge(s("p_u" + L), it + 1)
                v.tensor_tensor(hx[0:CAP, :], hx[0:CAP, :], ps[0:CAP, 1, :], ALU.mult).then_inc(s("h" + L), 1)

            def ht_lo_(it):
                dve.wait_ge(s("hth" + L), it + 1)
                v.tensor_tensor(ht_lo[:, :, 0:CAP], h_bank, ht_hi[:, :, 0:CAP].bitcast(F32), ALU.subtract).then_inc(s("htl" + L), 1)

            def step(it, prev=True, nxt=True):
                if prev:
                    h(it - 1)
                    lo(2, it - 1)
                    ht_lo_(it - 1)
                if nxt:
                    lo(0, it + 1)
                    xt_lo(it + 1)
                    lo(1, it + 1)

            lo(1, 0)
            xt_lo(0)
            step(0, prev=False)
            with dve.Fori(1, E - 1) as it:
                step(it)
            step(E - 1, nxt=False)
            h(E - 1)
            for h_ in range(2):
                dve.wait_ge(s("hi2" + L), E + h_)
                half = slice(CHUNK // 2 * h_, CHUNK // 2 * h_ + CHUNK // 2)
                v.tensor_tensor(wlo[2][:, half], raw[2][:, half], whi[2][:, half].bitcast(F32),
                                ALU.subtract).then_inc(s("lo2" + L), 1)
                if h_ == 0:
                    ht_lo_(E - 1)
            steps = step_count(dve, l)
            with dve.If(steps > E):
                with dve.Fori(E, steps) as it:
                    xt_lo(it)
                    lo(0, it)
                    lo(1, it)
                    h(it)
                    ht_lo_(it)
                    lo(2, it, 1)
                if l == 0:
                    v.memset(round_mark[:], 0.0).then_inc(s("rounds_over"), 1)

        def experts_pe(pe, mm3, l):
            L, te = f"_{l}", nc.tensor
            first = lambda it: isinstance(it, int) and it == 0

            def xt(it):
                pe.wait_ge(s("xe" + L), it * 16 + 16)
                if not first(it):
                    pe.wait_ge(s("xtl" + L), it)
                for k in range(KT):
                    ins = te.transpose(ps[:, 4 + k // 4, P * (k % 4):P * (k % 4) + CAP], xe[0:CAP, P * k:P * k + P], ident[0:CAP, 0:CAP])
                ins.then_inc(s("p_xt" + L), 1)

            def up(q, it, done):
                pe.wait_ge(s(f"lo{q}" + L), it + 1)
                pe.wait_ge(s("xtl" + L), it + 1)
                if not first(it):
                    pe.wait_ge(s(("silu" if q == 0 else "h") + L), it)
                wh = whi[q][:].rearrange("p (k n) -> p k n", k=KT)
                wl = wlo[q][:].rearrange("p (k n) -> p k n", k=KT)
                for k in range(KT):
                    ins = mm3(ps[0:CAP, q, :], xet_hi[:, k, 0:CAP], xet_lo[:, k, 0:CAP], wh[:, k, :], wl[:, k, :], k == 0, k == KT - 1)
                ins.then_inc(s(done + L), 1)

            def ht(it):
                pe.wait_ge(s("h" + L), it + 1)
                if not first(it):
                    pe.wait_ge(s("htl" + L), it)
                for k in range(4):
                    ins = te.transpose(ps[:, 6, P * k:P * k + CAP], hx[0:CAP, P * k:P * k + P], ident[0:CAP, 0:CAP])
                ins.then_inc(s("p_ht" + L), 1)

            def down(it, further=0):
                pe.wait_ge(s("lo2" + L), it + (1 + further))
                pe.wait_ge(s("htl" + L), it + 1)
                if not first(it):
                    pe.wait_ge(s("y_ev" + L), it)
                wh = whi[2][:].rearrange("p (k n) -> p k n", k=4)
                wl = wlo[2][:].rearrange("p (k n) -> p k n", k=4)
                for half in range(2):
                    cols = slice(512 * half, 512 * half + 512)
                    for k in range(4):
                        ins = mm3(ps[0:CAP, 2 + half, :], ht_hi[:, k, 0:CAP], ht_lo[:, k, 0:CAP], wh[:, k, cols], wl[:, k, cols],
                                  k == 0, k == 3)
                ins.then_inc(s("p_d" + L), 1)

            def step(it, prev=True, nxt=True):
                up(0, it, "p_g")
                if prev:
                    ht(it - 1)
                up(1, it, "p_u")
                if nxt:
                    xt(it + 1)
                if prev:
                    down(it - 1)

            xt(0)
            step(0, prev=False)
            with pe.Fori(1, E - 1) as it:
                step(it)
            step(E - 1, nxt=False)
            ht(E - 1)
            pe.wait_ge(s("htl" + L), E)
            pe.wait_ge(s("y_ev" + L), E - 1)
            wh = whi[2][:].rearrange("p (k n) -> p k n", k=4)
            wl = wlo[2][:].rearrange("p (k n) -> p k n", k=4)
            for kh in range(2):
                pe.wait_ge(s("lo2" + L), E + kh)
                for half in range(2):
                    cols = slice(512 * half, 512 * half + 512)
                    for k in (2 * kh, 2 * kh + 1):
                        ins = mm3(ps[0:CAP, 2 + half, :], ht_hi[:, k, 0:CAP], ht_lo[:, k, 0:CAP], wh[:, k, cols], wl[:, k, cols],
                                  k == 0, k == 3)
            ins.then_inc(s("p_d" + L), 1)
            steps = step_count(pe, l)
            with pe.If(steps > E):
                with pe.Fori(E, steps) as it:
                    xt(it)
                    up(0, it, "p_g")
                    up(1, it, "p_u")
                    ht(it)
                    down(it, 1)

        def gain_on_pool(l, i):
            return l == 1 and i < NT - 1

        def ln_dve_count(l, i):
            return 2 * (NT * l + i) + 1 if l == 0 else 2 * NT + i + 1

        def combine_pool(pool, l):
            L = f"_{l}"
            pool.wait_ge(s("y_st" + L), 16 * E)

            def gather(rows):
                for i, (t0, n) in enumerate(TILES):
                    if i >= 4:
                        pool.wait_ge(s("comb"), NT * l + i - 3)
                    for k in range(2):
                        pool.indirect_dma_start(out=ygat[i % 4][k][0:n, :], out_offset=None, in_=rows,
                                                in_offset=bass.IndirectOffsetOnAxis(ap=slot[0:n, k, i:i + 1], axis=0)
                                                ).then_inc(s(f"got{i % 4}"), 16)
                    if i == 1:
                        ln_gains_pool(pool, f"ffn{l}")

            steps = step_count(pool, l)
            with pool.If(steps > E):
                gather(yg)
            with pool.Else():
                gather(yg[0:SLOTS])
            for i, (t0, n) in enumerate(TILES):
                x = xtok[0:n, i, :]
                if gain_on_pool(l, i):
                    pool.wait_ge(s("ln_sd"), ln_sd_base[f"ffn{l}"] + 2 * i + 2)
                    pool.wait_ge(s("ln_gains"), 32 * ln_no[f"ffn{l}"] + 32)
                    nc.gpsimd.tensor_tensor(x, x, lng[0:n, :], ALU.mult).then_inc(s("x_alpha"), 1)
                    pool.wait_ge(s("x_alpha"), 2 * (l + 1) + i + 1)
                else:
                    pool.wait_ge(s("ln_dve"), ln_dve_count(l, i) + 1)
                nc.gpsimd.tensor_tensor(x, x, lnb[0:n, :], ALU.add).then_inc(s("ln_x"), 1)

        def combine_dve(dve, link, l, behind=None):
            v = nc.vector

            def add_experts(i):
                x, got = xtok[0:TILES[i][1], i, :], ygat[i % 4]
                n = TILES[i][1]
                dve.wait_ge(s("x_alpha"), 2 * (l + 1))
                dve.wait_ge(s(f"got{i % 4}"), 32 * (l * (1 + (i % 4 == 0)) + i // 4 + 1))
                link(v.scalar_tensor_tensor(out=x, in0=got[0][0:n, :], scalar=gate[0:n, 0, i:i + 1], in1=x,
                                            op0=ALU.mult, op1=ALU.add))
                v.scalar_tensor_tensor(out=x, in0=got[1][0:n, :], scalar=gate[0:n, 1, i:i + 1], in1=x,
                                       op0=ALU.mult, op1=ALU.add).then_inc(s("comb"), 1)
                dve.wait_ge(s("comb"), NT * l + i + 1)
                ln_stats(dve, link, f"ffn{l}", i)

            def factors(i):
                ln_root(dve, link, f"ffn{l}", i)
                mv = lnmv[0:TILES[i][1], i % 2]
                v.scalar_tensor_tensor(out=mv[:, 2:3], in0=mv[:, 0:1], scalar=-1.0, in1=mv[:, 3:4],
                                       op0=ALU.mult, op1=ALU.mult).then_inc(s("ln_dve"), 1)

            def scale(i):
                if gain_on_pool(l, i):
                    return
                x = xtok[0:TILES[i][1], i, :]
                dve.wait_ge(s("ln_sd"), ln_sd_base[f"ffn{l}"] + 2 * i + 2)
                dve.wait_ge(s("ln_gains"), 32 * ln_no[f"ffn{l}"] + 32)
                v.tensor_tensor(x, x, lng[0:TILES[i][1], :], ALU.mult).then_inc(s("ln_dve"), 1)

            for i in range(NT):
                add_experts(i)
                if i >= 2:
                    scale(i - 1)
                factors(i)
                if i == 0:
                    scale(0)
                if behind and i == 1:
                    behind(0)
                if behind and i >= 3:
                    behind(i - 2)
            scale(NT - 1)
            if behind:
                behind(NT - 2)
                behind(NT - 1)

        def combine_act(act, l, behind=None):
            for i, (t0, n) in enumerate(TILES):
                if behind and i == 1:
                    behind(0)
                act.wait_ge(s("ln_mv"), NT * ln_no[f"ffn{l}"] + i + 1)
                mv, x = lnmv[0:n, i % 2], xtok[0:n, i, :]
                nc.scalar.activation(mv[:, 2:3], mv[:, 1:2], ACT.Sqrt, bias=eps[0:n, 1:2]).then_inc(s("ln_sd"), 1)
                act.wait_ge(s("ln_dve"), ln_dve_count(l, i))
                nc.scalar.activation(x, x, ACT.Identity, scale=mv[:, 3:4], bias=mv[:, 2:3]).then_inc(s("ln_sd"), 1)
                if behind and i >= 2:
                    behind(i - 1)
            if behind:
                behind(NT - 1)

        def store_tokens(sp_, tag):
            yp, ys = o["y_prompt"][0], o["y_sample"][0]
            for i, (t0, n) in enumerate(TILES):
                sp_.wait_ge(s("ln_x"), NT * ln_no[tag] + i + 1)
                if t0 + n <= T_PROMPT:
                    parts = [(0, n, yp[t0:t0 + n])]
                else:
                    m = T_PROMPT - t0
                    parts = [(0, m, yp[t0:T_PROMPT]), (m, n - m, ys[0:n - m])]
                for r, m, rows in parts:
                    sp_.dma_start(rows, xtok[r:r + m, i, :]).then_inc(s("tokens_out"), 16)
            sp_.wait_ge(s("tokens_out"), 16 * (NT + 1))


        G, SP_, GC, CL = 64, 64, 16, 8
        NC_P, NC_S = T_PROMPT // CL, T_SAMPLE // CL
        NCH = NC_P + NC_S
        PAIRS = G // 2
        ar0 = SB0
        LEVELS = 2
        S_AT = NC_P + 2 ** LEVELS
        SLOTS_Z = S_AT + NC_S + 1
        Z_AT, UT_AT = ar0, ar0 + SLOTS_Z * 2 * PAIRS * 4
        SPAD_AT = UT_AT + G * NCH * 4
        UB_AT = RAW_AT[1]
        QP = 8
        W_AT = SPAD_AT + 2 * 2 * QP * 2 * NCH * 4
        CH_AT = W_AT + PAIRS * 2 * P * 4
        zst = at("s5_z", [P, SLOTS_Z, 2, PAIRS], Z_AT)
        ut = at("s5_ut", [P, G, NCH], UT_AT)
        spad = [at(f"s5_spad{i}", [P, 2, QP, 2, NCH], SPAD_AT + 4 * 2 * QP * 2 * NCH * i) for i in range(2)]
        QT = PAIRS // 4
        wt = [at(f"s5_wt{i}", [P, QT, CL, GC], SPAD_AT + 4 * QT * P * i) for i in range(4)]
        assert 4 * 4 * QT * P <= W_AT - SPAD_AT
        wl = at("s5_w", [P, 2, PAIRS, P], W_AT)
        u_g = at("s5_ug", [P, G, CL, GC], W_AT)
        mm_ = at("s5_m", [P, G, P], W_AT)
        craw = at("s5_craw", [P, 2, 4, P], UB_AT + 8192)
        u72 = at("s5_u", [P, CL, D], YT_AT)
        ct = at("s5_ct", [P, 2, PAIRS, GC], FT_AT + 4 * CL * D)
        ctn = at("s5_ctn", [P, 2, PAIRS, GC], CH_AT + 4096)
        ksb = at("s5_k", [P, PAIRS, P], FT_AT)
        ox = at("s5_o", [P, 2, CL + 1, PAIRS, GC], YT_AT)
        q_at = [Z_AT]

        def pre(name):
            x = at("q_" + name, [P, P], q_at[0])
            q_at[0] += 512
            return x[0:PAIRS, :]
        q = {n: pre(n) for n in ("are", "aim", "x", "y", "t", "e", "ex", "r", "k", "sn", "sh", "cm", "co", "nr", "den",
                                 "ar", "ai", "fr", "fi", "w1", "w2", "sre", "sim")}
        qdt = at("q_dt", [P, 3, 2], q_at[0])[0:PAIRS]
        qd = at("q_d", [P, 2 * GC], q_at[0] + 32)[0:PAIRS]
        qdi = at("q_di", [P, 2], q_at[0] + 32 + 128, I32)[0:PAIRS]
        q_at[0] += 32
        taken[0] = shared_end
        bb0_at = taken[0]
        bb0 = small("s5_b", [2, PAIRS, GC])
        bb = small("s5_bb", [2, PAIRS, GC])
        bd_at = taken[0]
        bd = small("s5_bd", [2, PAIRS, 2 * GC])
        otmp = bd
        o_tmp = at("s5_otmp", [P, CL, QT, GC], FT_AT + 20736)
        o8_tmp = at("s5_o8tmp", [P, 2, PAIRS, GC], FT_AT + 20736)
        pf = at("s5_pf", [P, 2, CL, PAIRS], FT_AT + 18688)
        assert PAIRS * P * 4 + 256 + 4 * 4 * P <= 18688 and 18688 + 8 * CL * PAIRS <= 20736
        w_tmp = [at("s5_wtmp0", [P, QT * CL * GC], bb0_at), at("s5_wtmp1", [P, QT * CL * GC], bd_at + 4096)]
        t4 = small("s5_t4", [4, PAIRS])
        pw = at("s5_pw", [P, 2, CL + 1, PAIRS], q_at[0] + 160)
        assert q_at[0] + 160 + 8 * (CL + 1) * PAIRS <= UB_AT
        dk = at("s5_dk", [P, PAIRS], FT_AT + PAIRS * P * 4)
        eye = at("s5_eye", [P, GC], FT_AT + PAIRS * P * 4 + 128)
        stf = at("s5_stf", [P, 4, P], FT_AT + PAIRS * P * 4 + 256)
        pr_ = at("s5_pr", [P, 2, CL, PAIRS], CH_AT)
        pole1 = at("s5_pole1", [P, 2, 2, PAIRS], CH_AT + 2048)
        pole24 = small("s5_pole24", [LEVELS, 2, 2, PAIRS])
        poles = [pole1[:]] + [pole24[:, lv] for lv in range(LEVELS)]
        J_AT = FT_AT + 27904
        sctmp = at("s5_tmp", [P, 2, 2, 2, PAIRS], J_AT)
        jtmp = at("s5_jtmp", [P, 2, SLOTS_Z // 2, 2, QP], J_AT)
        assert J_AT + 4 * 2 * (SLOTS_Z // 2) * 2 * QP <= FT_AT + 4 * CL * D and 20736 + 4 * CL * QT * GC <= 27904
        ych = [at(f"s5_y{i}", [P, CL, P], x_at) for i, x_at in enumerate((bb0_at, bb0_at + 4 * CL * P))]
        sg = [at(f"sg{i}", [P, 512], YT_AT + 8 * CHUNK + 2048 * i) for i in range(2)]
        whi_s5 = [whi[0], whi[1], at("whi3", [P, CHUNK], YT_AT, F32R)]
        wlo_s5 = [wlo[0], wlo[1], at("wlo3", [P, CHUNK], YT_AT + 4 * CHUNK, F32R)]
        split_slot = [0, 1, 0, 1, 2, 0]
        ub = [at(f"ub{i}", [P, D], UB_AT + 4096 * i) for i in range(2)]
        u_d = nc.dram_tensor("u_d", (T, D), F32, kind="Internal").ap()
        wis = a["w_in_s5"][0].rearrange("(k p) n -> p k n", p=P)
        wos = a["w_out_s5"][0].rearrange("(k p) n -> p k n", p=P)
        chunks1 = [wis[:, :, 0:512], wis[:, :, 512:D], wos[:, :, 0:512], wos[:, :, D:D + 512],
                   wos[:, :, 512:D], wos[:, :, D + 512:2 * D]]

        def half_of(h_):
            return slice(CHUNK // 2 * h_, CHUNK // 2 * h_ + CHUNK // 2)

        def s5_split(c, h_):
            return 8 + 2 * c + h_ + 1

        def pairs_of(x):
            return x.rearrange("(a b) p -> a (b p)", b=2)

        def s5_sp(sp_):
            def load(c):
                if c >= 2:
                    sp_.wait_ge(s("lo_done"), s5_split(c - 2, 1))
                sp_.dma_start(raw[c % 2][:].rearrange("p (k n) -> p k n", n=512), chunks1[c]).then_inc(s(f"w_landed{c % 2}"), 16)
            sp_.wait_ge(s("lo0_0"), E)
            load(0)
            sp_.wait_ge(s("lo1_0"), E)
            load(1)
            sp_.wait_ge(s("lo_done"), s5_split(1, 1))
            for dst, src in ((q["are"], pairs_of(a["s5_a_re"][0])), (q["aim"], pairs_of(a["s5_a_im"][0])),
                             (q["sre"], pairs_of(a["state_s5_re"][0, 0])), (q["sim"], pairs_of(a["state_s5_im"][0, 0])),
                             (qdt[:, 0, :], a["s5_log_dt"][0].rearrange("(a b) -> a b", b=2)),
                             (qd, a["s5_d"][0].rearrange("(a b) -> a b", b=2 * GC))):
                sp_.dma_start(dst, src).then_inc(s("s5_par"), 16)
            sp_.wait_ge(s("ln_x"), 2 * NT)
            for ri, nm in enumerate(("re", "im")):
                b_src = a[f"s5_b_{nm}"][0].rearrange("(a b) p c -> (b p) a c", b=2)
                sp_.dma_start(bb0[:, ri], b_src).then_inc(s("s5_bc"), 16)
                c_src = a[f"s5_c_{nm}"][0].rearrange("(q j b) c p -> q b j c p", b=2, j=8)
                for qq in range(4):
                    for b in range(2):
                        sp_.dma_start(craw[:, ri, qq, 64 * b:64 * b + 64], c_src[qq, b]).then_inc(s("s5_bc"), 16)
            for i, (t0, n) in enumerate(TILES):
                sp_.wait_ge(s("ub"), i + 1)
                sp_.dma_start(u_d[t0:t0 + n], ub[i % 2][0:n, :]).then_inc(s(f"u_out{i % 2}"), 16)
                sp_.wait_ge(s(f"u_out{i % 2}"), 16 * (i // 2) + 16)
                sp_.dma_start(u72[t0 // CL:(t0 + n) // CL].rearrange("n s c -> n (s c)"),
                              u_d[t0:t0 + n].rearrange("(n s) c -> n (s c)", s=CL)).then_inc(s("u72"), 16)
            sp_.wait_ge(s("kd"), 1)
            sp_.wait_ge(s("m_zero"), 2)
            for st in range(CL):
                for b in range(2):
                    sp_.dma_start(mm_[GC * st:GC * st + GC, b::2, GC * st:P],
                                  ksb[GC * b:GC * b + GC, :, 0:P - GC * st]).then_inc(s("s5_m"), 16)
            sp_.wait_ge(s("stf"), 1)
            for i, nm in enumerate(("p_s5_re", "p_s5_im", "s_s5_re", "s_s5_im")):
                sp_.dma_start(pairs_of(o[nm][0, 0]), stf[0:PAIRS, i, :]).then_inc(s("s5_so"), 16)
            assert RAW_AT[0] + 4 * CHUNK <= UT_AT <= RAW_AT[1] + 4 * CHUNK <= UT_AT + 6 * 8 * NCH * 4
            sp_.wait_ge(s("spad"), PAIRS // QP)
            load(2)
            sp_.wait_ge(s("y_mm"), 6)
            load(3)
            load(4)
            load(5)
            sp_.wait_ge(s("s5_so"), 64)

        def by_group(i):
            return (u_g[0:NCH, 16 * i:16 * i + 16].rearrange("n g t c -> n t g c"),
                    u72[0:NCH, :, 256 * i:256 * i + 256].rearrange("n t (g c) -> n t g c", c=GC))

        O_POOL = 7

        def o_turn(t):
            pairs, r_ = slice(QT * (t // 2), QT * (t // 2) + QT), t % 2
            shape = [P, CL, QT, GC]
            c_of = lambda table: table[:, r_, pairs].rearrange("p (x a) c -> p x a c", x=1).to_broadcast(shape)
            p_of = lambda part: pf[:, part, :, pairs].rearrange("p s (a x) -> p s a x", x=1).to_broadcast(shape)
            return ox[:, r_, 0:CL, pairs], (c_of(ct), p_of(0)), (c_of(ctn), p_of(1))

        def o_last():
            wide = lambda x: x.rearrange("p (x a y) -> p x a y", x=1, y=1).to_broadcast([P, 2, PAIRS, GC])
            return ox[:, :, CL], (ct[:], wide(poles[0][:, 0, 0])), (ctn[:], wide(poles[0][:, 1, 0]))

        def w_done(t):
            return 15 * (t // 4) + (5, 8, 11, 12)[t % 4]
        W_ALL = w_done(7)
        Z_STEPS = NC_P >> LEVELS

        def s5_pool(pool):
            g = nc.gpsimd
            pool.wait_ge(s("bbar"), 2)
            pool.wait_ge(s("ug_act"), 2)
            pool.wait_ge(s("ug_dve"), 2)
            pool.wait_ge(s("s5a"), 6)
            for t in range(O_POOL + 1):
                if t < O_POOL:
                    dst, first, second = o_turn(t)
                    g.tensor_tensor(dst, *first, ALU.mult).then_inc(s("o_c"), 1)
                if t:
                    pool.wait_ge(s("o_c"), 3 * t - 1)
                    last = o_turn(t - 1)[0]
                    g.tensor_tensor(last, last, o_tmp[:], ALU.add).then_inc(s("o_c"), 1)
                if t == O_POOL - 2:
                    pool.wait_ge(s("w_m"), W_ALL)
                    g.memset(bd[:], 0.0).then_inc(s("bd"), 1)
                if t < O_POOL:
                    if t:
                        pool.wait_ge(s("o_c"), 3 * t + 1)
                    g.tensor_tensor(o_tmp[:], *second, ALU.mult).then_inc(s("o_c"), 1)
            pool.wait_ge(s("x_done"), 16)
            g.memset(mm_[:, G // 2:G], 0.0).then_inc(s("m_zero"), 1)
            pool.wait_ge(s("s5_drain"), 32 + 9)
            g2 = 2 * GC
            g.tensor_tensor(eye[0:g2, :], ident[0:g2, 0:GC], ident[0:g2, GC:g2], ALU.add).then_inc(s("bd"), 1)
            pool.wait_ge(s("bd"), 4)
            d_eye = bb0[0:g2, 0]
            g.tensor_tensor(d_eye, dk[0:g2, :].rearrange("p (a x) -> p a x", x=1).to_broadcast([g2, PAIRS, GC]),
                            eye[0:g2, :].rearrange("p (x c) -> p x c", x=1).to_broadcast([g2, PAIRS, GC]),
                            ALU.mult).then_inc(s("bd"), 1)
            pool.wait_ge(s("bd"), 5)
            g.tensor_tensor(ksb[0:g2, :, 0:GC], ksb[0:g2, :, 0:GC], d_eye, ALU.add).then_inc(s("kd"), 1)
            dst, first, second = o_last()
            g.tensor_tensor(dst, *first, ALU.mult).then_inc(s("o_c"), 1)
            g.tensor_tensor(o8_tmp[:], *second, ALU.mult).then_inc(s("o_c"), 1)
            pool.wait_ge(s("o_c"), 3 * O_POOL + 2)
            g.tensor_tensor(dst, dst, o8_tmp[:], ALU.add).then_inc(s("o_c"), 1)
            pool.wait_ge(s("s5_fill"), 16 + 16)
            for i in range(2):
                g.memset(spad[i][:], 0.0).then_inc(s("spad0"), 1)
            ln_gains_after(pool)

        def ln_gains_after(pool):
            pool.wait_ge(s("yt_s5"), 8)
            ln_gains_pool(pool, "mix1")

        def s5_act(act):
            sa = nc.scalar
            def hi(c):
                act.wait_ge(s(f"w_landed{c % 2}"), count[c % 2] + 16 * (c // 2 + 1))
                if c == 5:
                    act.wait_ge(s("y"), 3 * NT)
                for h_ in range(2):
                    sa.activation(whi_s5[split_slot[c]][:, half_of(h_)], raw[c % 2][:, half_of(h_)],
                                  ACT.Copy).then_inc(s("hi_done"), 1)

            def x_hi(i):
                t0, n = TILES[i]
                for hf_ in range(2):
                    act.wait_ge(s("xt"), 2 * NT + 2 * i + hf_ + 1)
                    sa.activation(ft_hi[:, 4 * hf_:4 * hf_ + 4, t0:t0 + n],
                                  ps[:, 4 + 2 * (i % 2) + hf_, :].rearrange("p (k t) -> p k t", t=P)[:, :, 0:n],
                                  ACT.Copy).then_inc(s("xt_hi"), 1)

            hi(0)
            hi(1)

            def u_out(i):
                n, b = TILES[i][1], 2 * (i % 2)
                act.wait_ge(s("y"), NT + i + 1)
                if i >= 2:
                    act.wait_ge(s(f"u_out{i % 2}"), 16 * (i // 2))
                sa.activation(ub[i % 2][0:n, :].rearrange("p (a c) -> p a c", a=2), ps[0:n, b:b + 2, :],
                              ACT.Copy).then_inc(s("ub"), 1)

            def behind_norm(i):
                if i == NT - 1:
                    u_out(0)
                x_hi(i)

            combine_act(act, 0, behind_norm)
            u_out(1)
            act.wait_ge(s("s5d"), 1)
            sa.activation(qdt[:, 1, :], qdt[:, 0, :], ACT.Tanh, scale=0.5).then_inc(s("s5a"), 1)
            act.wait_ge(s("s5d"), 2)
            sa.activation(q["t"], q["x"], ACT.Tanh, scale=0.5).then_inc(s("s5a"), 1)
            act.wait_ge(s("s5d"), 3)
            sa.activation(q["sn"], q["r"], ACT.Sin).then_inc(s("s5a"), 1)
            sa.activation(q["sh"], q["r"], ACT.Sin, scale=0.5).then_inc(s("s5a"), 1)
            u_out(2)
            u_out(3)
            act.wait_ge(s("s5_pt"), 2)
            sa.activation(t4[:].rearrange("p a b -> p (a b)"), ps[:, 4, 0:4 * PAIRS], ACT.Copy).then_inc(s("s5a"), 1)
            u_out(4)
            for part, at_, sign in ((0, ct[:, 0], 1.0), (1, ct[:, 1], -1.0), (1, ctn[:, 0], -1.0), (0, ctn[:, 1], -1.0)):
                ins = sa.activation(at_.rearrange("p a b -> p (a b)"), ps[:, 5 + part, :], ACT.Copy, scale=sign)
            ins.then_inc(s("s5a"), 1)
            act.wait_ge(s("u72"), 16 * NT)
            for i in (0, 2):
                dst, src = by_group(i)
                sa.activation(dst, src, ACT.Copy).then_inc(s("ug_act"), 1)
            sa.activation(zst[:, S_AT].rearrange("p a b -> p (a b)"), ps[:, 4, 4 * PAIRS:6 * PAIRS],
                          ACT.Copy).then_inc(s("s5a"), 1)
            for i in range(G // 4):
                act.wait_ge(s("s5_fill"), i + 1)
                sa.activation(ut[:, 4 * i:4 * i + 4, :].rearrange("p g n -> p (g n)"), ps[:, 1 + i % 4, 0:4 * NCH],
                              ACT.Copy).then_inc(s("s5_drain"), 1)

            def w_out_of_psum(quarter):
                for t in (2 * quarter, 2 * quarter + 1):
                    for h_ in range(2):
                        i = 2 * t + h_
                        act.wait_ge(s("s5_fill"), 16 + i + 1)
                        p0 = QT * quarter + 4 * h_
                        sa.activation(wl[:, t % 2, p0:p0 + 4, :].rearrange("p a b -> p (a b)"), ps[:, 3 + i % 2, :],
                                      ACT.Copy).then_inc(s("s5_drain"), 1)

            def x_in(quarter):
                for i in range(4 * quarter, 4 * quarter + 4):
                    act.wait_ge(s("x_done"), i + 1)
                    for ri in range(2):
                        for sl, n0, n1 in ((1, 0, NC_P), (S_AT - NC_P + 1, NC_P, NCH)):
                            ins = sa.activation(zst[:, n0 + sl:n1 + sl, ri, 2 * i:2 * i + 2],
                                                ps[:, 5 + i % 2, 0:4 * NCH].rearrange("p (r a n) -> p r n a", r=2, a=2)[:, ri, n0:n1],
                                                ACT.Copy)
                    ins.then_inc(s("x_in"), 1)

            w_out_of_psum(0)
            for quarter in range(4):
                if quarter < 3:
                    w_out_of_psum(quarter + 1)
                x_in(quarter)
            act.wait_ge(s("bd"), 1)
            for b in range(2):
                r_ = slice(64 * b, 64 * b + 64)
                sa.activation(bd[r_, :, :, GC * b:GC * b + GC], bb[r_], ACT.Copy).then_inc(s("bd"), 1)
            act.wait_ge(s("x_done"), 16)
            sa.activation(mm_[:, 0:G // 2], ident[:].rearrange("p (x c) -> p x c", x=1).to_broadcast([P, G // 2, P]),
                          ACT.Copy, scale=0.0).then_inc(s("m_zero"), 1)
            for i in range(8):
                act.wait_ge(s("s5_fill"), 32 + i + 1)
                sa.activation(ksb[0:2 * GC, 4 * i:4 * i + 4, :].rearrange("p a b -> p (a b)"), ps[0:2 * GC, 3 + i % 2, :],
                              ACT.Copy).then_inc(s("s5_drain"), 1)
            sa.activation(dk[0:2 * GC, :], ps[0:2 * GC, 7, 0:PAIRS], ACT.Copy).then_inc(s("s5_drain"), 1)
            act.wait_ge(s("spad0"), 2)
            act.wait_ge(s("s5_pt"), 3)
            sa.activation(stf[0:PAIRS].rearrange("p a b -> p (a b)"), ps[0:PAIRS, 0, :], ACT.Copy).then_inc(s("stf"), 1)

            def pad_states(c):
                act.wait_ge(s("z_done"), Z_STEPS + c + 1)
                if c >= 2:
                    act.wait_ge(s("y_mm"), 2 * (c - 1))
                for b in range(2):
                    r_ = slice(64 * b, 64 * b + 64)
                    for n0, n1, sl in ((0, NC_P, 0), (NC_P, NCH, S_AT - NC_P)):
                        ins = sa.activation(spad[c % 2][r_, :, :, b, n0:n1],
                                            zst[r_, n0 + sl:n1 + sl, :, QP * c:QP * c + QP].rearrange("p n r a -> p r a n"),
                                            ACT.Copy)
                ins.then_inc(s("spad"), 1)

            def y_gelu(i):
                act.wait_ge(s("y_mm"), i + 1)
                if i >= 2:
                    act.wait_ge(s("yt_s5"), i - 1)
                for hb_ in range(2):
                    ins = sa.activation(ych[i % 2][0:NCH, :, 64 * hb_:64 * hb_ + 64].rearrange("n t (g c) -> n g t c", c=GC),
                                        ps[0:NCH, 2 * (i % 2) + hb_, :].rearrange("n (g t c) -> n g t c", g=4, c=GC),
                                        ACT.Gelu_apprx_tanh)
                ins.then_inc(s("y_gelu"), 1)

            def y_hi(i):
                act.wait_ge(s("yt_s5"), i + 1)
                for hb_ in range(2):
                    ins = sa.activation(ft_hi[:, i, :].rearrange("p (n t) -> p t n", t=CL)[:, 4 * hb_:4 * hb_ + 4, :],
                                        ps[:, 4 + 2 * (i % 2) + hb_, 0:4 * NCH].rearrange("p (t n) -> p t n", n=NCH), ACT.Copy)
                ins.then_inc(s("yth_s5"), 1)

            pad_states(0)
            pad_states(1)
            for i in range(8):
                y_gelu(i)
                if i in (1, 3):
                    pad_states(2 + i // 2)
                if i:
                    y_hi(i - 1)
            y_hi(7)
            hi(2)
            hi(3)
            hi(4)
            for ph in range(2):
                for i, (t0, n) in enumerate(TILES):
                    j = NT * ph + i
                    act.wait_ge(s("y"), 2 * NT + j + 1)
                    if j >= 2:
                        act.wait_ge(s("mix1_glu"), 2 * j - 2)
                    sa.activation(sg[j % 2][0:n, :], ps[0:n, 2 * (j % 2) + 1, :], ACT.Sigmoid).then_inc(s("sg"), 1)
                    if ph and i:
                        ln_act(act, "mix1", [i - 1])
                    if ph and i >= 2:
                        x1t_copy(act, 1, i - 2)
                if ph == 0:
                    hi(5)
            ln_act(act, "mix1", [NT - 1])
            x1t_copy(act, 1, NT - 2)

        def s5_dve(dve, link, split_lo):
            v = nc.vector
            tt, ts = v.tensor_tensor, v.tensor_scalar
            def lo(c):
                k = split_slot[c]
                for h_ in range(2):
                    dve.wait_ge(s("hi_done"), s5_split(c, h_))
                    tt(wlo_s5[k][:, half_of(h_)], raw[c % 2][:, half_of(h_)], whi_s5[k][:, half_of(h_)].bitcast(F32),
                       ALU.subtract).then_inc(s("lo_done"), 1)

            def x_lo(i):
                t0, n = TILES[i]
                for hf_ in range(2):
                    dve.wait_ge(s("xt_hi"), 2 * NT + 2 * i + hf_ + 1)
                    ins = tt(ft_lo[:, 4 * hf_:4 * hf_ + 4, t0:t0 + n],
                             ps[:, 4 + 2 * (i % 2) + hf_, :].rearrange("p (k t) -> p k t", t=P)[:, :, 0:n],
                             ft_hi[:, 4 * hf_:4 * hf_ + 4, t0:t0 + n].bitcast(F32), ALU.subtract)
                ins.then_inc(s("x_split"), 1)

            lo(0)
            lo(1)
            combine_dve(dve, link, 0, x_lo)
            M, A_, S_ = ALU.mult, ALU.add, ALU.subtract
            MAGIC = 12582912.0
            LN2_HI = 0.693145751953125
            LN2_LO = 0.6931471805599453 - LN2_HI
            d0, d1, d2 = (qdt[:, i, :] for i in range(3))
            dve.wait_ge(s("s5_par"), 16 * 6)
            link(ts(d2, d0, 1.0 / 0.6931471805599453, MAGIC, M, A_))
            link(ts(d2, d2, MAGIC, None, S_))
            link(v.scalar_tensor_tensor(out=d0, in0=d2, scalar=-LN2_HI, in1=d0, op0=M, op1=A_))
            v.scalar_tensor_tensor(out=d0, in0=d2, scalar=-LN2_LO, in1=d0, op0=M, op1=A_).then_inc(s("s5d"), 1)
            link(ts(d2, d2, 127.0, 8388608.0, A_, M))
            link(v.tensor_copy(qdi, d2))
            dve.wait_ge(s("s5a"), 1)
            link(ts(d2, d1, -1.0, 1.0, M, A_))
            link(v.reciprocal(d2, d2))
            link(ts(d1, d1, 1.0, None, A_))
            link(tt(d0, d1, d2, M))
            link(tt(d0, d0, qdi.bitcast(F32), M))
            two = lambda x: x.rearrange("p (b k) -> p b k", b=2)
            dtb = d0.rearrange("p (b x) -> p b x", x=1).to_broadcast([PAIRS, 2, SP_])
            tt(two(q["y"]), two(q["aim"]), dtb, M)
            tt(two(q["x"]), two(q["are"]), dtb, M).then_inc(s("s5d"), 1)
            dve.wait_ge(s("s5d"), 2)
            C1 = 6.28125
            C2 = 0.0019350051879882812
            C3 = 6.283185307179586 - C1 - C2
            link(ts(q["k"], q["y"], 1.0 / 6.283185307179586, MAGIC, M, A_))
            link(ts(q["k"], q["k"], MAGIC, None, S_))
            link(v.scalar_tensor_tensor(out=q["r"], in0=q["k"], scalar=-C1, in1=q["y"], op0=M, op1=A_))
            link(v.scalar_tensor_tensor(out=q["r"], in0=q["k"], scalar=-C2, in1=q["r"], op0=M, op1=A_))
            link(v.scalar_tensor_tensor(out=q["r"], in0=q["k"], scalar=-C3, in1=q["r"], op0=M, op1=A_))
            ts(q["r"], q["r"], 3.1415925, -3.1415925, ALU.min, ALU.max).then_inc(s("s5d"), 1)
            dve.wait_ge(s("s5a"), 2)
            link(ts(q["w1"], q["t"], -1.0, 1.0, M, A_))
            link(v.reciprocal(q["w1"], q["w1"]))
            link(v.scalar_tensor_tensor(out=q["e"], in0=q["t"], scalar=2.0, in1=q["w1"], op0=M, op1=M))
            link(ts(q["ex"], q["e"], 1.0, None, A_))
            dve.wait_ge(s("s5a"), 4)
            link(tt(q["cm"], q["sh"], q["sh"], M))
            link(ts(q["co"], q["cm"], -2.0, 1.0, M, A_))
            link(tt(q["ar"], q["ex"], q["co"], M))
            link(tt(q["ai"], q["ex"], q["sn"], M))
            link(tt(q["nr"], q["e"], q["co"], M))
            link(v.scalar_tensor_tensor(out=q["nr"], in0=q["cm"], scalar=-2.0, in1=q["nr"], op0=M, op1=A_))
            link(tt(q["w1"], q["are"], q["are"], M))
            link(tt(q["w2"], q["aim"], q["aim"], M))
            link(tt(q["den"], q["w1"], q["w2"], A_))
            link(v.reciprocal(q["den"], q["den"]))
            link(tt(q["w1"], q["nr"], q["are"], M))
            link(tt(q["w2"], q["ai"], q["aim"], M))
            link(tt(q["w1"], q["w1"], q["w2"], A_))
            link(tt(q["fr"], q["w1"], q["den"], M))
            link(tt(q["w1"], q["ai"], q["are"], M))
            link(tt(q["w2"], q["nr"], q["aim"], M))
            link(tt(q["w1"], q["w1"], q["w2"], S_))
            tt(q["fi"], q["w1"], q["den"], M).then_inc(s("s5d"), 1)
            dve.wait_ge(s("s5a"), 5)
            link(v.memset(pw[:, 1, 0, :], 0.0))
            link(v.memset(pw[:, 0, 0, :], 1.0))
            link(v.tensor_copy(pw[:, :, 1, :], t4[:, 0:2, :]))
            ot = otmp[:].rearrange("p a b c -> p (a b c)")
            tm = ot[:, 0:4 * PAIRS].rearrange("p (a n) -> p a n", n=PAIRS)

            def cmul(lo_, n, by):
                ar_, ai_ = (pw[:, r_, lo_:lo_ + n, :] for r_ in range(2))
                br_, bi_ = (pw[:, r_, by:by + 1, :].to_broadcast([P, n, PAIRS]) for r_ in range(2))
                out = slice(lo_ + by, lo_ + by + n)
                tr = tm[:, 0:n, :]
                link(tt(pw[:, 0, out, :], ar_, br_, M))
                link(tt(tr, ai_, bi_, M))
                link(tt(pw[:, 0, out, :], pw[:, 0, out, :], tr, S_))
                link(tt(pw[:, 1, out, :], ar_, bi_, M))
                link(tt(tr, ai_, br_, M))
                link(tt(pw[:, 1, out, :], pw[:, 1, out, :], tr, A_))
            cmul(1, 1, 1)
            cmul(1, 2, 2)
            cmul(1, 4, 4)
            pr1, pi1 = pw[:, 0, CL, :], pw[:, 1, CL, :]
            for lv in range(LEVELS):
                tt(tm[:, 0], pr1, pr1, M)
                tt(tm[:, 1], pi1, pi1, M)
                link(tt(tm[:, 2], pr1, pi1, M))
                for r_ in range(2):
                    tt(poles[lv + 1][:, r_, r_], tm[:, 0], tm[:, 1], S_)
                ts(poles[lv + 1][:, 1, 0], tm[:, 2], 2.0, None, M)
                link(ts(poles[lv + 1][:, 0, 1], tm[:, 2], -2.0, None, M))
                pr1, pi1 = poles[lv + 1][:, 0, 0], poles[lv + 1][:, 1, 0]
            dve.wait_ge(s("s5_bc"), 16 * 18)
            over = lambda x: x.rearrange("p (a x) -> p a x", x=1).to_broadcast([P, PAIRS, GC])
            fr, fi = over(t4[:, 2, :]), over(t4[:, 3, :])
            tb = ot[:, 0:PAIRS * GC].rearrange("p (a c) -> p a c", c=GC)
            link(tt(bb[:, 0], bb0[:, 0], fr, M))
            link(tt(tb, bb0[:, 1], fi, M))
            link(tt(bb[:, 0], bb[:, 0], tb, S_))
            link(tt(bb[:, 1], bb0[:, 1], fr, M))
            link(tt(tb, bb0[:, 0], fi, M))
            tt(bb[:, 1], bb[:, 1], tb, A_).then_inc(s("bbar"), 1)
            dve.wait_ge(s("bbar"), 1)
            dve.wait_ge(s("y"), 2 * NT)
            for st in range(CL):
                v.tensor_copy(pr_[:, :, st, :], pw[:, :, CL - 1 - st, :])
            v.tensor_copy(pf[:], pw[:, :, 0:CL, :])
            for r_ in range(2):
                v.tensor_copy(poles[0][:, r_, r_, :], pw[:, 0, CL, :])
            ts(poles[0][:, 0, 1, :], pw[:, 1, CL, :], -1.0, None, M)
            v.tensor_copy(poles[0][:, 1, 0, :], pw[:, 1, CL, :]).then_inc(s("bbar"), 1)
            dve.wait_ge(s("bbar"), 2)

            def w_products(t):
                pairs, ri = slice(QT * (t // 2), QT * (t // 2) + QT), t % 2
                shape = [P, QT, CL, GC]
                b_r, b_i = (bb[:, r_, pairs].rearrange("p a (x c) -> p a x c", x=1).to_broadcast(shape) for r_ in range(2))
                p_of = lambda r_: pr_[:, r_, :, pairs].rearrange("p s (a x) -> p a s x", x=1).to_broadcast(shape)
                if t >= 4:
                    dve.wait_ge(s("s5_fill"), 16 + 2 * (t - 4) + 2)
                tt(wt[t % 4][:], b_r, p_of(ri), M).then_inc(s("w_m"), 1)
                if t % 4 >= 2:
                    dve.wait_ge(s("w_m"), w_done(t - 2))
                tt(w_tmp[t % 2][:].rearrange("p (a s c) -> p a s c", a=QT, c=GC), b_i, p_of(1 - ri), M).then_inc(s("w_m"), 1)

            def w_sum(t):
                dve.wait_ge(s("w_m"), w_done(t) - 3 + (t % 4 == 3) * 2)
                tt(wt[t % 4][:], wt[t % 4][:], w_tmp[t % 2][:].rearrange("p (a s c) -> p a s c", a=QT, c=GC),
                   S_ if t % 2 == 0 else A_).then_inc(s("w_m"), 1)

            def w_turns(t0, t1, first, last):
                for t in range(t0, t1):
                    w_products(t)
                    if t > first:
                        w_sum(t - 1)
                if t1 == last:
                    w_sum(last - 1)
            w_turns(0, 2, 0, 4)
            dve.wait_ge(s("u72"), 16 * NT)
            for i in (1, 3):
                dst, src = by_group(i)
                v.tensor_copy(dst, src).then_inc(s("ug_dve"), 1)
            w_turns(2, 4, 0, 4)
            dve.wait_ge(s("s5a"), 6)
            dve.wait_ge(s("ug_act"), 2)
            dst, first, second = o_turn(O_POOL)
            tmp = w_tmp[0][:].rearrange("p (s a c) -> p s a c", s=CL, c=GC)
            dve.wait_ge(s("w_m"), 12)
            tt(dst, *first, M).then_inc(s("w_m"), 1)
            tt(tmp, *second, M).then_inc(s("w_m"), 1)
            dve.wait_ge(s("w_m"), 14)
            tt(dst, dst, tmp, A_).then_inc(s("w_m"), 1)
            dve.wait_ge(s("w_m"), 15)
            w_turns(4, 8, 4, 8)

            def join(lv, first, c):
                pairs, step = slice(QP * c, QP * c + QP), 2 << lv
                n = len(range(first, SLOTS_Z, step))
                to, src = zst[:, first::step, :, pairs], zst[:, first - (1 << lv):SLOTS_Z - (1 << lv):step, :, pairs]
                for k in range(2):
                    ins = tt(jtmp[:, k, 0:n], src, poles[lv][:, k, :, pairs].rearrange("p (x r) a -> p x r a", x=1
                                                                                ).to_broadcast([P, n, 2, QP]), M)
                link(ins)
                link(tt(to, to, jtmp[:, :, 0:n, 0].rearrange("p k n a -> p n k a"), A_))
                return tt(to, to, jtmp[:, :, 0:n, 1].rearrange("p k n a -> p n k a"), A_)

            v.memset(zst[:, NC_P + 1:S_AT], 0.0)
            link(v.memset(zst[:, 0], 0.0))
            for c in range(PAIRS // QP):
                dve.wait_ge(s("x_in"), 4 * c + 4)
                for lv in range(LEVELS):
                    link(join(lv, 2 << lv, c))
            FOUR = 1 << LEVELS
            for m in range(Z_STEPS):
                groups = 1 + (m < NC_S // FOUR)
                z0, z1 = (zst[:, j:j + S_AT * (groups - 1) + 1:S_AT] for j in (FOUR * m, FOUR * m + FOUR))
                tmp = sctmp[:, 0:groups]
                if m:
                    dve.wait_ge(s("z_done"), m)
                tt(tmp.rearrange("p s k r a -> p s k (r a)"),
                   z0.rearrange("p s (k r) a -> p s k (r a)", k=1).to_broadcast([P, groups, 2, 2 * PAIRS]),
                   poles[LEVELS].rearrange("p (s k) r a -> p s k (r a)", s=1).to_broadcast([P, groups, 2, 2 * PAIRS]),
                   M).then_inc(s("z_a"), 1)
                dve.wait_ge(s("z_a"), 2 * m + 1)
                tt(z1, z1, tmp[:, :, :, 0], A_).then_inc(s("z_a"), 1)
                dve.wait_ge(s("z_a"), 2 * m + 2)
                tt(z1, z1, tmp[:, :, :, 1], A_).then_inc(s("z_done"), 1)

            def between(c):
                dve.wait_ge(s("z_done"), Z_STEPS + c)
                for lv in reversed(range(LEVELS)):
                    ins = join(lv, 1 << lv, c)
                    if lv:
                        link(ins)
                ins.then_inc(s("z_done"), 1)
            between(0)
            between(1)
            between(2)
            dve.wait_ge(s("s5_so"), 64)
            for i in range(8):
                dve.wait_ge(s("yth_s5"), i + 1)
                for hb_ in range(2):
                    dst = ft_lo[:, i, :].rearrange("p (n t) -> p t n", t=CL)[:, 4 * hb_:4 * hb_ + 4, :]
                    ins = tt(dst, ps[:, 4 + 2 * (i % 2) + hb_, 0:4 * NCH].rearrange("p (t n) -> p t n", n=NCH),
                             ft_hi[:, i, :].bitcast(F32).rearrange("p (n t) -> p t n", t=CL)[:, 4 * hb_:4 * hb_ + 4, :], S_)
                ins.then_inc(s("ytl_s5"), 1)
                if i == 0:
                    between(3)
            lo(2)
            lo(3)
            lo(4)
            for ph in range(2):
                if ph:
                    lo(5)
                for i, (t0, n) in enumerate(TILES):
                    j = NT * ph + i
                    dve.wait_ge(s("sg"), j + 1)
                    x = xtok[0:n, i, 512 * ph:512 * ph + 512]
                    tt(sg[j % 2][0:n, :], sg[j % 2][0:n, :], ps[0:n, 2 * (j % 2), :], M).then_inc(s("mix1_glu"), 1)
                    dve.wait_ge(s("mix1_glu"), 2 * j + 1)
                    v.scalar_tensor_tensor(out=x, in0=x, scalar=ALPHA, in1=sg[j % 2][0:n, :], op0=M,
                                           op1=A_).then_inc(s("mix1_glu"), 1)
                    if ph:
                        dve.wait_ge(s("mix1_glu"), 2 * j + 2)
                        ln_dve(dve, link, "mix1", i)

        def s5_pe(pe, mm3):
            te = nc.tensor

            def x_transpose(i):
                n = TILES[i][1]
                pe.wait_ge(s("ln_x"), NT + i + 1)
                if i >= 2:
                    pe.wait_ge(s("x_split"), NT + i - 1)
                for k in range(KT):
                    ins = te.transpose(ps[:, 4 + 2 * (i % 2) + k // 4, P * (k % 4):P * (k % 4) + n],
                                       xtok[0:n, i, P * k:P * k + P], ident[0:n, 0:n])
                    if k % 4 == 3:
                        ins.then_inc(s("xt"), 1)

            def token_major(i, j, slots, first_chunk, between=None):
                t0, n = TILES[i]
                for half in range(2):
                    if half and between is not None:
                        x_transpose(between)
                    wh = whi_s5[slots[half]][:].rearrange("p (k n) -> p k n", n=512)
                    wl_ = wlo_s5[slots[half]][:].rearrange("p (k n) -> p k n", n=512)
                    for k in range(KT):
                        if k in (0, KT // 2):
                            pe.wait_ge(s("lo_done"), s5_split(first_chunk + half, k // (KT // 2)))
                        ins = mm3(ps[0:n, 2 * (j % 2) + half, :], ft_hi[:, k, t0:t0 + n], ft_lo[:, k, t0:t0 + n],
                                  wh[:, k, :], wl_[:, k, :], k == 0, k == KT - 1)
                ins.then_inc(s("y"), 1)

            x_transpose(0)
            for i in range(NT):
                if i == NT - 1:
                    pe.wait_ge(s("x_split"), 2 * NT)
                    pe.wait_ge(s("s5d"), 4)
                    pe.wait_ge(s("s5_bc"), 16 * 18)
                    for m, nm in enumerate(("ar", "ai", "fr", "fi", "sre", "sim")):
                        te.transpose(ps[:, 4, PAIRS * m:PAIRS * m + PAIRS], q[nm], ident[0:PAIRS, 0:PAIRS])
                    te.transpose(ps[0:2 * GC, 7, 0:PAIRS], qd, ident[0:PAIRS, 0:PAIRS]).then_inc(s("s5_pt"), 1)
                    for ri in range(2):
                        for qq in range(4):
                            ins = te.transpose(ps[:, 5 + ri, P * qq:P * qq + P], craw[:, ri, qq, :], ident[:])
                    ins.then_inc(s("s5_pt"), 1)
                if i >= 2:
                    pe.wait_ge(s("ub"), i - 1)
                pe.wait_ge(s("x_split"), NT + i + 1)
                token_major(i, i, (0, 1), 0, 2 * i + 1 if i < 2 else None)
                if i < 2:
                    x_transpose(2 * i + 2)
            pe.wait_ge(s("ub"), NT)
            pe.wait_ge(s("s5a"), 7)
            for i in range(G // 4):
                if i % 4 == 0:
                    pe.wait_ge(s("ug_dve" if i % 8 else "ug_act"), i // 8 + 1)
                if i >= 4:
                    pe.wait_ge(s("s5_drain"), i - 3)
                for j in range(4):
                    g_ = 4 * i + j
                    ins = te.transpose(ps[:, 1 + i % 4, NCH * j:NCH * j + NCH], u_g[0:NCH, g_].rearrange("n t c -> n (t c)"),
                                       ident[0:NCH, 0:NCH])
                ins.then_inc(s("s5_fill"), 1)

            def w_transposes(quarter):
                for t in (2 * quarter, 2 * quarter + 1):
                    pe.wait_ge(s("w_m"), w_done(t))
                    for i in (2 * t, 2 * t + 1):
                        pe.wait_ge(s("s5_drain"), 16 + i - 1)
                        for j in range(4):
                            ins = te.transpose(ps[:, 3 + i % 2, P * j:P * j + P],
                                               wt[t % 4][:, 4 * (i % 2) + j].rearrange("p a b -> p (a b)"), ident[:])
                        ins.then_inc(s("s5_fill"), 1)

            def x_products(quarter):
                pe.wait_ge(s("s5_drain"), 16 + 4 * quarter + 4)
                for i in range(4 * quarter, 4 * quarter + 4):
                    if i >= 2:
                        pe.wait_ge(s("x_in"), i - 1)
                    for ri in range(2):
                        for j in range(2):
                            for b in range(2):
                                pair = 2 * i + j
                                c0 = (2 * ri + j) * NCH
                                ins = te.matmul(ps[64 * b:64 * b + 64, 5 + i % 2, c0:c0 + NCH],
                                                wl[:, ri, pair, 64 * b:64 * b + 64], ut[:, 2 * pair + b, :], start=True, stop=True)
                    ins.then_inc(s("x_done"), 1)

            w_transposes(0)
            for quarter in range(4):
                if quarter < 3:
                    w_transposes(quarter + 1)
                x_products(quarter)
            pe.wait_ge(s("bd"), 3)
            for i in range(8):
                if i % 2 == 0:
                    pe.wait_ge(s("o_c"), min(3 * i + 7, 3 * O_POOL))
                    if i == 6:
                        pe.wait_ge(s("w_m"), 15)
                if i >= 2:
                    pe.wait_ge(s("s5_drain"), 32 + i - 1)
                for j in range(4):
                    pair = 4 * i + j
                    for ri in range(2):
                        ins = te.matmul(ps[0:2 * GC, 3 + i % 2, P * j:P * j + P], bd[:, ri, pair, :],
                                        ox[:, ri, 0:CL, pair, :], start=(ri == 0), stop=(ri == 1))
                ins.then_inc(s("s5_fill"), 1)
            pe.wait_ge(s("z_done"), Z_STEPS)
            for i, (sl, ri) in enumerate(((NC_P, 0), (NC_P, 1), (S_AT + NC_S, 0), (S_AT + NC_S, 1))):
                ins = te.transpose(ps[0:PAIRS, 0, P * i:P * i + P], zst[:, sl, ri, :], ident[:])
            ins.then_inc(s("s5_pt"), 1)
            pe.wait_ge(s("o_c"), 3 * O_POOL + 3)
            pe.wait_ge(s("s5_m"), 16 * 16)
            pe.wait_ge(s("stf"), 1)
            pe.wait_ge(s("s5_drain"), 32 + 9)
            pe.wait_ge(s("x_in"), 16)
            def outputs(i):
                pe.wait_ge(s("spad"), i // 2 + 1)
                if i >= 2:
                    pe.wait_ge(s("y_gelu"), i - 1)
                for j in range(8):
                    g_ = 8 * i + j
                    pair, b = g_ // 2, g_ % 2
                    out = ps[0:NCH, 2 * (i % 2) + j // 4, P * (j % 4):P * (j % 4) + P]
                    te.matmul(out, ut[:, g_, :], mm_[:, g_, :], start=True, stop=False)
                    for ri in range(2):
                        ins = te.matmul(out, spad[(i // 2) % 2][:, ri, pair % QP, b, :], ox[:, ri, 1:CL + 1, pair, :],
                                        start=False, stop=(ri == 1))
                ins.then_inc(s("y_mm"), 1)

            def outputs_t(i):
                pe.wait_ge(s("y_gelu"), i + 1)
                if i >= 2:
                    pe.wait_ge(s("ytl_s5"), i - 1)
                for st in range(CL):
                    ins = te.transpose(ps[:, 4 + 2 * (i % 2) + st // 4, NCH * (st % 4):NCH * (st % 4) + NCH],
                                       ych[i % 2][0:NCH, st, :], ident[0:NCH, 0:NCH])
                ins.then_inc(s("yt_s5"), 1)

            for i in range(8):
                outputs(i)
                if i:
                    outputs_t(i - 1)
            outputs_t(7)
            pe.wait_ge(s("ytl_s5"), 8)
            for ph in range(2):
                for i in range(NT):
                    j = NT * ph + i
                    if j >= 2:
                        pe.wait_ge(s("mix1_glu"), 2 * j - 2)
                    token_major(i, j, ((0, 1), (2, 0))[ph], 2 + 2 * ph)
                    if ph:
                        route_early(pe, 1, i)

        block = ctx.enter_context(nc.Block())

        @block.sync
        def _(sp_):
            def load_chunk(c):
                if c >= 2:
                    sp_.wait_ge(s("lo_done"), c - 1)
                for src, col, n in chunks0[c]:
                    dst = raw[c % 2][:].rearrange("p (k n) -> p k n", n=512)[:, :, col:col + n]
                    sp_.dma_start(dst, src).then_inc(s(f"w_landed{c % 2}"), 16)

            for i, (t0, n) in enumerate(TILES):
                for r, m, rows in x_rows(t0, n):
                    sp_.dma_start(xin[i][r:r + m, :], rows).then_inc(s(f"x_landed{x_group[i]}"), 16)
            load_chunk(0)
            load_chunk(1)
            for c in range(2, len(chunks0)):
                load_chunk(c)
            for i, (t0, n) in enumerate(TILES):
                sp_.wait_ge(s("ycat_lo"), KT)
                for r, m, rows in x_rows(t0, n):
                    sp_.dma_start(xtok[r:r + m, i, :], rows).then_inc(s("res_landed"), 16)
            sp_.wait_ge(s("res_landed"), 16 * (NT + 1))
            experts_sp(sp_, 0)
            s5_sp(sp_)
            experts_sp(sp_, 1)
            store_tokens(sp_, "ffn1")

        @block.gpsimd
        def _(pool):
            g = nc.gpsimd
            g.memset(ident[:], 0.0).then_inc(s("pc"), 1)
            pool.wait_ge(s("pc"), 1)
            g.affine_select(out=ident[:], in_=ident[:], compare_op=ALU.not_equal, fill=1.0, base=0,
                            pattern=[[-1, P]], channel_multiplier=1).then_inc(s("pc"), 1)
            for dst, src in param_dmas:
                with nc.allow_non_contiguous_dma(reason="per-channel parameters, one word to a partition"):
                    pool.dma_start(dst, src).then_inc(s("params"), 16)
            g.memset(wr[:], 0.0).then_inc(s("wz"), 1)
            g.memset(wi[:], 0.0).then_inc(s("wz"), 1)
            for i in range(2):
                g.memset(zx[i][:, 0:CONV - 1], 0.0).then_inc(s("wz"), 1)
                g.memset(zx[i][:, LRU_W - 1:LRU_W], 0.0).then_inc(s("wz"), 1)
            pool.wait_ge(s("wz"), 6)
            for hh in range(2):
                r = slice(64 * hh, 64 * hh + 64)
                for dst, nm in ((wr, "lru_w_r"), (wi, "lru_w_i")):
                    pool.dma_start(dst[r, :, 64 * hh:64 * hh + 64],
                                   a[nm][0].rearrange("(j b) k n -> b k j n", b=2)[hh]).then_inc(s("wri"), 16)
            g.memset(causal[:], 1.0).then_inc(s("pc"), 1)
            g.memset(blkmask[:], 1.0).then_inc(s("pc"), 1)
            g.memset(ones[:], 1.0).then_inc(s("pc"), 1)
            g.memset(m0[:], 1.0).then_inc(s("pc"), 1)
            g.memset(eps[:, 0:1], RMS_EPS).then_inc(s("pc"), 1)
            g.memset(eps[:, 1:2], LN_EPS).then_inc(s("pc"), 1)
            g.memset(lstrict[:], 1.0).then_inc(s("pc"), 1)
            for q in range(PER_GROUP):
                g.memset(wt4[:, q:q + 1], float(PER_GROUP - q)).then_inc(s("pc"), 1)
            for q in range(E):
                g.memset(e128[:, q:q + 1], float(CAP * q)).then_inc(s("pc"), 1)
            g.memset(zeros[:], 0.0).then_inc(s("pc"), 1)
            pool.wait_ge(s("pc"), 30)
            g.affine_select(out=lstrict[:], in_=lstrict[:], compare_op=ALU.is_ge, fill=0.0, base=-1,
                            pattern=[[1, P]], channel_multiplier=-1).then_inc(s("pc"), 1)
            g.affine_select(out=causal[:], in_=causal[:], compare_op=ALU.is_ge, fill=0.0, base=0,
                            pattern=[[1, P]], channel_multiplier=-1).then_inc(s("pc"), 1)
            g.affine_select(out=blkmask[:], in_=blkmask[:], compare_op=ALU.is_ge, fill=0.0, base=0,
                            pattern=[[-BLK, 8]], channel_multiplier=1).then_inc(s("pc"), 1)
            g.memset(m0[:, 0:1], 0.0).then_inc(s("pc"), 1)
            pool.wait_ge(s("pc"), 34)
            g.affine_select(out=blkmask[:], in_=blkmask[:], compare_op=ALU.is_ge, fill=0.0, base=BLK - 1,
                            pattern=[[BLK, 8]], channel_multiplier=-1).then_inc(s("pc"), 1)
            g.affine_select(out=causal[:].rearrange("p (b i) -> p b i", i=BLK),
                            in_=causal[:].rearrange("p (b i) -> p b i", i=BLK),
                            compare_op=ALU.is_ge, fill=0.0, base=0, pattern=[[-BLK, 8], [0, BLK]],
                            channel_multiplier=1).then_inc(s("pc"), 1)
            pool.wait_ge(s("lo_done"), 2)
            for q in range(4):
                pool.dma_start(xg[CAP * 4 * q:CAP * 4 * q + CAP * 4].rearrange("(q p) d -> p q d", p=P),
                               zeros[:].rearrange("p (q d) -> p q d", q=1).to_broadcast([P, 4 * CAP // P, D])
                               ).then_inc(s("xg_zero"), 16)
            pool.wait_ge(s("lru_st"), 4 * LRU_TILES)
            for i, tag in enumerate(("p", "s")):
                with nc.allow_non_contiguous_dma(reason="states, one word to a channel"):
                    for k in range(CONV - 1):
                        pool.dma_start(o[tag + "_lru_conv"][0, 0, k].rearrange("(j p) -> p j", p=P),
                                       convst[:, i, k]).then_inc(s("lru_out"), 16)
                    pool.dma_start(o[tag + "_lru_h"][0, 0].rearrange("(j p) -> p j", p=P),
                                   hst[:, i]).then_inc(s("lru_out"), 16)
            pool.wait_ge(s("ycat_lo"), LRU_TILES)
            pool.wait_ge(s("xg_zero"), 16 * 4)
            pool.dma_start(s_in[:], a["state_hgrn2"][0, 0, 0]).then_inc(s("st_in"), 16)
            for h in range(HEADS):
                for tt, (t0, n) in enumerate(HTILES):
                    i = 5 * h + tt
                    nb = n // BLK
                    pool.wait_ge(s("hg_tok"), 4 * h + 2)
                    if i:
                        pool.wait_ge(s("uinc"), 9 * h + 2 * tt)
                    g.tensor_tensor(vmask[0:n, 0:nb, :],
                                    vtok[0:n, tt:tt + 1, :].to_broadcast([n, nb, P]),
                                    blkmask[0:n, 0:nb].rearrange("p (b x) -> p b x", x=1).to_broadcast([n, nb, P]),
                                    ALU.mult).then_inc(s("vmask"), 1)
                pool.wait_ge(s("state"), NBLK * h + NBLK_P)
                pool.dma_start(o["p_hgrn2"][0, 0, h], srn[:, NBLK_P % SRING, :]).then_inc(s("st_out"), 16)
                pool.wait_ge(s("state"), NBLK * (h + 1))
                pool.dma_start(o["s_hgrn2"][0, 0, h], srn[:, (NBLK + 1) % SRING, :]).then_inc(s("st_out"), 16)
                if h + 1 < HEADS:
                    pool.wait_ge(s("o_done"), 5 * (h + 1))
                    pool.dma_start(s_in[:], a["state_hgrn2"][0, 0, h + 1]).then_inc(s("st_in"), 16)
            pool.wait_ge(s("st_out"), 32 * HEADS)
            pool.wait_ge(s("lru_out"), 16 * 8)
            pool.wait_ge(s("ycat_lo"), KT)
            ln_gains_pool(pool, "mix0")
            route_pool(pool, 0)
            experts_pool(pool, 0)
            combine_pool(pool, 0)
            s5_pool(pool)
            route_pool(pool, 1)
            experts_pool(pool, 1)
            combine_pool(pool, 1)

        @block.scalar
        def _(act):
            sc_ = nc.scalar
            n_link = [0]

            def link(ins):
                n_link[0] += 1
                ins.then_inc(s("act_chain"), 1)
                act.wait_ge(s("act_chain"), n_link[0])

            def split_hi(c):
                act.wait_ge(s(f"w_landed{c % 2}"), landed[c])
                if c >= 2:
                    act.wait_ge(s("z"), 4 * (c - 1))
                sc_.activation(whi[c % 2][:], raw[c % 2][:], ACT.Copy).then_inc(s("hi_done"), 1)

            for i, (t0, n) in enumerate(TILES):
                for hf_ in range(2):
                    b = 2 * (i % 2) + hf_
                    act.wait_ge(s("xt"), 2 * i + hf_ + 1)
                    sc_.activation(ft_hi[:, 4 * hf_:4 * hf_ + 4, t0:t0 + n],
                                   ps[:, b, :].rearrange("p (k t) -> p k t", t=P)[:, :, 0:n],
                                   ACT.Copy).then_inc(s("xt_hi"), 1)
            split_hi(0)
            act.wait_ge(s("prep"), 1)
            sc_.activation(sp[:, 1, :], sp[:, 0, :], ACT.Exp, scale=-1.0).then_inc(s("prep_a"), 1)
            sc_.activation(lbs[:, 0:2, :], lbs[:, 2:4, :], ACT.Exp).then_inc(s("prep_a"), 1)
            split_hi(1)

            def conv_input(j):
                zi, x = 4 * (j // 2) + j % 2, zx[j % 2]
                act.wait_ge(s("z"), zi + 1)
                b = 2 * (zi % 2)
                if j >= 2:
                    act.wait_ge(s("u_done"), j - 1)
                    act.wait_ge(s("lru_st"), 8 * (j // 2 - 1) + 2 * (j % 2) + 2)
                else:
                    act.wait_ge(s("wz"), 6)
                    act.wait_ge(s("params"), 16 * len(param_dmas))
                sc_.activation(x[:, S0_AT:S0_AT + CONV - 1], past[:, :, j], ACT.Copy)
                sc_.activation(x[:, 3:3 + HALF], ps[:, b, 0:HALF], ACT.Copy)
                sc_.activation(x[:, 3 + HALF:3 + T_PROMPT], ps[:, b + 1, 0:T_PROMPT - HALF], ACT.Copy)
                sc_.activation(x[:, S0_AT + 3:S0_AT + 3 + T_SAMPLE],
                               ps[:, b + 1, T_PROMPT - HALF:HALF], ACT.Copy).then_inc(s("z_free"), 1)

            def gates(j):
                h2 = LRU_U // 2
                act.wait_ge(s("ri"), j + 1)
                if j:
                    act.wait_ge(s("lru_y"), j)
                sc_.activation(lr[:].rearrange("p (a t) -> p a t", a=2), ps[:, 4:6, 0:h2], ACT.Sigmoid,
                               bias=b_r[:, j:j + 1]).then_inc(s("lru_act"), 1)
                sc_.activation(li[:].rearrange("p (a t) -> p a t", a=2), ps[:, 6:8, 0:h2], ACT.Sigmoid,
                               bias=b_i[:, j:j + 1]).then_inc(s("lru_act"), 1)
                act.wait_ge(s("lru_act"), 4 * j + 1)
                act.wait_ge(s("spl"), 1)
                sc_.activation(lt[:], lr[:], ACT.Tanh, scale=spl4[:, j:j + 1]).then_inc(s("lru_act"), 1)
                act.wait_ge(s("lru_act"), 4 * j + 3)
                sc_.activation(lq[:], lt[:], ACT.Sqrt).then_inc(s("lru_act"), 1)

            def gelu_gate(j):
                zi = 4 * (j // 2) + 2 + j % 2
                act.wait_ge(s("z"), zi + 1)
                if j >= 2:
                    act.wait_ge(s("lru_y"), j - 1)
                b = 2 * (zi % 2)
                sc_.activation(gz[j % 2][:].rearrange("p (a t) -> p a t", a=2), ps[:, b:b + 2, 0:HALF],
                               ACT.Gelu_apprx_tanh).then_inc(s("z_free"), 1)

            def lru_y_hi(j):
                act.wait_ge(s("lru_y"), j + 1)
                sc_.activation(yt_hi[:, j, :], ld[:, 0:T], ACT.Copy).then_inc(s("ycat_hi"), 1)

            for jp in range(LRU_TILES // 2):
                j = 2 * jp
                conv_input(j)
                conv_input(j + 1)
                if jp:
                    lru_y_hi(j - 1)
                gates(j)
                gelu_gate(j)
                lru_y_hi(j)
                gates(j + 1)
                gelu_gate(j + 1)
                split_hi(jp + 2)
            lru_y_hi(LRU_TILES - 1)

            def head_input(h, m):
                zi = 8 + 4 * h + m
                dst, fn = ((hf, ACT.Sigmoid), (hq, ACT.Copy), (hv, ACT.Copy), (hg, ACT.Silu))[m]
                if h == 1:
                    act.wait_ge(s("ycat_lo"), LRU_TILES)
                if h >= 2:
                    act.wait_ge(s("head_y"), h - 1)
                    act.wait_ge(s("ycat_lo"), LRU_TILES + h - 1 if m == 3 else LRU_TILES)
                act.wait_ge(s("z"), zi + 1)
                b = 2 * (zi % 2)
                sc_.activation(dst[h % 2][:].rearrange("p (a t) -> p a t", a=2), ps[:, b:b + 2, 0:HALF],
                               fn).then_inc(s("z_free"), 1)

            def head_y_hi(h):
                act.wait_ge(s("head_y"), h + 1)
                sc_.activation(yt_hi[:, LRU_TILES + h, :], hg[h % 2][:], ACT.Copy).then_inc(s("ycat_hi"), 1)

            act.wait_ge(s("pc"), 36)
            for m in range(4):
                head_input(0, m)
            for h in range(HEADS):
                if h:
                    act.wait_ge(s("vmask"), 5 * h)
                    act.wait_ge(s("o_done"), 5 * h)
                for k, dst in enumerate((vtok, ktok)):
                    act.wait_ge(s("hg_T"), 2 * h + 1 + k)
                    sc_.activation(dst[:, 0:4, :], ps[:, 4, :].rearrange("p (a t) -> p a t", a=4),
                                   ACT.Copy).then_inc(s("hg_tok"), 1)
                    sc_.activation(dst[0:64, 4, :], ps[0:64, 5, 0:P], ACT.Copy).then_inc(s("hg_tok"), 1)
                if h:
                    head_y_hi(h - 1)
                split_hi(4 + h)
                for tt, (t0, n) in enumerate(HTILES):
                    if h + 1 < HEADS and tt < 2:
                        head_input(h + 1, tt)
                    act.wait_ge(s("o_done"), 5 * h + tt + 1)
                    sc_.activation(ho[h % 2][:, t0:t0 + n], ps[:, 4, 0:n], ACT.Copy).then_inc(s("ho"), 1)
                act.wait_ge(s("ho"), 5 * (h + 1))
                sc_.activation(hv[h % 2][:], ho[h % 2][:], ACT.Square).then_inc(s("hsq"), 1)
                act.wait_ge(s("rms"), h + 1)
                sc_.activation(hr[h % 2][:].rearrange("p (a t) -> p a t", a=2), ps[:, 6:8, 0:HALF], ACT.Sqrt,
                               bias=eps[:, 0:1], scale=1.0 / P).then_inc(s("hrs"), 1)
                if h + 1 < HEADS:
                    head_input(h + 1, 2)
                    head_input(h + 1, 3)
            head_y_hi(HEADS - 1)
            for i in range(NT):
                ln_act(act, "mix0", [i])
                if i >= 2:
                    x1t_copy(act, 0, i - 2)
            x1t_copy(act, 0, NT - 2)
            route_act(act, 0)
            experts_act(act, 0)
            s5_act(act)
            route_act(act, 1)
            experts_act(act, 1)
            combine_act(act, 1)

        @block.vector
        def _(dve):
            v = nc.vector
            n_link = [0]

            def link(ins):
                n_link[0] += 1
                ins.then_inc(s("dve_chain"), 1)
                dve.wait_ge(s("dve_chain"), n_link[0])

            def split_lo(c):
                dve.wait_ge(s("hi_done"), c + 1)
                v.tensor_tensor(wlo[c % 2][:], raw[c % 2][:], whi[c % 2][:].bitcast(F32),
                                ALU.subtract).then_inc(s("lo_done"), 1)

            for i, (t0, n) in enumerate(TILES):
                for hf_ in range(2):
                    b = 2 * (i % 2) + hf_
                    dve.wait_ge(s("xt_hi"), 2 * i + hf_ + 1)
                    ins = v.tensor_tensor(ft_lo[:, 4 * hf_:4 * hf_ + 4, t0:t0 + n],
                                          ps[:, b, :].rearrange("p (k t) -> p k t", t=P)[:, :, 0:n],
                                          ft_hi[:, 4 * hf_:4 * hf_ + 4, t0:t0 + n].bitcast(F32), ALU.subtract)
                ins.then_inc(s("x_split"), 1)
            split_lo(0)
            dve.wait_ge(s("params"), 16 * len(param_dmas))
            link(v.tensor_scalar(sp[:, 2, :], lam[:], -1.0, None, ALU.mult))
            link(v.tensor_tensor(sp[:, 0, :], sp[:, 2, :], lam[:], ALU.max))
            link(v.tensor_tensor(lbs[:, 2, :], lbl[:, 0, :], lbl[:, 1, :], ALU.max))
            link(v.tensor_tensor(lbs[:, 3, :], lbl[:, 1, :], lbs[:, 2, :], ALU.subtract))
            link(v.tensor_tensor(lbs[:, 2, :], lbl[:, 0, :], lbs[:, 2, :], ALU.subtract))
            v.tensor_scalar(sp[:, 2, :], sp[:, 2, :], 0.0, None, ALU.max).then_inc(s("prep"), 1)
            split_lo(1)
            dve.wait_ge(s("prep_a"), 2)
            link(v.tensor_scalar(sp[:, 3, :], sp[:, 1, :], 2.0, None, ALU.add))
            link(v.reciprocal(sp[:, 4, :], sp[:, 3, :]))
            link(v.tensor_tensor(sp[:, 3, :], sp[:, 1, :], sp[:, 4, :], ALU.mult))
            link(v.tensor_tensor(sp[:, 4, :], sp[:, 3, :], sp[:, 3, :], ALU.mult))
            link(v.tensor_scalar(sp[:, 1, :], sp[:, 4, :], 1.0 / 15, 1.0 / 13, ALU.mult, ALU.add))
            for q in (11, 9, 7, 5, 3, 1):
                link(v.tensor_tensor(sp[:, 1, :], sp[:, 1, :], sp[:, 4, :], ALU.mult))
                link(v.tensor_scalar(sp[:, 1, :], sp[:, 1, :], 1.0 / q, None, ALU.add))
            link(v.tensor_tensor(sp[:, 1, :], sp[:, 1, :], sp[:, 3, :], ALU.mult))
            link(v.scalar_tensor_tensor(out=sp[:, 1, :], in0=sp[:, 1, :], scalar=2.0, in1=sp[:, 2, :],
                                        op0=ALU.mult, op1=ALU.add))
            v.tensor_scalar(spl4[:], sp[:, 1, :], 4.0, None, ALU.mult).then_inc(s("spl"), 1)
            link(v.tensor_tensor(lbs[:, 2, :], lbs[:, 0, :], lbs[:, 1, :], ALU.add))
            link(v.reciprocal(lbs[:, 3, :], lbs[:, 2, :]))
            link(v.tensor_tensor(lb[:], lbs[:, 0, :], lbs[:, 3, :], ALU.mult))
            link(v.tensor_scalar(omlb[:], lb[:], -1.0, 1.0, ALU.mult, ALU.add))
            link(v.tensor_scalar(nomlb[:], omlb[:], -1.0, None, ALU.mult))

            def conv(j):
                x, u = zx[j % 2], lu[j % 2]
                dve.wait_ge(s("z_free"), 4 * (j // 2) + j % 2 + 1)
                if j >= 2:
                    dve.wait_ge(s("ri"), j - 1)
                v.tensor_copy(convst[:, 0, :, j], x[:, T_PROMPT:T_PROMPT + 3]).then_inc(s("lru_st"), 1)
                v.tensor_copy(convst[:, 1, :, j], x[:, S0_AT + T_SAMPLE:S0_AT + T_SAMPLE + 3]).then_inc(s("lru_st"), 1)
                link(v.tensor_scalar(u[:], x[:, 0:LRU_U], convw[:, j, 0:1], convb[:, j:j + 1], ALU.mult, ALU.add))
                for k in range(1, CONV):
                    ins = v.scalar_tensor_tensor(out=u[:], in0=x[:, k:k + LRU_U], scalar=convw[:, j, k:k + 1],
                                                 in1=u[:], op0=ALU.mult, op1=ALU.add)
                    if k < CONV - 1:
                        link(ins)
                ins.then_inc(s("u_done"), 1)

            def recur(j):
                dve.wait_ge(s("u_done"), j + 1)
                dve.wait_ge(s("lru_act"), 4 * j + 3)
                if j:
                    dve.wait_ge(s("ycat_lo"), j)
                link(v.tensor_scalar(ld[:], lt[:], 1.0, None, ALU.add))
                link(v.reciprocal(ld[:], ld[:]))
                v.tensor_scalar(la[:], ld[:], 2.0, -1.0, ALU.mult, ALU.add).then_inc(s("scan"), 1)
                dve.wait_ge(s("lru_act"), 4 * j + 4)
                link(v.scalar_tensor_tensor(out=lq[:], in0=lq[:], scalar=2.0, in1=ld[:], op0=ALU.mult, op1=ALU.mult))
                link(v.tensor_tensor(lq[:], lq[:], li[:], ALU.mult))
                link(v.tensor_tensor(lq[:], lq[:], lu[j % 2][:], ALU.mult))
                dve.wait_ge(s("scan"), 3 * j + 1)
                v.tensor_tensor_scan(lr[:, 0:T_PROMPT], la[:, 0:T_PROMPT], lq[:, 0:T_PROMPT], 0.0,
                                     ALU.mult, ALU.add).then_inc(s("scan"), 1)
                v.tensor_tensor_scan(lr[:, S0_AT:S0_AT + T_SAMPLE], la[:, S0_AT:S0_AT + T_SAMPLE],
                                     lq[:, S0_AT:S0_AT + T_SAMPLE], h0[:, j:j + 1], ALU.mult, ALU.add).then_inc(s("scan"), 1)
                dve.wait_ge(s("scan"), 3 * (j + 1))
                v.tensor_copy(hst[:, 0, j:j + 1], lr[:, T_PROMPT - 1:T_PROMPT]).then_inc(s("lru_st"), 1)
                v.tensor_copy(hst[:, 1, j:j + 1], lr[:, S0_AT + T_SAMPLE - 1:S0_AT + T_SAMPLE]).then_inc(s("lru_st"), 1)
                dve.wait_ge(s("z_free"), 4 * (j // 2) + 3 + j % 2)
                v.tensor_tensor(ld[:, 0:T_PROMPT], lr[:, 0:T_PROMPT], gz[j % 2][:, 0:T_PROMPT], ALU.mult)
                v.tensor_tensor(ld[:, T_PROMPT:T], lr[:, S0_AT:S0_AT + T_SAMPLE], gz[j % 2][:, T_PROMPT:T],
                                ALU.mult).then_inc(s("lru_y"), 1)
                dve.wait_ge(s("ycat_hi"), j + 1)
                v.tensor_tensor(yt_lo[:, j, :], ld[:, 0:T], yt_hi[:, j, :].bitcast(F32),
                                ALU.subtract).then_inc(s("ycat_lo"), 1)

            dve.wait_ge(s("params"), 16 * len(param_dmas))
            for jp in range(LRU_TILES // 2):
                conv(2 * jp)
                conv(2 * jp + 1)
                recur(2 * jp)
                recur(2 * jp + 1)
                split_lo(2 + jp)
            n_state = 0
            dve.wait_ge(s("pc"), 36)
            dve.wait_ge(s("xg_zero"), 16 * 4)
            dve.wait_ge(s("ycat_lo"), LRU_TILES)
            blocks = lambda x: x.rearrange("p (b i) -> p b i", i=BLK)

            def decays(h):
                zbase = 8 + 4 * h
                f_, q_ = hf[h % 2], hq[h % 2]
                dve.wait_ge(s("z_free"), zbase + 1)
                v.tensor_scalar(hk[:], f_[:], nomlb[:, h:h + 1], omlb[:, h:h + 1], ALU.mult, ALU.add).then_inc(s("hg_dve"), 1)
                dve.wait_ge(s("hg_dve"), 4 * h + 1)
                if h:
                    dve.wait_ge(s("o_done"), 5 * h)
                link(v.tensor_scalar(f_[:], f_[:], omlb[:, h:h + 1], lb[:, h:h + 1], ALU.mult, ALU.add))
                m0b = m0[:].rearrange("p (x i) -> p x i", x=1).to_broadcast([P, NBLK, BLK])
                link(v.tensor_tensor(blocks(ha[:]), blocks(f_[:]), m0b, ALU.mult))
                link(v.tensor_tensor(hb[:], f_[:], ha[:], ALU.subtract))
                link(v.tensor_tensor_scan(hp[:], ha[:], hb[:], 0.0, ALU.mult, ALU.add))
                link(v.reciprocal(f_[:], hp[:]))
                dve.wait_ge(s("z_free"), zbase + 2)
                v.tensor_tensor(ha[:], q_[:], hp[:], ALU.mult).then_inc(s("hg_dve"), 1)
                v.tensor_tensor(hb[:], hk[:], f_[:], ALU.mult).then_inc(s("hg_dve"), 1)
                dve.wait_ge(s("hg_dve"), 4 * h + 3)
                last = blocks(hp[:])[:, :, BLK - 1:BLK].to_broadcast([P, NBLK, BLK])
                v.tensor_tensor(blocks(q_[:]), blocks(hb[:]), last, ALU.mult).then_inc(s("hg_dve"), 1)

            def head_end(h):
                r_, o_, g_ = hr[h % 2], ho[h % 2], hg[h % 2]
                dve.wait_ge(s("hrs"), h + 1)
                link(v.reciprocal(r_[:], r_[:]))
                link(v.scalar_tensor_tensor(out=o_[:], in0=o_[:], scalar=hg_g[:, h:h + 1], in1=r_[:],
                                            op0=ALU.mult, op1=ALU.mult))
                v.tensor_tensor(g_[:], o_[:], g_[:], ALU.mult).then_inc(s("head_y"), 1)

            def head_y_lo(h):
                dve.wait_ge(s("ycat_hi"), LRU_TILES + h + 1)
                v.tensor_tensor(yt_lo[:, LRU_TILES + h, :], hg[h % 2][:], yt_hi[:, LRU_TILES + h, :].bitcast(F32),
                                ALU.subtract).then_inc(s("ycat_lo"), 1)

            decays(0)
            for h in range(HEADS):
                if h:
                    dve.wait_ge(s("st_out"), 32 * h)
                link(v.memset(srn[:, 0, :], 0.0))
                for tt, (t0, n) in enumerate(HTILES):
                    i = 5 * h + tt
                    if i:
                        dve.wait_ge(s("o_done"), i)
                    if tt == 4:
                        dve.wait_ge(s("st_in"), 16 * (h + 1))
                    for b in range(n // BLK):
                        g_ = t0 // BLK + b
                        k = g_ + (tt == 4)
                        if b % 4 == 0:
                            dve.wait_ge(s("uinc"), 9 * h + 2 * tt + b // 4 + 1)
                        if n_state:
                            dve.wait_ge(s("state"), n_state)
                        v.scalar_tensor_tensor(out=srn[:, (k + 1) % SRING, :],
                                               in0=s_in[:] if g_ == NBLK_P else srn[:, k % SRING, :],
                                               scalar=hp[:, BLK * g_ + BLK - 1:BLK * g_ + BLK],
                                               in1=ps[:, 6 + b // 4, P * (b % 4):P * (b % 4) + P],
                                               op0=ALU.mult, op1=ALU.add).then_inc(s("state"), 1)
                        n_state += 1
                        if b == 3:
                            dve.wait_ge(s("score"), i + 1)
                            v.tensor_tensor(sc[0:n, 0:n], ps[0:n, 5, 0:n], causal[0:n, 0:n], ALU.mult).then_inc(s("scm"), 1)
                    if tt == 0:
                        if h:
                            head_y_lo(h - 1)
                        split_lo(4 + h)
                if h + 1 < HEADS:
                    decays(h + 1)
                head_end(h)
            head_y_lo(HEADS - 1)
            dve.wait_ge(s("res_landed"), 16 * (NT + 1))
            for i, (t0, n) in enumerate(TILES):
                dve.wait_ge(s("y"), i + 1)
                x = xtok[0:n, i, :]
                b = 2 * (i % 2)
                v.scalar_tensor_tensor(out=x.rearrange("p (a c) -> p a c", a=2),
                                       in0=x.rearrange("p (a c) -> p a c", a=2), scalar=ALPHA,
                                       in1=ps[0:n, b:b + 2, :], op0=ALU.mult, op1=ALU.add).then_inc(s("mix0_sum"), 1)
                dve.wait_ge(s("mix0_sum"), i + 1)
                ln_dve(dve, link, "mix0", i)
            route_dve(dve, link, 0)
            experts_dve(dve, 0)
            s5_dve(dve, link, split_lo)
            route_dve(dve, link, 1)
            experts_dve(dve, 1)
            combine_dve(dve, link, 1)

        @block.tensor
        def _(pe):
            te = nc.tensor
            pe.wait_ge(s("pc"), 2)
            for i, (t0, n) in enumerate(TILES):
                pe.wait_ge(s(f"x_landed{x_group[i]}"), x_loads[x_group[i]])
                if i >= 2:
                    pe.wait_ge(s("x_split"), i - 1)
                for k in range(KT):
                    b = 2 * (i % 2) + k // 4
                    ins = te.transpose(ps[:, b, P * (k % 4):P * (k % 4) + n], xin[i][0:n, P * k:P * k + P],
                                       ident[0:n, 0:n])
                    if k % 4 == 3:
                        ins.then_inc(s("xt"), 1)

            def mm3(out, l_hi, l_lo, r_hi, r_lo, first, last):
                te.matmul(out, l_lo, r_hi, start=first, stop=False)
                te.matmul(out, l_hi, r_lo, start=False, stop=False)
                return te.matmul(out, l_hi, r_hi, start=False, stop=last)

            zi = 0

            def z_tile(c, m):
                nonlocal zi
                if m == 0:
                    pe.wait_ge(s("lo_done"), c + 1)
                if c == 0 and m == 0:
                    pe.wait_ge(s("x_split"), NT)
                if zi >= 2:
                    pe.wait_ge(s("z_free"), zi - 1)
                whc = whi[c % 2][:].rearrange("p (k n) -> p k n", n=512)
                wlc = wlo[c % 2][:].rearrange("p (k n) -> p k n", n=512)
                for half in range(2):
                    for k in range(KT):
                        cols = slice(P * m, P * m + P)
                        tk = slice(HALF * half, HALF * half + HALF)
                        ins = mm3(ps[:, 2 * (zi % 2) + half, 0:HALF], whc[:, k, cols], wlc[:, k, cols],
                                  ft_hi[:, k, tk], ft_lo[:, k, tk], k == 0, k == KT - 1)
                ins.then_inc(s("z"), 1)
                zi += 1

            def lru_gates(j):
                pe.wait_ge(s("wri"), 16 * 4)
                pe.wait_ge(s("u_done"), j + 1)
                if j:
                    pe.wait_ge(s("lru_act"), 4 * j - 2)
                h2 = LRU_U // 2
                for w, b in ((wr, 4), (wi, 6)):
                    for half in range(2):
                        ins = te.matmul(ps[:, b + half, 0:h2], w[:, j, :], lu[j % 2][:, h2 * half:h2 * half + h2],
                                        start=True, stop=True)
                ins.then_inc(s("ri"), 1)

            for jp in range(LRU_TILES // 2):
                z_tile(jp, 0)
                z_tile(jp, 1)
                lru_gates(2 * jp)
                z_tile(jp, 2)
                lru_gates(2 * jp + 1)
                z_tile(jp, 3)
            for m in range(4):
                z_tile(2, m)
            pe.wait_ge(s("pc"), 36)
            for h in range(HEADS):
                if h == 0:
                    pe.wait_ge(s("lru_act"), 4 * LRU_TILES - 2)
                else:
                    pe.wait_ge(s("ho"), 5 * h)
                    pe.wait_ge(s("hrs"), h)
                    pe.wait_ge(s("scm"), 5 * h)
                pe.wait_ge(s("z_free"), 8 + 4 * h + 3)
                for src, nm in ((hv[h % 2], "vT"), (hq[h % 2], "kT")):
                    if nm == "kT":
                        pe.wait_ge(s("hg_dve"), 4 * h + 4)
                        pe.wait_ge(s("hg_tok"), 4 * h + 2)
                    for tt, (t0, n) in enumerate(HTILES):
                        out = ps[0:n, 4, P * tt:P * tt + P] if tt < 4 else ps[0:n, 5, 0:P]
                        ins = te.transpose(out, src[:, t0:t0 + n], ident[:])
                    ins.then_inc(s("hg_T"), 1)
                pe.wait_ge(s("hg_tok"), 4 * h + 4)

                def score(tt):
                    t0, n = HTILES[tt]
                    if 5 * h + tt:
                        pe.wait_ge(s("scm"), 5 * h + tt)
                    te.matmul(ps[0:n, 5, 0:n], hb[:, t0:t0 + n], ha[:, t0:t0 + n], start=True,
                              stop=True).then_inc(s("score"), 1)

                def increments(tt, u):
                    n = HTILES[tt][1]
                    pe.wait_ge(s("vmask"), 5 * h + tt + 1)
                    if h or tt:
                        pe.wait_ge(s("state"), NBLK * h + (8 * (tt - 1) + 4 * (u + 1) if tt else 0))
                    te.matmul(ps[:, 6 + u, :], ktok[0:n, tt, :], vmask[0:n, 4 * u:4 * u + 4, :].rearrange("p b d -> p (b d)"),
                              start=True, stop=True).then_inc(s("uinc"), 1)

                score(0)
                increments(0, 0)
                increments(0, 1)
                for tt, (t0, n) in enumerate(HTILES):
                    i = 5 * h + tt
                    if h + 1 < HEADS and tt < 2:
                        z_tile(3 + h, tt)
                    pe.wait_ge(s("scm"), i + 1)
                    if i:
                        pe.wait_ge(s("ho"), i)
                    te.matmul(ps[:, 4, 0:n], vtok[0:n, tt, :], sc[0:n, 0:n], start=True, stop=False)
                    nb = n // BLK
                    for b in range(nb):
                        g_ = t0 // BLK + b
                        k = g_ + (tt == 4)
                        if b == 4 and tt < 4:
                            increments(tt + 1, 0)
                        if g_ == NBLK_P:
                            pe.wait_ge(s("st_in"), 16 * (h + 1))
                        elif g_:
                            pe.wait_ge(s("state"), NBLK * h + g_)
                        ins = te.matmul(ps[:, 4, BLK * b:BLK * b + BLK], s_in[:] if g_ == NBLK_P else srn[:, k % SRING, :],
                                        ha[:, BLK * g_:BLK * g_ + BLK], start=False, stop=(b == nb - 1))
                    ins.then_inc(s("o_done"), 1)
                    if tt < 4:
                        score(tt + 1)
                        if HTILES[tt + 1][1] == P:
                            increments(tt + 1, 1)
                pe.wait_ge(s("hsq"), h + 1)
                pe.wait_ge(s("state"), NBLK * (h + 1))
                for half in range(2):
                    ins = te.matmul(ps[:, 6 + half, 0:HALF], ones[:], hv[h % 2][:, HALF * half:HALF * half + HALF],
                                    start=True, stop=True)
                ins.then_inc(s("rms"), 1)
                if h + 1 < HEADS:
                    z_tile(3 + h, 2)
                    z_tile(3 + h, 3)
            pe.wait_ge(s("ycat_lo"), KT)
            pe.wait_ge(s("lo_done"), 8)
            pe.wait_ge(s("z_free"), 24)
            for i, (t0, n) in enumerate(TILES):
                if i >= 2:
                    pe.wait_ge(s("mix0_sum"), i - 1)
                for half in range(2):
                    wh = whi[half][:].rearrange("p (k n) -> p k n", n=512)
                    wl = wlo[half][:].rearrange("p (k n) -> p k n", n=512)
                    for k in range(KT):
                        ins = mm3(ps[0:n, 2 * (i % 2) + half, :], yt_hi[:, k, t0:t0 + n], yt_lo[:, k, t0:t0 + n],
                                  wh[:, k, :], wl[:, k, :], k == 0, k == KT - 1)
                ins.then_inc(s("y"), 1)
                route_early(pe, 0, i)
            route_pe(pe, 0)
            experts_pe(pe, mm3, 0)
            s5_pe(pe, mm3)
            route_pe(pe, 1)
            experts_pe(pe, mm3, 1)


_OUTS = {
    "y_prompt": (1, 512, 1024), "y_sample": (1, 64, 1024),
    "p_lru_h": (1, 1, 512), "p_lru_conv": (1, 1, 3, 512), "p_hgrn2": (1, 1, 4, 128, 128),
    "p_s5_re": (1, 1, 64, 64), "p_s5_im": (1, 1, 64, 64),
    "s_lru_h": (1, 1, 512), "s_lru_conv": (1, 1, 3, 512), "s_hgrn2": (1, 1, 4, 128, 128),
    "s_s5_re": (1, 1, 64, 64), "s_s5_im": (1, 1, 64, 64),
}


def kernel(**inputs):
    import numpy as _np
    import concourse.bacc as _bacc
    from concourse.bass_utils import run_bass_kernel_spmd as _run

    nc = _bacc.Bacc("TRN2", target_bir_lowering=False, num_devices=1)
    arrays, ins, outs = {}, {}, {}
    for name, value in inputs.items():
        value = _np.ascontiguousarray(value)
        arrays[f"in_{name}"] = value
        ins[name] = nc.dram_tensor(f"in_{name}", value.shape, mybir.dt.from_np(value.dtype), kind="ExternalInput").ap()
    for name, shape in _OUTS.items():
        outs[name] = nc.dram_tensor(f"out_{name}", shape, F32, kind="ExternalOutput").ap()
    stream_kernel(nc, ins, outs)
    r = _run(nc, [arrays], core_ids=[0])
    return tuple(r.results[0][f"out_{name}"] for name in _OUTS)
```
